# Optimizing a Trainium2 kernel written in Bass

```python
import math
import jax
import jax.numpy as jnp
from jax import lax
import numpy as np

D_MODEL = 1024
BATCH = 1
SEQ = 128
DEPTH = 2
DEC_BATCH = 1
DEC_SEQ = 256
PAST_LEN = 128

GRID_W = 64
N_EVEN = (DEPTH + 1) // 2
N_ODD = DEPTH // 2
EPS = 1e-6
H_A = 4
DK_A = 128
DV_A = 128
W_A = H_A * DV_A
CHUNK = 64
C_B = 512
SHORT_W = 3
FILTER_BANDS = 16
FILTER_EMB = 1 + 2 * FILTER_BANDS
FILTER_HIDDEN = 64
DECAY_MIN = math.log(1e-2) / 1.5
DECAY_MAX = math.log(1e-2) / 0.3
H_C = 4
KV_C = 2
G_C = H_C // KV_C
HD_C = 128
H_D = 4
DK_D = 64
DV_D = 128
ROPE_THETA = 10000.0
Q_BLOCK = 128
N_GROUPS = 4
EXP_PER_GROUP = 4
N_EXPERTS = N_GROUPS * EXP_PER_GROUP
TOP_K = 2
D_EXPERT = 512
EVEN_SPLITS = (H_A * DK_A, 2 * H_A * DK_A, 3 * H_A * DK_A, 3 * H_A * DK_A + W_A, 3 * H_A * DK_A + 2 * W_A)
EVEN_IN = 3 * H_A * DK_A + 2 * W_A + 3 * C_B
ODD_SPLITS = (H_C * HD_C, H_C * HD_C + KV_C * HD_C, H_C * HD_C + 2 * KV_C * HD_C, H_C * HD_C + 2 * KV_C * HD_C + 2 * H_D * DK_D, H_C * HD_C + 2 * KV_C * HD_C + 4 * H_D * DK_D)
ODD_IN = H_C * HD_C + 2 * KV_C * HD_C + 4 * H_D * DK_D + H_D * DV_D
MIX_AB = W_A + C_B
MIX_CD = H_C * HD_C + H_D * DV_D

kernel_name = 'hybrid_diffusion_prefix_step'

def rms_norm(x, g):
    xf = x.astype(jnp.float32)
    y = xf * lax.rsqrt(jnp.mean(xf * xf, axis=-1, keepdims=True) + EPS)
    return (y * g.astype(jnp.float32)).astype(x.dtype)

def adaln(cvec, w, b):
    m = jax.nn.silu(cvec) @ w + b
    m = m.reshape(cvec.shape[:-1] + (1, 6, D_MODEL))
    return [m[..., i, :] for i in range(6)]

def modulate(x, shift, scale):
    return x * (1.0 + scale) + shift

def axial_rope(L, dim):
    ROWS = L // GRID_W
    row_idx = jnp.repeat(jnp.arange(ROWS), GRID_W).astype(jnp.float32)
    col_idx = jnp.tile(jnp.arange(GRID_W), ROWS).astype(jnp.float32)
    half = dim // 2
    inv = ROPE_THETA ** (-jnp.arange(0, half, 2, dtype=jnp.float32) / half)
    ang = jnp.concatenate([row_idx[:, None] * inv, col_idx[:, None] * inv], axis=-1)
    return jnp.cos(ang), jnp.sin(ang)

def apply_rope(x, cos, sin):
    shape = (x.shape[1],) + (1,) * (x.ndim - 3) + (x.shape[-1] // 2,)
    cos = cos.reshape(shape)
    sin = sin.reshape(shape)
    xf = x.astype(jnp.float32).reshape(x.shape[:-1] + (x.shape[-1] // 2, 2))
    x1, x2 = xf[..., 0], xf[..., 1]
    out = jnp.stack([x1 * cos - x2 * sin, x1 * sin + x2 * cos], axis=-1).reshape(x.shape)
    return out.astype(x.dtype)

def hgrn2_chunk_scan(q, k, v, logf, s0):
    B, L, H, DK = q.shape
    DV = v.shape[-1]
    n = L // CHUNK

    def to_chunks(a):
        return a.reshape(B, n, CHUNK, H, a.shape[-1]).transpose(1, 0, 3, 2, 4)

    mask = jnp.tril(jnp.ones((CHUNK, CHUNK), dtype=bool))[:, :, None]

    def step(S, inp):
        qc, kc, vc, lf = inp
        b = jnp.cumsum(lf, axis=2)
        diff = b[:, :, :, None, :] - b[:, :, None, :, :]
        decay = jnp.exp(jnp.where(mask, diff, -jnp.inf))
        scores = jnp.einsum('bhtk,bhsk,bhtsk->bhts', qc, kc, decay)
        o = jnp.einsum('bhts,bhsv->bhtv', scores, vc) + jnp.einsum('bhtk,bhkv->bhtv', qc * jnp.exp(b), S)
        b_last = b[:, :, -1:, :]
        S = jnp.exp(b_last[:, :, 0, :])[..., None] * S + jnp.einsum('bhsk,bhsv->bhkv', kc * jnp.exp(b_last - b), vc)
        return S, o

    s_fin, o = lax.scan(step, s0, (to_chunks(q), to_chunks(k), to_chunks(v), to_chunks(logf)))
    o = o.transpose(1, 0, 3, 2, 4).reshape(B, L, H, DV)
    return o, s_fin

def short_conv(u, w, b):
    ch = u.shape[-1]
    y = lax.conv_general_dilated(u, w[:, None, :].astype(u.dtype), window_strides=(1,), padding=[(SHORT_W // 2, SHORT_W // 2)], dimension_numbers=('NWC', 'WIO', 'NWC'), feature_group_count=ch)
    return y + b

def hyena_filters(L, w1, b1, fr1, w2, b2, fr2, w3):
    t = jnp.linspace(0.0, 1.0, L, dtype=jnp.float32)[:, None]
    w = 2.0 * math.pi * jnp.arange(L, dtype=jnp.float32) / L
    f = jnp.linspace(1e-4, FILTER_BANDS - 1, FILTER_BANDS, dtype=jnp.float32)
    ang = w[:, None] * f[None, :]
    z = jnp.concatenate([t, jnp.cos(ang), -jnp.sin(ang)], axis=-1)
    h = jnp.sin(fr1 * (z @ w1 + b1))
    h = jnp.sin(fr2 * (h @ w2 + b2))
    h = (h @ w3).astype(jnp.float32)
    deltas = jnp.abs(jnp.linspace(DECAY_MIN, DECAY_MAX, C_B, dtype=jnp.float32))
    window = jnp.exp(-t * deltas[None, :])
    return h.reshape(L, 2, C_B) * window[:, None, :]

def fft_conv(u, h):
    L = u.shape[1]
    n = 2 * L
    y = jnp.fft.irfft(jnp.fft.rfft(u, n=n, axis=1) * jnp.fft.rfft(h, n=n, axis=0)[None], n=n, axis=1)
    return y[:, :L]

def block_attention(q, k, v):
    B, Hk, G, Lq, d = q.shape
    nb = Lq // Q_BLOCK
    qb = q.reshape(B, Hk, G, nb, Q_BLOCK, d).transpose(3, 0, 1, 2, 4, 5)
    scale = d ** -0.5

    def one(qi):
        s = jnp.einsum('bhgqd,bhkd->bhgqk', qi, k).astype(jnp.float32) * scale
        p = jax.nn.softmax(s, axis=-1)
        return jnp.einsum('bhgqk,bhkv->bhgqv', p.astype(v.dtype), v)

    o = lax.map(one, qb)
    return o.transpose(1, 2, 3, 0, 4, 5).reshape(B, Hk, G, Lq, v.shape[-1])

def even_mixer(h, s0, w_in, w_out, lb, norm_g, conv_w, conv_b, fw1, fb1, ffr1, fw2, fb2, ffr2, fw3, hbias):
    f32 = jnp.float32
    B, L, _ = h.shape
    p = h @ w_in
    qa, ffa, fba, ia, ga, hy = jnp.split(p, EVEN_SPLITS, axis=-1)
    q = jax.nn.silu(qa.astype(f32)).reshape(B, L, H_A, DK_A)
    v = ia.astype(f32).reshape(B, L, H_A, DV_A)

    def forget(z):
        f = lb + (1.0 - lb) * jax.nn.sigmoid(z.astype(f32).reshape(B, L, H_A, DK_A))
        return jnp.log(f), 1.0 - f

    lf_f, k_f = forget(ffa)
    lf_b, k_b = forget(fba)
    o_f, s_f = hgrn2_chunk_scan(q, k_f, v, lf_f, s0[:, 0])
    o_r, s_b = hgrn2_chunk_scan(jnp.flip(q, 1), jnp.flip(k_b, 1), jnp.flip(v, 1), jnp.flip(lf_b, 1), s0[:, 1])
    o_a = rms_norm(o_f + jnp.flip(o_r, 1), norm_g).reshape(B, L, W_A) * jax.nn.silu(ga.astype(f32))
    u = short_conv(hy, conv_w, conv_b).astype(f32)
    x0, x1, vh = jnp.split(u, 3, axis=-1)
    filt = hyena_filters(L, fw1, fb1, ffr1, fw2, fb2, ffr2, fw3)
    z = vh * x1
    z = fft_conv(z, filt[:, 0]) + jnp.flip(fft_conv(jnp.flip(z, 1), filt[:, 1]), 1) + hbias * z
    o_b = z * x0
    out = jnp.concatenate([o_a, o_b], axis=-1).astype(h.dtype) @ w_out
    return out, jnp.stack([s_f, s_b], axis=1)

def odd_mixer(h, ctx_kv, use_rope, w_in, w_out, cqg, ckg, dqg, dkg, lam, lam_init, subln_g):
    B, L, _ = h.shape
    p = h @ w_in
    qc, kc, vc, qd, kd, vd = jnp.split(p, ODD_SPLITS, axis=-1)
    qc = rms_norm(qc.reshape(B, L, H_C, HD_C), cqg)
    kc = rms_norm(kc.reshape(B, L, KV_C, HD_C), ckg)
    qd = rms_norm(qd.reshape(B, L, H_D, 2, DK_D), dqg)
    kd = rms_norm(kd.reshape(B, L, H_D, 2, DK_D), dkg)
    if use_rope:
        cos_c, sin_c = axial_rope(L, HD_C)
        qc = apply_rope(qc, cos_c, sin_c)
        kc = apply_rope(kc, cos_c, sin_c)
        cos_d, sin_d = axial_rope(L, DK_D)
        qd = apply_rope(qd, cos_d, sin_d)
        kd = apply_rope(kd, cos_d, sin_d)
    qc = qc.reshape(B, L, KV_C, G_C, HD_C).transpose(0, 2, 3, 1, 4)
    kc = kc.transpose(0, 2, 1, 3)
    vc = vc.reshape(B, L, KV_C, HD_C).transpose(0, 2, 1, 3)
    qd = qd.transpose(0, 2, 3, 1, 4)
    kd = kd.reshape(B, L, H_D, 2 * DK_D).transpose(0, 2, 1, 3)
    vd = vd.reshape(B, L, H_D, DV_D).transpose(0, 2, 1, 3)
    if ctx_kv is None:
        kc_all, vc_all, kd_all, vd_all = kc, vc, kd, vd
    else:
        kc_all = jnp.concatenate([ctx_kv[0].astype(kc.dtype), kc], axis=2)
        vc_all = jnp.concatenate([ctx_kv[1].astype(vc.dtype), vc], axis=2)
        kd_all = jnp.concatenate([ctx_kv[2].astype(kd.dtype), kd], axis=2)
        vd_all = jnp.concatenate([ctx_kv[3].astype(vd.dtype), vd], axis=2)
    oc = block_attention(qc, kc_all, vc_all).transpose(0, 3, 1, 2, 4).reshape(B, L, H_C * HD_C)
    o1 = block_attention(qd[:, :, 0:1], kd_all[..., :DK_D], vd_all)[:, :, 0]
    o2 = block_attention(qd[:, :, 1:2], kd_all[..., DK_D:], vd_all)[:, :, 0]
    od = rms_norm(o1 - lam * o2, subln_g) * (1.0 - lam_init)
    od = od.transpose(0, 2, 1, 3).reshape(B, L, H_D * DV_D)
    out = jnp.concatenate([oc, od.astype(oc.dtype)], axis=-1) @ w_out
    return out, kc, vc, kd, vd

def hier_moe(h, w_grp, b_grp, w_rt, b_rt, w_gate, w_up, w_down):
    B, L, D = h.shape
    t = h.reshape(B * L, D)
    g_prob = jax.nn.softmax((t @ w_grp + b_grp).astype(jnp.float32), axis=-1)
    g_p, g_i = lax.top_k(g_prob, 1)
    e_logits = (t @ w_rt + b_rt).astype(jnp.float32).reshape(-1, N_GROUPS, EXP_PER_GROUP)
    e_logits = jnp.take_along_axis(e_logits, g_i[:, :, None], axis=1)[:, 0]
    e_p, e_i = lax.top_k(jax.nn.softmax(e_logits, axis=-1), TOP_K)
    wts = g_p * e_p / jnp.sum(e_p, axis=-1, keepdims=True)
    idx = g_i * EXP_PER_GROUP + e_i
    gates = jnp.sum(jax.nn.one_hot(idx, N_EXPERTS, dtype=jnp.float32) * wts[..., None], axis=1)
    a = jnp.einsum('td,edf->tef', t, w_gate)
    u = jnp.einsum('td,edf->tef', t, w_up)
    hid = jax.nn.silu(a) * u * gates[..., None].astype(t.dtype)
    y = jnp.einsum('tef,efd->td', hid, w_down)
    return y.reshape(B, L, D)

def setup_inputs(seed: int = 0) -> dict:
    key = jax.random.key(seed)
    ks = jax.random.split(key, 45)
    f32 = jnp.float32

    def nrm(i, shape, scale):
        return scale * jax.random.normal(ks[i], shape, f32)

    def gain(i, shape):
        return 1.0 + 0.1 * jax.random.normal(ks[i], shape, f32)

    d_in = D_MODEL ** -0.5
    return {
        'x_prompt': nrm(0, (BATCH, SEQ, D_MODEL), 1.0),
        'x_sample': nrm(1, (DEC_BATCH, DEC_SEQ, D_MODEL), 1.0),
        'state_hgrn': nrm(2, (DEC_BATCH, N_EVEN, 2, H_A, DK_A, DV_A), 1.0),
        'cache_c_k': nrm(3, (DEC_BATCH, N_ODD, KV_C, PAST_LEN, HD_C), 1.0),
        'cache_c_v': nrm(4, (DEC_BATCH, N_ODD, KV_C, PAST_LEN, HD_C), 1.0),
        'cache_d_k': nrm(5, (DEC_BATCH, N_ODD, H_D, PAST_LEN, 2 * DK_D), 1.0),
        'cache_d_v': nrm(6, (DEC_BATCH, N_ODD, H_D, PAST_LEN, DV_D), 1.0),
        'c': nrm(7, (DEC_BATCH, D_MODEL), 1.0),
        'c_ctx': nrm(8, (D_MODEL,), 1.0),
        'norm1_g': gain(9, (DEPTH, D_MODEL)),
        'norm2_g': gain(10, (DEPTH, D_MODEL)),
        'w_mod': nrm(11, (DEPTH, D_MODEL, 6 * D_MODEL), 0.5 * d_in),
        'b_mod': nrm(12, (DEPTH, 6 * D_MODEL), 0.02),
        'even_w_in': nrm(13, (N_EVEN, D_MODEL, EVEN_IN), d_in),
        'even_w_out': nrm(14, (N_EVEN, MIX_AB, D_MODEL), MIX_AB ** -0.5),
        'hgrn_lower': nrm(15, (N_EVEN + 1, H_A * DK_A), 0.5),
        'hgrn_norm_g': gain(16, (N_EVEN, DV_A)),
        'hy_conv_w': nrm(17, (N_EVEN, SHORT_W, 3 * C_B), SHORT_W ** -0.5),
        'hy_conv_b': nrm(18, (N_EVEN, 3 * C_B), 0.02),
        'hy_w1': nrm(19, (N_EVEN, FILTER_EMB, FILTER_HIDDEN), FILTER_EMB ** -0.5),
        'hy_b1': nrm(20, (N_EVEN, FILTER_HIDDEN), 0.02),
        'hy_freq1': gain(21, (N_EVEN, FILTER_HIDDEN)),
        'hy_w2': nrm(22, (N_EVEN, FILTER_HIDDEN, FILTER_HIDDEN), FILTER_HIDDEN ** -0.5),
        'hy_b2': nrm(23, (N_EVEN, FILTER_HIDDEN), 0.02),
        'hy_freq2': gain(24, (N_EVEN, FILTER_HIDDEN)),
        'hy_w3': nrm(25, (N_EVEN, FILTER_HIDDEN, 2 * C_B), 0.1 * FILTER_HIDDEN ** -0.5),
        'hy_bias': nrm(26, (N_EVEN, C_B), 0.5),
        'odd_w_in': nrm(27, (N_ODD, D_MODEL, ODD_IN), d_in),
        'odd_w_out': nrm(28, (N_ODD, MIX_CD, D_MODEL), MIX_CD ** -0.5),
        'c_qnorm_g': gain(29, (N_ODD, HD_C)),
        'c_knorm_g': gain(30, (N_ODD, HD_C)),
        'd_qnorm_g': gain(31, (N_ODD, DK_D)),
        'd_knorm_g': gain(32, (N_ODD, DK_D)),
        'd_lambda_q1': nrm(33, (N_ODD, DK_D), 0.1),
        'd_lambda_k1': nrm(34, (N_ODD, DK_D), 0.1),
        'd_lambda_q2': nrm(35, (N_ODD, DK_D), 0.1),
        'd_lambda_k2': nrm(36, (N_ODD, DK_D), 0.1),
        'd_subln_g': gain(37, (N_ODD, DV_D)),
        'moe_w_grp': nrm(38, (DEPTH, D_MODEL, N_GROUPS), d_in),
        'moe_b_grp': nrm(39, (DEPTH, N_GROUPS), 0.01),
        'moe_w_rt': nrm(40, (DEPTH, D_MODEL, N_EXPERTS), d_in),
        'moe_b_rt': nrm(41, (DEPTH, N_EXPERTS), 0.01),
        'moe_w_gate': nrm(42, (DEPTH, N_EXPERTS, D_MODEL, D_EXPERT), d_in),
        'moe_w_up': nrm(43, (DEPTH, N_EXPERTS, D_MODEL, D_EXPERT), d_in),
        'moe_w_down': nrm(44, (DEPTH, N_EXPERTS, D_EXPERT, D_MODEL), D_EXPERT ** -0.5),
    }

def reference(x_prompt, x_sample, state_hgrn, cache_c_k, cache_c_v, cache_d_k, cache_d_v, c, c_ctx, norm1_g, norm2_g, w_mod, b_mod, even_w_in, even_w_out, hgrn_lower, hgrn_norm_g, hy_conv_w, hy_conv_b, hy_w1, hy_b1, hy_freq1, hy_w2, hy_b2, hy_freq2, hy_w3, hy_bias, odd_w_in, odd_w_out, c_qnorm_g, c_knorm_g, d_qnorm_g, d_knorm_g, d_lambda_q1, d_lambda_k1, d_lambda_q2, d_lambda_k2, d_subln_g, moe_w_grp, moe_b_grp, moe_w_rt, moe_b_rt, moe_w_gate, moe_w_up, moe_w_down):
    f32 = jnp.float32
    lower = jnp.cumsum(jax.nn.softmax(hgrn_lower.astype(f32), axis=0), axis=0)
    ctx = x_prompt
    lat = x_sample
    hgrn_states, ck_list, cv_list, dk_list, dv_list = [], [], [], [], []
    for l in range(DEPTH):
        j = l // 2
        m_ctx = adaln(c_ctx, w_mod[l], b_mod[l])
        m_lat = adaln(c, w_mod[l], b_mod[l])
        h_ctx = modulate(rms_norm(ctx, norm1_g[l]), m_ctx[0], m_ctx[1])
        h_lat = modulate(rms_norm(lat, norm1_g[l]), m_lat[0], m_lat[1])
        if l % 2 == 0:
            p = (even_w_in[j], even_w_out[j], lower[j].reshape(H_A, DK_A), hgrn_norm_g[j], hy_conv_w[j], hy_conv_b[j], hy_w1[j], hy_b1[j], hy_freq1[j], hy_w2[j], hy_b2[j], hy_freq2[j], hy_w3[j], hy_bias[j])
            s_zero = jnp.zeros((ctx.shape[0], 2, H_A, DK_A, DV_A), f32)
            o_ctx, s_ctx = even_mixer(h_ctx, s_zero, *p)
            o_lat, _ = even_mixer(h_lat, state_hgrn[:, j].astype(f32), *p)
            hgrn_states.append(s_ctx)
        else:
            lam_init = 0.8 - 0.6 * math.exp(-0.3 * l)
            lam = (jnp.exp(jnp.sum(d_lambda_q1[j].astype(f32) * d_lambda_k1[j].astype(f32)))
                   - jnp.exp(jnp.sum(d_lambda_q2[j].astype(f32) * d_lambda_k2[j].astype(f32))) + lam_init)
            p = (odd_w_in[j], odd_w_out[j], c_qnorm_g[j], c_knorm_g[j], d_qnorm_g[j], d_knorm_g[j], lam, lam_init, d_subln_g[j])
            o_ctx, kc, vc, kd, vd = odd_mixer(h_ctx, None, False, *p)
            o_lat, _, _, _, _ = odd_mixer(h_lat, (cache_c_k[:, j], cache_c_v[:, j], cache_d_k[:, j], cache_d_v[:, j]), True, *p)
            ck_list.append(kc)
            cv_list.append(vc)
            dk_list.append(kd)
            dv_list.append(vd)
        ctx = ctx + m_ctx[2] * o_ctx
        lat = lat + m_lat[2] * o_lat
        mp = (moe_w_grp[l], moe_b_grp[l], moe_w_rt[l], moe_b_rt[l], moe_w_gate[l], moe_w_up[l], moe_w_down[l])
        ctx = ctx + m_ctx[5] * hier_moe(modulate(rms_norm(ctx, norm2_g[l]), m_ctx[3], m_ctx[4]), *mp)
        lat = lat + m_lat[5] * hier_moe(modulate(rms_norm(lat, norm2_g[l]), m_lat[3], m_lat[4]), *mp)
    new_state_hgrn = jnp.stack(hgrn_states, axis=1)
    new_cache_c_k = jnp.stack(ck_list, axis=1)
    new_cache_c_v = jnp.stack(cv_list, axis=1)
    new_cache_d_k = jnp.stack(dk_list, axis=1)
    new_cache_d_v = jnp.stack(dv_list, axis=1)
    return (ctx, lat, new_state_hgrn, new_cache_c_k, new_cache_c_v, new_cache_d_k, new_cache_d_v)


_drawn_inputs = setup_inputs


def setup_inputs(seed=0):
    import zlib

    import numpy as np

    out = dict(_drawn_inputs(seed))
    spreads = {}
    factors = {'state_hgrn': 7.899,
     'cache_c_k': 4.809,
     'cache_c_v': 4.999,
     'hgrn_norm_g': 3.092,
     'hy_conv_b': 6.959,
     'hy_b1': 8.0,
     'hy_freq1': 8.0,
     'hy_b2': 8.0,
     'hy_freq2': 5.187,
     'c_qnorm_g': 8.0,
     'd_qnorm_g': 6.288,
     'd_lambda_q1': 5.439,
     'd_lambda_k1': 3.291,
     'd_lambda_q2': 6.833,
     'd_lambda_k2': 4.521,
     'd_subln_g': 3.944,
     'moe_b_grp': 8.0,
     'moe_b_rt': 7.27}
    for name, (base, spread) in spreads.items():
        noise = np.random.default_rng([zlib.crc32(name.encode()), seed]).standard_normal(out[name].shape)
        drawn = base * np.exp(spread * noise) if base else spread * noise
        out[name] = jnp.asarray(drawn.astype(out[name].dtype))
    for name, factor in factors.items():
        out[name] = (out[name] * factor).astype(out[name].dtype)
    return out
```

```python
import math
from contextlib import ExitStack

import concourse.bass as bass
import numpy as np
from concourse import mybir
from concourse.alu_op_type import AluOpType as ALU

ACT = mybir.ActivationFunctionType
F32 = mybir.dt.float32
U32 = mybir.dt.uint32
AX_X = mybir.AxisListType.X

P = 128
D = 1024
KD = D // P
SEQ, DEC = 128, 256
T = SEQ + DEC
NT = T // P
CTX, LAT = slice(0, SEQ), slice(SEQ, T)
SEGS = (CTX, LAT)
DEPTH = 2
EPS = 1e-6
H = 4
BLK = 32
NBLK = P // BLK
HALF = 512
NHID = 64
NFEAT = 33
NE = 16
NG = 4
EPG = 4
FE = 512
NF = FE // P
LAM_INIT = 0.8 - 0.6 * math.exp(-0.3)
MAGIC = 1.5 * 2.0**23
TWO_PI_HI = 6.28125
TWO_PI_LO = 2 * math.pi - 6.28125
PI_BELOW = 3.1415925
BANKS = 8
PROJ_SLOTS = 3

MOD_BLOCKS = 6 * D // HALF
EVEN_ORDER = ["hy0", "hy1", "hy2", "q", "v", "ff", "fb", "g"]
EVEN_COLUMN = {"q": 0, "ff": 1, "fb": 2, "v": 3, "g": 4, "hy0": 5, "hy1": 6, "hy2": 7}
ODD_ORDER = ["qc", "kv", "qd", "kd", "vd"]
STREAM = (
    [("mod", 0, b) for b in range(MOD_BLOCKS)]
    + [("even", n) for n in EVEN_ORDER]
    + [("even_out", b) for b in range(2)]
    + [("mod", 1, b) for b in range(MOD_BLOCKS)]
    + [("odd", n) for n in ODD_ORDER]
    + [("odd_out", b) for b in range(2)]
)
LAYER_BLOCKS = [MOD_BLOCKS + len(EVEN_ORDER) + 2, MOD_BLOCKS + len(ODD_ORDER) + 2]


class Columns:

    def __init__(self, widths):
        self.at, self.total = {}, 0
        for name, width in widths:
            self.at[name] = (self.total, width)
            self.total += width

    def of(self, tensor, name, parts=P):
        start, width = self.at[name]
        return tensor[0:parts, start : start + width]


PARAMS = Columns([
    ("cond", KD * 2), ("b_mod", DEPTH * 48), ("n1", DEPTH * KD), ("n2", DEPTH * KD),
    ("conv_w", 3 * 12), ("conv_b", 12), ("hgrn_g", 1), ("subln_g", 1),
    ("hb1", 1), ("hf1", 1), ("hb2", 1), ("hf2", 1), ("hy_bias", 4),
    ("lower", 2 * HALF), ("cq", P), ("ck", P), ("dq", 64), ("dk", 64),
    ("lam", 4 * 64), ("b_rt", DEPTH * 20), ("w_rt", DEPTH * KD * 20),
])
HYPAR = Columns([("w1", NHID), ("w2", NHID), ("w3", 2 * HALF)])
CONSTS = Columns([
    ("ident", P), ("ones", P), ("eps", 1), ("iota16", NE),
    ("mid0", P), ("inc0", P), ("mid1", P), ("inc1", P), ("last0", P), ("last1", P),
    ("cosc", 2 * 64), ("sinc", 2 * 64), ("cosd", 2 * 32), ("sind", 2 * 32),
])
HYCONST = Columns([
    ("pos", T), ("window", NT * HALF), ("dft_lat", 2 * 768), ("dft_ctx", 512),
    ("inv_lat", 4 * DEC), ("inv_ctx", 2 * SEQ),
])


class Banks:

    def __init__(self):
        self.at, self.used, self.next = {}, [0] * BANKS, 0

    def take(self, *name):
        bank = self.next
        self.next = (bank + 1) % BANKS
        self.used[bank] += 1
        self.at[name] = (bank, self.used[bank])


GATEUP_BANKS, DOWN_BANKS = 4, 4
MOE_GROUPS = [(q % GATEUP_BANKS) for q in range(2 * NF)] + [GATEUP_BANKS + d % DOWN_BANKS for d in range(2 * NT)]
MOE_USES = [MOE_GROUPS.count(b) for b in range(BANKS)]
UNITS = [(0, 0), (1, 0), (0, 1), (1, 2), (0, 2), (1, 1)]
def even_groups(name):
    return NT if name in ("v", "ff", "fb") else 4


ATTN = [("c", h, i) for h in range(H) for i in range(NT)] + [("d", h, i) for h in range(H) for i in range(NT)]
SCAN_GROUPS = {"decays": ("b01", "b23", "kT", "rl"), "products": ("sc", "U0", "U1", "U2", "U3"), "out": ("o",)}
SCAN_ORDER = [("decays", 0)]
for _u in range(len(UNITS)):
    SCAN_ORDER += ([("decays", _u + 1)] if _u + 1 < len(UNITS) else []) + [("products", _u), ("out", _u)]
FILTER_DFT = [("lat", "re", 0), ("lat", "re", 1), ("lat", "im", 0), ("lat", "im", 1), ("lat", "re2", 0),
              ("ctx", "re", 0), ("ctx", "im", 0), ("ctx", "re2", 0)]
SIGNAL_DFT = [("lat", 0), ("lat", 1), ("ctx", 0)]


def plan_banks():
    banks = Banks()
    moe_base = []
    for layer in range(DEPTH):
        banks.take("mod", layer)
        banks.take("norm1", layer)
        if layer == 0:
            banks.take("hf1")
            banks.take("hf2")
            for i in range(NT):
                for half in range(2):
                    banks.take("hf3", i, half)
            for g in range(len(FILTER_DFT)):
                banks.take("G", g)
            for name in EVEN_ORDER:
                for j in range(even_groups(name)):
                    banks.take("even", name, j)
                if name == "hy2":
                    for i in range(NT):
                        banks.take("zt", i)
                    for s in range(len(SIGNAL_DFT)):
                        banks.take("Ur", s)
                        banks.take("Ui", s)
                    for c in range(4):
                        banks.take("inv", c)
            for stage, u in SCAN_ORDER:
                for g in SCAN_GROUPS[stage]:
                    banks.take("scan", u, g)
            for h in range(H):
                banks.take("on", h)
        else:
            for name in ODD_ORDER:
                for i in range(NT):
                    banks.take("odd", name, i)
            for name in ("qc", "kv", "qd", "kd"):
                for i in range(NT):
                    banks.take("tr", name, i)
            order = []
            for u in range(len(ATTN) + 2):
                if u < len(ATTN):
                    order += [("S", u, m) for m in range(2 if ATTN[u][0] == "d" else 1)]
                if 0 < u <= len(ATTN):
                    order.append(("PT", u - 1))
                if u > 1:
                    order.append(("O", u - 2))
            for name in order:
                banks.take(*name)
            for h in range(H):
                banks.take("sn", h)
        for j in range(KD):
            banks.take("out", layer, j)
        banks.take("norm2", layer)
        for i in range(NT):
            banks.take("rt", layer, i)
        moe_base.append(list(banks.used))
        banks.used = [u + NE * n for u, n in zip(banks.used, MOE_USES)]
        banks.next = 0
        for c in range(KD):
            banks.take("yt", layer, c)
    return banks, moe_base


def trunk_kernel(nc, params_d, hypar_d, consts_d, hyconst_d, x_d, s0_d, ck_d, cv_d, dk_d, dv_d,
                 proj_d, moe_d, y_d, state_d, ock_d, ocv_d, odk_d, odv_d):
    banks, moe_base = plan_banks()
    with ExitStack() as ctx:
        def sb(name, shape, dt=F32):
            return ctx.enter_context(nc.sbuf_tensor(name, shape, dt))

        def sem(name):
            return ctx.enter_context(nc.semaphore(name))

        xT = sb("xT", [P, KD, T])
        hT = sb("hT", [P, KD, T])
        cT = sb("cT", [P, KD, T])
        par = sb("par", [P, PARAMS.total])
        con = sb("con", [P, CONSTS.total])
        ring = sb("ring", [P, PROJ_SLOTS, KD * HALF])
        mod = sb("mod", [P, DEPTH, 48, 2])
        gs = sb("gs", [P, DEPTH, 2, KD, 2])
        condT = sb("condT", [P, KD, 2])
        rs = sb("rs", [P, T])
        lnt = sb("lnt", [P, T])
        stats = sb("stats", [P, 64])
        arena_cols = 26700
        arena = sb("arena", [P, arena_cols])
        psum = [ctx.enter_context(nc.psum_tensor(f"bank{b}", [P, HALF], F32)) for b in range(BANKS)]

        def carve(shapes):
            out, at = {}, 0
            for name, shape in shapes:
                n = int(np.prod(shape))
                view = arena[:, at : at + n]
                if len(shape) == 2:
                    view = view.rearrange("p (a b) -> p a b", a=shape[0])
                elif len(shape) == 3:
                    view = view.rearrange("p (a b c) -> p a b c", a=shape[0], b=shape[1])
                out[name] = view
                at += n
            assert at <= arena_cols, at
            return out

        hy = carve([("hyc", (HYCONST.total,)), ("hyp", (HYPAR.total,)), ("G", (8, HALF)),
                    ("u", (12, T)), ("hp", (NT, HALF)), ("hm", (NT, HALF)),
                    ("a", (HALF,)), ("b", (HALF,)), ("n", (T,)), ("s", (T,))])
        hz = carve([("hyc", (HYCONST.total,)), ("hyp", (HYPAR.total,)), ("G", (8, HALF)),
                    ("u", (12, T)), ("z_tm", (NT, HALF)), ("Z", (6, HALF)),
                    ("t1", (HALF,)), ("t2", (HALF,))])
        z_tm, Z = hz["z_tm"], hz["Z"]
        sc = carve([("q", (H, T)), ("v", (NT, HALF)), ("lf0", (NT, HALF)), ("lf1", (NT, HALF)),
                    ("k0", (NT, HALF)), ("k1", (NT, HALF)), ("g", (H, T)), ("o", (H, T)),
                    ("vx", (H, NBLK, P)), ("S", (2, H, (NBLK - 1) * P)), ("s0", (2, H, P)), ("carry", (4, H, P)),
                    ("ep", (2, H, P)), ("en", (2, H, P)), ("ei", (2, H, P)), ("el", (2, H, P)),
                    ("P0", (H, P)), ("P1", (H, P)), ("decay", (2, H, NBLK))])
        at = carve([("vc", (4, 2 * P)), ("vd", (4, HALF)), ("qcT", (H, T)), ("kcT", (2, 4 * P)),
                    ("qd0", (H, T)), ("qd1", (H, T)), ("kdT", (H, 4 * P)), ("raw0", (NT, HALF)),
                    ("raw1", (NT, HALF)), ("raw2", (NT, HALF)), ("raw3", (NT, HALF)),
                    ("t", (4, HALF)), ("t2", (4, HALF)), ("ss", (4, 24)), ("lt", (4, 24)), ("lam", (8,)),
                    ("od", (H, T)), ("Pb", (4, T)), ("PT", (2, T)), ("mx", (2, 8))])
        mo = carve([("ring", (3, KD * HALF)), ("hid", (NF, T)), ("sg", (2, T)),
                    ("lg", (NT, 20)), ("l8", (NT, 8)), ("m8", (NT, 8)), ("i8", (NT, 8)), ("f8", (NT, 8)),
                    ("oh", (NT, NG)), ("ml", (NT, NE)), ("m2", (NT, 8)), ("w", (NT, 8)), ("e4", (NT, NG)),
                    ("g1", (NT, NE)), ("gates", (NT, NE))])

        params_in, consts_in, hyc_in, x_in = sem("params_in"), sem("consts_in"), sem("hyc_in"), sem("x_in")
        s0_in, caches_in = sem("s0_in"), sem("caches_in")
        slot_loaded = [sem(f"slot_loaded{s}") for s in range(2 * PROJ_SLOTS)]
        bank_full = [sem(f"bank_full{b}") for b in range(BANKS)]
        bank_free = [sem(f"bank_free{b}") for b in range(BANKS)]
        mod_blocks = sem("mod_blocks")
        dve_link, act_link, pool_link = sem("dve_link"), sem("act_link"), sem("pool_link")
        cond_ready, mod_ready, lb_diff, lb_exp = sem("cond_ready"), sem("mod_ready"), sem("lb_diff"), sem("lb_exp")
        squares_ready, rs_ready, scaled, h_ready = sem("squares_ready"), sem("rs_ready"), sem("scaled"), sem("h_ready")
        sin_arg, sin_done, filter_ready = sem("sin_arg"), sem("sin_done"), sem("filter_ready")
        conv_bias, z_ready, spec_ready, hyena_done = sem("conv_bias"), sem("z_ready"), sem("spec_ready"), sem("hyena_done")
        f_ready, lf_ready, zeroed, vx_ready = sem("f_ready"), sem("lf_ready"), sem("zeroed"), sem("vx_ready")
        exps_ready, qk_scaled, probs_masked, states_ready = sem("exps_ready"), sem("qk_scaled"), sem("probs_masked"), sem("states_ready")
        head_squares, head_rs, mixed = sem("head_squares"), sem("head_rs"), sem("mixed")
        ss_ready, qk_rs, normed, roped = sem("ss_ready"), sem("qk_rs"), sem("normed"), sem("roped")
        lam_dots, lam_exps, pads_zero = sem("lam_dots"), sem("lam_exps"), sem("pads_zero")
        neg_max, probs_ready = sem("neg_max"), sem("probs_ready")
        route_max, route_exp = sem("route_max"), sem("route_exp")
        state_out, cache_out, y_out = sem("state_out"), sem("cache_out"), sem("y_out")

        def full(eng, *name):
            b, n = banks.at[name]
            eng.wait_ge(bank_full[b], n)

        def bank(*name):
            return psum[banks.at[name][0]]

        def freed(eng, *name):
            b, n = banks.at[name]
            eng.wait_ge(bank_free[b], n)

        def free_of(*name):
            return bank_free[banks.at[name][0]]

        def full_of(*name):
            return bank_full[banks.at[name][0]]

        def residual(eng, adds):
            freed(eng, "out" if adds % 2 else "yt", (adds - 1) // 2, KD - 1)

        def state_before(u, n, h):
            if n:
                return sc["S"][:, UNITS[u][0], h, P * (n - 1) : P * n]
            return None if u < 2 else sc["s0"][:, UNITS[u][0], h, :] if u < 4 else sc["carry"][:, u - 2, h, :]

        c = lambda name: CONSTS.of(con, name)
        pr = lambda name, parts=P: PARAMS.of(par, name, parts)
        ident, ones, eps = c("ident"), c("ones"), c("eps")
        n1 = pr("n1").rearrange("p (l k) -> p l k", l=DEPTH)
        n2 = pr("n2").rearrange("p (l k) -> p l k", l=DEPTH)
        hyc = lambda name: HYCONST.of(hy["hyc"], name)
        hyp = lambda name, parts: HYPAR.of(hy["hyp"], name, parts)
        dft = {"lat": hyc("dft_lat").rearrange("p (k n) -> p k n", k=2),
               "ctx": hyc("dft_ctx").rearrange("p (k n) -> p k n", k=1)}
        seq_tiles = {"ctx": [0], "lat": [1, 2]}
        n_freq = {"ctx": 1, "lat": 2}
        inv_lat = hyc("inv_lat").rearrange("p (f t) -> p f t", f=4)
        inv_ctx = hyc("inv_ctx").rearrange("p (f t) -> p f t", f=2)
        window = hyc("window").rearrange("p (i n) -> p i n", i=NT)
        conv_w = pr("conv_w").rearrange("p (t c) -> p t c", t=3)
        lower = pr("lower").rearrange("p (r n) -> p r n", r=2)
        lb, omlb = lower[:, 0, :], lower[:, 1, :]

        def dft_columns(seq, part, m):
            n = n_freq[seq] * P
            start = {"re": m * P, "im": n + m * P, "imp": 2 * n if m == 0 else n + m * P, "re2": 2 * n + P}[part]
            return slice(start, start + P)

        def slot_of(n):
            layer = 0 if n < LAYER_BLOCKS[0] else 1
            first = 0 if layer == 0 else LAYER_BLOCKS[0]
            s = (n - first) % PROJ_SLOTS
            earlier = sum(1 for m in range(first) if m % PROJ_SLOTS == s) + (NE // 2 if layer else 0)
            return s, earlier + (n - first) // PROJ_SLOTS + 1

        index = {name: n for n, name in enumerate(STREAM)}

        def last_group(name):
            if name[0] == "mod":
                return ("mod", name[1])
            if name[0] == "even":
                return ("even", name[1], even_groups(name[1]) - 1)
            if name[0] == "odd":
                return ("odd", name[1], NT - 1)
            return ("out", 0 if name[0] == "even_out" else 1, 4 * name[1] + 3)

        def moe_block(side, kind):
            return (mo["ring"] if side else ring)[:, kind, :]

        def moe_loaded(side, kind):
            return slot_loaded[PROJ_SLOTS * side + kind]

        def moe_loads(layer, side, kind):
            if side:
                return layer * NE // 2
            return sum(slot_of(n)[0] == kind for n in range(sum(LAYER_BLOCKS[: layer + 1]))) + layer * NE // 2

        def moe_count(layer, g, e, uses=None):
            b = MOE_GROUPS[g]
            uses = MOE_GROUPS[: g + 1].count(b) if uses is None else uses
            return e * MOE_USES[b] + (moe_base[layer][b] + uses)

        block = ctx.enter_context(nc.Block())

        @block.sync
        def _(sp):
            sp.dma_start(par[:, :], params_d).then_inc(params_in, 16)
            sp.dma_start(xT[:, :, :], x_d).then_inc(x_in, 16)
            sp.dma_start(con[:, :], consts_d).then_inc(consts_in, 16)

            def load_blocks(first, count):
                for n in range(first, first + count):
                    s, _ = slot_of(n)
                    before = n - PROJ_SLOTS
                    if before >= first:
                        kind, layer_or_name = STREAM[before][:2]
                        if kind == "mod" and STREAM[before][2] < MOD_BLOCKS - 1:
                            sp.wait_ge(mod_blocks, layer_or_name * (MOD_BLOCKS - 1) + STREAM[before][2] + 1)
                        else:
                            full(sp, *last_group(STREAM[before]))
                    sp.dma_start(ring[:, s, :], proj_d[n]).then_inc(slot_loaded[s], 16)
                    if n == 2:
                        sp.dma_start(hy["hyc"], hyconst_d).then_inc(hyc_in, 16)
                        sp.dma_start(hy["hyp"], hypar_d).then_inc(hyc_in, 16)

            def load_experts(layer):
                end = sum(LAYER_BLOCKS[: layer + 1])
                for n in range(end - PROJ_SLOTS, end):
                    full(sp, *last_group(STREAM[n]))

                def load(i, side, kind):
                    at_block = i * 6 + (layer * NE * 3 + 3 * side + kind)
                    sp.dma_start(moe_block(side, kind),
                                 moe_d[bass.ds(at_block, 1)].rearrange("o p n -> p (o n)")).then_inc(moe_loaded(side, kind), 16)

                for kind in range(3):
                    load(0, 0, kind)
                sp.wait_ge(mixed, H * (layer + 1))
                if layer == 0:
                    sp.wait_ge(state_out, 32)
                else:
                    sp.wait_ge(cache_out, 64)
                for kind in range(3):
                    load(0, 1, kind)
                with sp.Fori(1, NE // 2) as i:
                    for side in range(2):
                        for kind in range(3):
                            g = 2 * (NF - 1) + kind if kind < 2 else 2 * NF + 2 * NT - 1
                            sp.wait_ge(bank_full[MOE_GROUPS[g]], moe_count(layer, g, i * 2 + (side - 2)))
                            load(i, side, kind)

            load_blocks(0, LAYER_BLOCKS[0])
            load_experts(0)
            g = 2 * NF + 2 * NT - 1
            sp.wait_ge(bank_full[MOE_GROUPS[g]], moe_count(0, g, NE - 1))
            load_blocks(LAYER_BLOCKS[0], LAYER_BLOCKS[1])
            load_experts(1)
            for k in range(KD):
                freed(sp, "yt", 1, k)
                sp.dma_start(y_d[:, k, :], xT[:, k, :]).then_inc(y_out, 16)
            sp.wait_ge(y_out, 16 * KD)

        @block.gpsimd
        def _(pool):
            pool.wait_ge(hyena_done, 4)
            nc.gpsimd.memset(sc["vx"], 0.0).then_inc(zeroed, 1)
            nc.gpsimd.memset(sc["P0"], 0.0).then_inc(zeroed, 1)
            nc.gpsimd.memset(sc["P1"], 0.0).then_inc(zeroed, 1)
            pool.dma_start(sc["s0"], s0_d).then_inc(s0_in, 16)
            pool.wait_ge(zeroed, 3)
            for u, (d, i) in enumerate(UNITS):
                freed(pool, "even", "v", i)
                if u:
                    for h in range(H):
                        full(pool, "scan", u - 1, f"U{h}")
                for j in range(NBLK):
                    rows = slice(BLK * j, BLK * j + BLK)
                    nc.gpsimd.tensor_copy(
                        sc["vx"][rows, :, j, :], sc["v"][rows, i, :].rearrange("p (h n) -> p h n", h=H)
                    ).then_inc(vx_ready, 1)
                if u in (1, 2):
                    freed(pool, "scan", u - 1, "U3")
                    pool.dma_start(state_d[u - 1], sc["carry"][:, u - 1]).then_inc(state_out, 16)
            pool.wait_ge(state_out, 32)
            freed(pool, "yt", 0, KD - 1)
            nc.gpsimd.memset(at["qd0"][64:P], 0.0).then_inc(pads_zero, 1)
            nc.gpsimd.memset(at["qd1"][0:64], 0.0).then_inc(pads_zero, 1)
            for dst, src in ((at["kcT"][:, :, P : 2 * P], ck_d), (at["kdT"][:, :, P : 2 * P], dk_d),
                             (at["vc"][:, 1, :], cv_d), (at["vd"][:, 1, :], dv_d)):
                pool.dma_start(dst, src).then_inc(caches_in, 16)
            pool.wait_ge(normed, 2)
            pool.dma_start(ock_d, at["raw1"][:, 0, 0 : 2 * P]).then_inc(cache_out, 16)
            freed(pool, "odd", "kv", 0)
            pool.dma_start(ocv_d, at["vc"][:, 0, :]).then_inc(cache_out, 16)
            pool.wait_ge(normed, 4)
            pool.dma_start(odk_d, at["raw3"][:, 0, :]).then_inc(cache_out, 16)
            freed(pool, "odd", "vd", 0)
            pool.dma_start(odv_d, at["vd"][:, 0, :]).then_inc(cache_out, 16)
            pool.wait_ge(cache_out, 64)

        @block.scalar
        def _(act):
            links = [0]

            def link(ins):
                links[0] += 1
                ins.then_inc(act_link, 1)
                act.wait_ge(act_link, links[0])

            def norm(layer, which):
                count = 2 * layer + which
                if count:
                    residual(act, count)
                for k in range(KD):
                    nc.scalar.activation(hT[:, k, :], xT[:, k, :], ACT.Square).then_inc(squares_ready, 1)
                name = (f"norm{which + 1}", layer)
                full(act, *name)
                nc.scalar.activation(lnt[:, :], bank(*name)[:, 0:T], ACT.Ln, bias=eps, scale=1.0 / D).then_inc(free_of(*name), 1)
                freed(act, *name)
                nc.scalar.activation(rs[:, :], lnt[:, :], ACT.Exp, scale=-0.5).then_inc(rs_ready, 1)
                act.wait_ge(mod_ready, layer + 1)
                for k in range(KD):
                    for s, seg in enumerate(SEGS):
                        act.wait_ge(scaled, count * 2 * KD + 2 * k + s + 1)
                        nc.scalar.activation(hT[:, k, seg], hT[:, k, seg], ACT.Identity,
                                             bias=mod[:, layer, 24 * which + k, s : s + 1]).then_inc(h_ready, 1)

            def head_norm(count, groups, src, sq):
                nc.scalar.activation(sq, src, ACT.Square).then_inc(head_squares, 1)
                for h in range(H):
                    full(act, groups, h)
                    if h:
                        act.wait_ge(head_rs, H * count + h)
                    nc.scalar.activation(lnt[:, :], bank(groups, h)[:, 0:T], ACT.Ln, bias=eps, scale=1.0 / P).then_inc(free_of(groups, h), 1)
                    freed(act, groups, h)
                    if h:
                        act.wait_ge(mixed, H * count + h)
                    nc.scalar.activation(rs[:, :], lnt[:, :], ACT.Exp, scale=-0.5).then_inc(head_rs, 1)

            def experts(layer):
                act.wait_ge(route_max, 2 * layer + 1)
                nc.scalar.activation(mo["e4"], mo["e4"], ACT.Exp).then_inc(route_exp, 1)
                act.wait_ge(route_max, 2 * layer + 2)
                nc.scalar.activation(mo["w"][:, :, 0:1], mo["w"][:, :, 0:1], ACT.Exp).then_inc(route_exp, 1)
                with act.Fori(0, NE // 2) as i:
                    for side in range(2):
                        for f in range(NF):
                            g, up = 2 * f, 2 * f + 1
                            act.wait_ge(bank_free[MOE_GROUPS[up]], moe_count(layer, up, i * 2 + side, f // 2))
                            act.wait_ge(bank_full[MOE_GROUPS[g]], moe_count(layer, g, i * 2 + side))
                            nc.scalar.activation(mo["sg"][:, f % 2, :], psum[MOE_GROUPS[g]][:, 0:T],
                                                 ACT.Silu).then_inc(bank_free[MOE_GROUPS[g]], 1)

            act.wait_ge(params_in, 16)
            nc.scalar.activation(condT[:, :, :], pr("cond").rearrange("p (k s) -> p k s", s=2), ACT.Silu).then_inc(cond_ready, 1)
            act.wait_ge(lb_diff, 1)
            nc.scalar.activation(omlb, omlb, ACT.Exp).then_inc(lb_exp, 1)
            act.wait_ge(x_in, 16)
            act.wait_ge(consts_in, 16)
            norm(0, 0)
            for step in range(2):
                act.wait_ge(sin_arg, step + 1)
                nc.scalar.activation(hy["s"][0:NHID, :], hy["n"][0:NHID, :], ACT.Sin).then_inc(sin_done, 1)
            for g in range(len(FILTER_DFT)):
                full(act, "G", g)
                nc.scalar.activation(hy["G"][:, g, :], bank("G", g)[:, :], ACT.Copy).then_inc(free_of("G", g), 1)
            for name in EVEN_ORDER:
                for j in range(even_groups(name)):
                    full(act, "even", name, j)
                    ps = bank("even", name, j)
                    if name.startswith("hy"):
                        ch = 4 * int(name[2]) + j
                        nc.scalar.activation(hy["u"][:, ch, :], ps[:, 0:T], ACT.Identity,
                                             bias=pr("conv_b")[:, ch : ch + 1],
                                             scale=conv_w[:, 1, ch : ch + 1]).then_inc(conv_bias, 1)
                    elif name in ("q", "g"):
                        nc.scalar.activation(sc[name][:, j, :], ps[:, 0:T], ACT.Silu).then_inc(free_of("even", name, j), 1)
                    elif name == "v":
                        nc.scalar.activation(sc["v"][:, j, :], ps[:, :], ACT.Copy).then_inc(free_of("even", name, j), 1)
                    else:
                        kk = sc["k0" if name == "ff" else "k1"]
                        nc.scalar.activation(kk[:, j, :], ps[:, :], ACT.Sigmoid).then_inc(free_of("even", name, j), 1)
                if name == "hy2":
                    for i in range(NT):
                        full(act, "zt", i)
                        if i == 0:
                            full(act, "G", len(FILTER_DFT) - 1)
                        nc.scalar.activation(z_tm[:, i, :], bank("zt", i)[:, :], ACT.Copy).then_inc(free_of("zt", i), 1)
                    act.wait_ge(hyena_done, 4)
            for d in range(2):
                for i in range(NT):
                    act.wait_ge(f_ready, NT * d + i + 1)
                    lf = sc[f"lf{d}"][:, i, :]
                    nc.scalar.activation(lf, lf, ACT.Ln).then_inc(lf_ready, 1)
            for u in range(len(UNITS)):
                b = u % 2
                if u >= 2:
                    full(act, "scan", u - 2, "o")
                    full(act, "scan", u - 2, "U3")
                    full(act, "scan", u - 2, "sc")
                for pair, g in enumerate(("b01", "b23")):
                    full(act, "scan", u, g)
                    ps = bank("scan", u, g)[:, :].rearrange("p (h c n) -> p h c n", h=2, c=2)
                    hs = slice(2 * pair, 2 * pair + 2)
                    nc.scalar.activation(sc["ep"][:, b, hs, :], ps[:, :, 0, :], ACT.Exp).then_inc(exps_ready, 1)
                    nc.scalar.activation(sc["en"][:, b, hs, :], ps[:, :, 0, :], ACT.Exp, scale=-1.0).then_inc(exps_ready, 1)
                    nc.scalar.activation(sc["ei"][:, b, hs, :], ps[:, :, 1, :], ACT.Exp).then_inc(free_of("scan", u, g), 1)
                full(act, "scan", u, "rl")
                nc.scalar.activation(sc["el"][:, b], bank("scan", u, "rl")[:, :].rearrange("p (h n) -> p h n", h=H),
                                     ACT.Exp).then_inc(free_of("scan", u, "rl"), 1)
            for u in range(len(UNITS)):
                freed(act, "scan", u, "o")
            head_norm(0, "on", sc["o"], sc["vx"].rearrange("p h j n -> p (h j n)")[:, 0 : H * T].rearrange("p (h n) -> p h n", h=H))
            norm(0, 1)
            experts(0)
            norm(1, 0)
            for b, name in enumerate(ODD_ORDER):
                for i in range(NT):
                    full(act, "odd", name, i)
                    ps = bank("odd", name, i)
                    done = free_of("odd", name, i)
                    slot = (0, 2, 3)[i]
                    if name == "vd":
                        nc.scalar.activation(at["vd"][:, slot, :], ps[:, :], ACT.Copy).then_inc(done, 1)
                    elif name == "kv":
                        nc.scalar.activation(at["raw1"][:, i, 0 : 2 * P], ps[:, 0 : 2 * P], ACT.Copy)
                        nc.scalar.activation(at["vc"][:, slot, :], ps[:, 2 * P :], ACT.Copy).then_inc(done, 1)
                    else:
                        nc.scalar.activation(at[f"raw{b}"][:, i, :], ps[:, :], ACT.Copy).then_inc(done, 1)
                    if name == "vd" and i == 0:
                        act.wait_ge(lam_dots, 1)
                        nc.scalar.activation(at["lam"][:, 2:4], at["lam"][:, 0:2], ACT.Exp).then_inc(lam_exps, 1)
            for b, n in enumerate((4, 2, 8, 8)):
                act.wait_ge(ss_ready, b + 1)
                link(nc.scalar.activation(at["lt"][:, b, 0 : NT * n], at["ss"][:, b, 0 : NT * n], ACT.Ln, bias=eps,
                                          scale=1.0 / (P if b < 2 else 64)))
                nc.scalar.activation(at["ss"][:, b, 0 : NT * n], at["lt"][:, b, 0 : NT * n], ACT.Exp, scale=-0.5).then_inc(qk_rs, 1)
            act.wait_ge(pads_zero, 2)
            for b, name in enumerate(("qc", "kv", "qd", "kd")):
                for i in range(NT):
                    full(act, "tr", name, i)
                    ps = bank("tr", name, i)[:, :].rearrange("p (h n) -> p h n", h=H)
                    done = free_of("tr", name, i)
                    cols, slot = slice(P * i, P * i + P), (0, 2, 3)[i]
                    keys = slice(P * slot, P * slot + P)
                    if name == "qc":
                        nc.scalar.activation(at["qcT"][:, :, cols], ps, ACT.Copy).then_inc(done, 1)
                    elif name == "kv":
                        nc.scalar.activation(at["kcT"][:, :, keys], ps[:, 0:2, :], ACT.Copy).then_inc(done, 1)
                    elif name == "qd":
                        nc.scalar.activation(at["qd0"][0:64, :, cols], ps[0:64], ACT.Copy)
                        nc.scalar.activation(at["qd1"][64:P, :, cols], ps[64:P], ACT.Copy).then_inc(done, 1)
                    else:
                        nc.scalar.activation(at["kdT"][:, :, keys], ps, ACT.Copy).then_inc(done, 1)
            maps_done = 0
            for u in range(len(ATTN) + 2):
                if u < len(ATTN):
                    kind, h, i = ATTN[u]
                    nk = P if i == 0 else 3 * P
                    for m in range(2 if kind == "d" else 1):
                        maps_done += 1
                        act.wait_ge(neg_max, maps_done)
                        if u >= 2:
                            full(act, "PT", u - 2)
                        col = 4 * m
                        nc.scalar.activation(at["Pb"][:, 2 * (u % 2) + m, 0:nk], bank("S", u, m)[:, 0:nk], ACT.Exp,
                                             bias=at["mx"][:, u % 2, col + 1 : col + 2],
                                             scale=(P if kind == "c" else 64) ** -0.5,
                                             accum_out=at["mx"][:, u % 2, col + 2 : col + 3]).then_inc(free_of("S", u, m), 1)
                if 0 < u <= len(ATTN):
                    i = ATTN[u - 1][2]
                    nk = P if i == 0 else 3 * P
                    full(act, "PT", u - 1)
                    if u >= 3:
                        full(act, "O", u - 3)
                    nc.scalar.activation(at["PT"][:, (u - 1) % 2, 0:nk], bank("PT", u - 1)[:, 0:nk], ACT.Copy).then_inc(free_of("PT", u - 1), 1)
                if u > 1:
                    kind, h, i = ATTN[u - 2]
                    cols = slice(P * i, P * i + P)
                    full(act, "O", u - 2)
                    dst = cT[:, h, cols] if kind == "c" else at["od"][:, h, cols]
                    nc.scalar.activation(dst, bank("O", u - 2)[:, 0:P], ACT.Copy).then_inc(free_of("O", u - 2), 1)
            freed(act, "O", len(ATTN) - 1)
            head_norm(1, "sn", at["od"], at["raw0"].rearrange("p i n -> p (i n)").rearrange("p (h n) -> p h n", h=H))
            norm(1, 1)
            experts(1)

        @block.vector
        def _(dve):
            links = [0]

            def link(ins):
                links[0] += 1
                ins.then_inc(dve_link, 1)
                dve.wait_ge(dve_link, links[0])

            V = nc.vector

            def modulation(layer):
                full(dve, "mod", layer)
                m = mod[:, layer]
                b_mod = pr("b_mod").rearrange("p (l n) -> p l n", l=DEPTH)[:, layer]
                V.tensor_tensor(m, bank("mod", layer)[:, 0:96].rearrange("p (n s) -> p n s", s=2),
                                b_mod.unsqueeze(2).to_broadcast([P, 48, 2]), ALU.add).then_inc(free_of("mod", layer), 1)
                freed(dve, "mod", layer)
                for which, gain in enumerate((n1, n2)):
                    g = gain[:, layer].unsqueeze(2).to_broadcast([P, KD, 2])
                    ins = V.scalar_tensor_tensor(gs[:, layer, which], m[:, 24 * which + KD : 24 * which + 2 * KD, :], 1.0, g,
                                                 ALU.add, ALU.mult)
                    if which == 0:
                        link(ins)
                    else:
                        ins.then_inc(mod_ready, 1)
                dve.wait_ge(mod_ready, layer + 1)

            def norm(layer, which):
                count = 2 * layer + which
                dve.wait_ge(rs_ready, count + 1)
                if count == 0:
                    dve.wait_ge(x_in, 16)
                else:
                    residual(dve, count)
                for k in range(KD):
                    for s, seg in enumerate(SEGS):
                        ins = V.scalar_tensor_tensor(hT[:, k, seg], xT[:, k, seg], gs[:, layer, which, k, s : s + 1],
                                                     rs[:, seg], ALU.mult, ALU.mult)
                        ins.then_inc(scaled, 1)
                return

            def sine_argument(step):
                a, n, t = hy["a"][0:NHID, 0:T], hy["n"][0:NHID, :], hy["b"][0:NHID, 0:T]
                full(dve, f"hf{step + 1}")
                V.tensor_scalar(a, bank(f"hf{step + 1}")[0:NHID, 0:T], pr(f"hb{step + 1}", NHID), pr(f"hf{step + 1}", NHID),
                                ALU.add, ALU.mult).then_inc(free_of(f"hf{step + 1}"), 1)
                freed(dve, f"hf{step + 1}")
                link(V.tensor_scalar(t, a, 1.0 / (2 * math.pi), MAGIC, ALU.mult, ALU.add))
                link(V.tensor_scalar(t, t, MAGIC, None, ALU.subtract))
                link(V.scalar_tensor_tensor(a, t, -TWO_PI_HI, a, ALU.mult, ALU.add))
                link(V.scalar_tensor_tensor(a, t, -TWO_PI_LO, a, ALU.mult, ALU.add))
                V.tensor_scalar(n, a, PI_BELOW, -PI_BELOW, ALU.min, ALU.max).then_inc(sin_arg, 1)

            def filters():
                for i in range(NT):
                    full(dve, "hf3", i, 0)
                    V.tensor_tensor(hy["a"], bank("hf3", i, 0)[:, :], window[:, i, :], ALU.mult).then_inc(free_of("hf3", i, 0), 1)
                    full(dve, "hf3", i, 1)
                    V.tensor_tensor(hy["b"], bank("hf3", i, 1)[:, :], window[:, i, :], ALU.mult).then_inc(free_of("hf3", i, 1), 1)
                    freed(dve, "hf3", i, 0)
                    freed(dve, "hf3", i, 1)
                    V.tensor_tensor(hy["hp"][:, i, :], hy["a"], hy["b"], ALU.add).then_inc(filter_ready, 1)
                    V.tensor_tensor(hy["hm"][:, i, :], hy["a"], hy["b"], ALU.subtract).then_inc(filter_ready, 1)
                    dve.wait_ge(filter_ready, 2 * i + 2)

            def short_conv(name, j):
                ch = 4 * int(name[2]) + j
                dve.wait_ge(conv_bias, ch + 1)
                ps, u = bank("even", name, j), hy["u"]
                for tap, shift in ((0, -1), (2, 1)):
                    for seg in SEGS:
                        a, b = seg.start, seg.stop
                        dst = slice(a + 1, b) if shift < 0 else slice(a, b - 1)
                        src = slice(a, b - 1) if shift < 0 else slice(a + 1, b)
                        ins = V.scalar_tensor_tensor(u[:, ch, dst], ps[:, src], conv_w[:, tap, ch : ch + 1], u[:, ch, dst],
                                                     ALU.mult, ALU.add)
                        if tap == 2 and seg is LAT:
                            ins.then_inc(free_of("even", name, j), 1)
                        elif tap == 0 and seg is LAT:
                            link(ins)

            def spectra():
                G = hy["G"]
                for s, (seq, m) in enumerate(SIGNAL_DFT):
                    re = FILTER_DFT.index((seq, "re", m))
                    im = FILTER_DFT.index((seq, "im", m))
                    re2 = FILTER_DFT.index((seq, "re2", m)) if m == 0 else re
                    full(dve, "Ur", s)
                    full(dve, "Ui", s)
                    Ur, Ui = bank("Ur", s)[:, :], bank("Ui", s)[:, :]
                    for g in (re, im, re2):
                        freed(dve, "G", g)
                    V.tensor_tensor(hz["t1"], Ur, G[:, re, :], ALU.mult)
                    link(V.tensor_tensor(hz["t2"], Ui, G[:, im, :], ALU.mult))
                    link(V.tensor_tensor(Z[:, 2 * s, :], hz["t1"], hz["t2"], ALU.subtract))
                    V.tensor_tensor(hz["t1"], Ur, G[:, im, :], ALU.mult).then_inc(free_of("Ur", s), 1)
                    V.tensor_tensor(hz["t2"], Ui, G[:, re2, :], ALU.mult).then_inc(free_of("Ui", s), 1)
                    freed(dve, "Ur", s)
                    freed(dve, "Ui", s)
                    V.tensor_tensor(Z[:, 2 * s + 1, :], hz["t1"], hz["t2"], ALU.add).then_inc(spec_ready, 1)
                    dve.wait_ge(spec_ready, s + 1)

            def forget(d):
                name = "fb" if d else "ff"
                for i in range(NT):
                    lf, kk = sc[f"lf{d}"][:, i, :], sc[f"k{d}"][:, i, :]
                    freed(dve, "even", name, i)
                    link(V.tensor_tensor(lf, kk, omlb, ALU.mult))
                    link(V.tensor_tensor(lf, lf, lb, ALU.add))
                    V.tensor_scalar(kk, lf, -1.0, 1.0, ALU.mult, ALU.add).then_inc(f_ready, 1)

            def scan_unit(u):
                d, i = UNITS[u]
                b, cols = u % 2, slice(P * i, P * i + P)
                ep, en, ei, el = (sc[n][:, b] for n in ("ep", "en", "ei", "el"))
                q = sc["q"][:, :, cols]
                dve.wait_ge(exps_ready, 4 * u + 4)
                freed(dve, "scan", u, "b01")
                freed(dve, "scan", u, "b23")
                if u >= 2:
                    full(dve, "scan", u - 2, "sc")
                ends = ei.rearrange("p h (j t) -> p h j t", t=BLK)[:, :, :, (0 if d else BLK - 1)]
                link(V.tensor_copy(sc["decay"][:, b], ends))
                V.tensor_tensor(ep, ep, q, ALU.mult).then_inc(qk_scaled, 1)
                full(dve, "scan", u, "kT")
                V.tensor_tensor(en, bank("scan", u, "kT")[:, :].rearrange("p (h n) -> p h n", h=H), en, ALU.mult).then_inc(free_of("scan", u, "kT"), 1)
                freed(dve, "scan", u, "rl")
                kk = sc[f"k{d}"][:, i, :].rearrange("p (h n) -> p h n", h=H)
                V.tensor_tensor(el, el, kk, ALU.mult).then_inc(qk_scaled, 1)
                V.tensor_tensor(ei, ei, q, ALU.mult).then_inc(qk_scaled, 1)
                full(dve, "scan", u, "sc")
                if u < 2:
                    dve.wait_ge(zeroed, 3)
                else:
                    full(dve, "scan", u - 2, "o")
                mask = c(f"inc{d}").bitcast(U32).unsqueeze(1).to_broadcast([P, H, P])
                V.copy_predicated(sc[f"P{d}"], mask, bank("scan", u, "sc")[:, :].rearrange("p (h n) -> p h n", h=H)).then_inc(free_of("scan", u, "sc"), 1)
                for h in range(H):
                    full(dve, "scan", u, f"U{h}")
                if u >= 2:
                    dve.wait_ge(s0_in, 16)
                order = list(range(NBLK - 1, -1, -1) if d else range(NBLK))
                steps = NBLK if u < 4 else NBLK - 1
                for n, j in enumerate(order[:steps]):
                    for h in range(H):
                        dst = sc["carry"][:, u, h, :] if n == NBLK - 1 else sc["S"][:, d, h, P * n : P * n + P]
                        U = bank("scan", u, f"U{h}")[:, P * j : P * j + P]
                        src = state_before(u, n, h)
                        if src is None:
                            ins = V.tensor_copy(dst, U)
                        else:
                            ins = V.scalar_tensor_tensor(dst, src, sc["decay"][:, b, h, j : j + 1], U, ALU.mult, ALU.add)
                        if n == steps - 1:
                            ins.then_inc(free_of("scan", u, f"U{h}"), 1)
                    if n == NBLK - 2 and u < 4:
                        ins.then_inc(states_ready, 1)
                        dve.wait_ge(states_ready, u + 1)
                    elif n < steps - 1:
                        link(ins)
                full(dve, "scan", u, "o")
                first = i not in [UNITS[w][1] for w in range(u)]
                ps = bank("scan", u, "o")[:, :].rearrange("p (h n) -> p h n", h=H)
                o = sc["o"][:, :, cols]
                if first:
                    V.tensor_copy(o, ps).then_inc(free_of("scan", u, "o"), 1)
                else:
                    w = [x for x in range(u) if UNITS[x][1] == i][0]
                    freed(dve, "scan", w, "o")
                    V.tensor_tensor(o, o, ps, ALU.add).then_inc(free_of("scan", u, "o"), 1)

            def project_out(layer):
                gate = mod[:, layer, 2 * KD : 3 * KD]
                for j in range(KD):
                    full(dve, "out", layer, j)
                    for s, seg in enumerate(SEGS):
                        ins = V.scalar_tensor_tensor(xT[:, j, seg], bank("out", layer, j)[:, seg], gate[:, j, s : s + 1], xT[:, j, seg],
                                                     ALU.mult, ALU.add)
                    ins.then_inc(free_of("out", layer, j), 1)

            def route(layer):
                b_rt = pr("b_rt").rearrange("p (l n) -> p l n", l=DEPTH)[:, layer]
                lg, l8, m8, i8, f8, oh, ml = (mo[n] for n in ("lg", "l8", "m8", "i8", "f8", "oh", "ml"))
                w, e4, m2, g1, gates = mo["w"], mo["e4"], mo["m2"], mo["g1"], mo["gates"]
                iota = c("iota16")
                for i in range(NT):
                    full(dve, "rt", layer, i)
                    V.tensor_tensor(lg[:, i, :], bank("rt", layer, i)[:, 0:20], b_rt, ALU.add).then_inc(free_of("rt", layer, i), 1)
                    freed(dve, "rt", layer, i)
                link(V.memset(l8, -3.0e38))
                link(V.tensor_copy(l8[:, :, 0:NG], lg[:, :, 0:NG]))
                for i in range(NT):
                    link(V.max(m8[:, i, :], l8[:, i, :]))
                    link(V.max_index(i8[:, i, :].bitcast(U32), m8[:, i, :], l8[:, i, :]))
                link(V.tensor_copy(f8, i8.bitcast(U32)))
                V.tensor_tensor(e4, lg[:, :, 0:NG], m8[:, :, 0:1].to_broadcast([P, NT, NG]), ALU.subtract).then_inc(route_max, 1)
                link(V.tensor_tensor(oh, iota[:, 0:NG].unsqueeze(1).to_broadcast([P, NT, NG]), f8[:, :, 0:1].to_broadcast([P, NT, NG]), ALU.is_equal))
                ml4 = ml.rearrange("p i (g e) -> p (i g) e", g=NG)
                g14 = g1.rearrange("p i (g e) -> p (i g) e", g=NG)
                oh4 = oh.rearrange("p i g -> p (i g)").unsqueeze(2).to_broadcast([P, NT * NG, EPG])
                link(V.tensor_scalar(g14, oh4, 1.0e30, 1.0e30, ALU.mult, ALU.subtract))
                link(V.tensor_tensor(ml, lg[:, :, NG:20], g1, ALU.add))
                link(V.tensor_copy(g14, oh4))
                for i in range(NT):
                    link(V.max(m8[:, i, :], ml[:, i, :]))
                    link(V.max_index(i8[:, i, :].bitcast(U32), m8[:, i, :], ml[:, i, :]))
                link(V.tensor_copy(f8, i8.bitcast(U32)))
                V.tensor_tensor(w[:, :, 0:1], m8[:, :, 1:2], m8[:, :, 0:1], ALU.subtract).then_inc(route_max, 1)
                dve.wait_ge(route_exp, 2 * layer + 1)
                link(V.tensor_reduce(w[:, :, 1:2], e4, AX_X, ALU.add))
                dve.wait_ge(route_exp, 2 * layer + 2)
                link(V.tensor_scalar(w[:, :, 2:3], w[:, :, 0:1], 1.0, None, ALU.add))
                link(V.tensor_tensor(w[:, :, 3:4], w[:, :, 1:2], w[:, :, 2:3], ALU.mult))
                link(V.reciprocal(w[:, :, 4:5], w[:, :, 3:4]))
                link(V.tensor_tensor(w[:, :, 5:6], w[:, :, 4:5], w[:, :, 0:1], ALU.mult))
                it = iota.unsqueeze(1).to_broadcast([P, NT, NE])
                link(V.tensor_tensor(gates, it, f8[:, :, 0:1].to_broadcast([P, NT, NE]), ALU.is_equal))
                link(V.tensor_tensor(gates, gates, w[:, :, 4:5].to_broadcast([P, NT, NE]), ALU.mult))
                link(V.tensor_tensor(g1, it, f8[:, :, 1:2].to_broadcast([P, NT, NE]), ALU.is_equal))
                link(V.tensor_tensor(g1, g1, w[:, :, 5:6].to_broadcast([P, NT, NE]), ALU.mult))
                link(V.tensor_tensor(gates, gates, g1, ALU.add))

            def experts(layer):
                y = cT[:, :, :].rearrange("p k t -> p (k t)").rearrange("p (i n) -> p i n", i=NT)
                if layer == 0:
                    dve.wait_ge(state_out, 32)
                else:
                    dve.wait_ge(cache_out, 64)
                full(dve, "out", layer, KD - 1)
                link(V.memset(y, 0.0))
                route(layer)
                hid, sg = mo["hid"], mo["sg"]
                with dve.Fori(0, NE // 2) as i:
                    for side in range(2):
                        e = i * 2 + side
                        down_last = 2 * NF + 2 * NT - 1
                        dve.wait_ge(bank_full[MOE_GROUPS[down_last]], moe_count(layer, down_last, e, 0))
                        for f in range(NF):
                            g, up = 2 * f, 2 * f + 1
                            dve.wait_ge(bank_full[MOE_GROUPS[up]], moe_count(layer, up, e))
                            dve.wait_ge(bank_free[MOE_GROUPS[g]], moe_count(layer, g, e))
                            V.tensor_tensor(hid[:, f, :], psum[MOE_GROUPS[up]][:, 0:T], sg[:, f % 2, :],
                                            ALU.mult).then_inc(bank_free[MOE_GROUPS[up]], 1)
                        for dd in range(2 * NT):
                            t, half = dd // 2, slice(HALF * (dd % 2), HALF * (dd % 2) + HALF)
                            g = 2 * NF + dd
                            bnk = MOE_GROUPS[g]
                            dve.wait_ge(bank_full[bnk], moe_count(layer, g, e))
                            dve.wait_ge(bank_free[bnk], moe_count(layer, g, e, MOE_GROUPS[: g + 1].count(bnk) - MOE_USES[bnk]))
                            V.scalar_tensor_tensor(y[:, t, half], psum[bnk][:, :], mo["gates"][:, t, bass.ds(e, 1)], y[:, t, half],
                                                   ALU.mult, ALU.add).then_inc(bank_free[bnk], 1)
                gate = mod[:, layer, 5 * KD : 6 * KD]
                for k in range(KD):
                    full(dve, "yt", layer, k)
                    for s, seg in enumerate(SEGS):
                        ins = V.scalar_tensor_tensor(xT[:, k, seg], bank("yt", layer, k)[:, seg], gate[:, k, s : s + 1], xT[:, k, seg],
                                                     ALU.mult, ALU.add)
                    ins.then_inc(free_of("yt", layer, k), 1)

            dve.wait_ge(params_in, 16)
            V.tensor_tensor(omlb, omlb, lb, ALU.subtract).then_inc(lb_diff, 1)
            dve.wait_ge(lb_exp, 1)
            link(V.tensor_scalar(omlb, omlb, 1.0, None, ALU.add))
            link(V.reciprocal(lb, omlb))
            link(V.tensor_scalar(omlb, lb, -1.0, 1.0, ALU.mult, ALU.add))
            modulation(0)
            norm(0, 0)
            dve.wait_ge(hyc_in, 32)
            sine_argument(0)
            dve.wait_ge(sin_done, 1)
            sine_argument(1)
            filters()
            for name in EVEN_ORDER:
                if name.startswith("hy"):
                    for j in range(4):
                        short_conv(name, j)
            for j in range(4):
                freed(dve, "even", "hy2", j)
                V.tensor_tensor(hy["u"][:, 4 + j, :], hy["u"][:, 4 + j, :], hy["u"][:, 8 + j, :], ALU.mult).then_inc(z_ready, 1)
            full(dve, "G", len(FILTER_DFT) - 1)
            spectra()
            dve.wait_ge(z_ready, 4)
            for j in range(4):
                full(dve, "inv", j)
                V.scalar_tensor_tensor(hy["u"][:, 8 + j, :], hy["u"][:, 4 + j, :], pr("hy_bias")[:, j : j + 1], bank("inv", j)[:, 0:T],
                                       ALU.mult, ALU.add).then_inc(free_of("inv", j), 1)
                freed(dve, "inv", j)
                V.tensor_tensor(cT[:, 4 + j, :], hy["u"][:, 8 + j, :], hy["u"][:, j, :], ALU.mult).then_inc(hyena_done, 1)
            dve.wait_ge(hyena_done, 4)
            forget(0)
            forget(1)

            for j in range(H):
                freed(dve, "even", "q", j)
            for u in range(len(UNITS)):
                scan_unit(u)
            for h in range(H):
                freed(dve, "even", "g", h)
                dve.wait_ge(head_rs, h + 1)
                link(V.scalar_tensor_tensor(sc["o"][:, h, :], sc["o"][:, h, :], pr("hgrn_g"), rs[:, :], ALU.mult, ALU.mult))
                V.tensor_tensor(cT[:, h, :], sc["o"][:, h, :], sc["g"][:, h, :], ALU.mult).then_inc(mixed, 1)
            project_out(0)
            norm(0, 1)
            experts(0)
            modulation(1)
            norm(1, 0)
            link(V.tensor_tensor_reduce(out=at["t"][:, 0, 0:64], in0=pr("lam")[:, 0:64], in1=pr("lam")[:, 64:128], scale=1.0, scalar=0.0,
                                        op0=ALU.mult, op1=ALU.add, accum_out=at["lam"][:, 0:1]))
            V.tensor_tensor_reduce(out=at["t"][:, 0, 0:64], in0=pr("lam")[:, 128:192], in1=pr("lam")[:, 192:256], scale=1.0, scalar=0.0,
                                   op0=ALU.mult, op1=ALU.add, accum_out=at["lam"][:, 1:2]).then_inc(lam_dots, 1)
            dve.wait_ge(lam_dots, 1)
            norms = (("qc", 4, P, "cq", "cosc", "sinc"), ("kv", 2, P, "ck", "cosc", "sinc"),
                     ("qd", 8, 64, "dq", "cosd", "sind"), ("kd", 8, 64, "dk", "cosd", "sind"))
            for b, (name, n, d, gain, cos, sin) in enumerate(norms):
                for i in range(NT):
                    freed(dve, "odd", name, i)
                x = at[f"raw{b}"][:, :, 0 : n * d]
                t = at["t"][:, 0:NT, 0 : n * d]
                link(V.tensor_tensor(t, x, x, ALU.mult))
                for i in range(NT):
                    ins = V.tensor_reduce(at["ss"][:, b, n * i : n * i + n], t[:, i, :].rearrange("p (h d) -> p h d", h=n), AX_X, ALU.add)
                ins.then_inc(ss_ready, 1)
                dve.wait_ge(ss_ready, b + 1)
            for b, (name, n, d, gain, cos, sin) in enumerate(norms):
                dve.wait_ge(qk_rs, b + 1)
                raw = at[f"raw{b}"]
                g = pr(gain).unsqueeze(1).to_broadcast([P, n, d])
                for i in range(NT):
                    x = raw[:, i, 0 : n * d].rearrange("p (h d) -> p h d", h=n)
                    link(V.tensor_tensor(x, x, at["ss"][:, b, n * i : n * i + n].unsqueeze(2).to_broadcast([P, n, d]), ALU.mult))
                    ins = V.tensor_tensor(x, x, g, ALU.mult)
                    if i == 0:
                        ins.then_inc(normed, 1)
                        dve.wait_ge(normed, b + 1)
                    else:
                        link(ins)
                for i in range(1, NT):
                    x = raw[:, i, 0 : n * d].rearrange("p (h r two) -> p h r two", h=n, two=2)
                    x1, x2 = x[:, :, :, 0], x[:, :, :, 1]
                    cs = c(cos).rearrange("p (i r) -> p i r", i=2)[:, i - 1].unsqueeze(1).to_broadcast([P, n, d // 2])
                    sn = c(sin).rearrange("p (i r) -> p i r", i=2)[:, i - 1].unsqueeze(1).to_broadcast([P, n, d // 2])
                    t = [at["t"][:, m, 0 : n * d // 2].rearrange("p (h r) -> p h r", h=n) for m in range(4)]
                    V.tensor_tensor(t[0], x1, cs, ALU.mult)
                    V.tensor_tensor(t[1], x2, sn, ALU.mult)
                    V.tensor_tensor(t[2], x1, sn, ALU.mult)
                    link(V.tensor_tensor(t[3], x2, cs, ALU.mult))
                    V.tensor_tensor(x1, t[0], t[1], ALU.subtract)
                    ins = V.tensor_tensor(x2, t[2], t[3], ALU.add)
                    if i == 1:
                        link(ins)
                    else:
                        ins.then_inc(roped, 1)
                        dve.wait_ge(roped, b + 1)
            dve.wait_ge(lam_exps, 1)
            lam = at["lam"][:, 4:5]
            link(V.tensor_tensor(lam, at["lam"][:, 2:3], at["lam"][:, 3:4], ALU.subtract))
            link(V.tensor_scalar(lam, lam, LAM_INIT, None, ALU.add))
            link(V.tensor_scalar(at["lam"][:, 5:6], pr("subln_g"), 1.0 - LAM_INIT, None, ALU.mult))

            def row_max(u):
                kind, h, i = ATTN[u]
                nk = P if i == 0 else 3 * P
                for m in range(2 if kind == "d" else 1):
                    full(dve, "S", u, m)
                    if u >= 2:
                        dve.wait_ge(probs_ready, u - 1)
                    mx = at["mx"][:, u % 2, 4 * m : 4 * m + 4]
                    link(V.tensor_reduce(mx[:, 0:1], bank("S", u, m)[:, 0:nk], AX_X, ALU.max))
                    V.tensor_scalar(mx[:, 1:2], mx[:, 0:1], -((P if kind == "c" else 64) ** -0.5), None, ALU.mult).then_inc(neg_max, 1)

            def normalise(u):
                kind, h, i = ATTN[u]
                nk = P if i == 0 else 3 * P
                mx, Pb = at["mx"][:, u % 2, :], at["Pb"]
                for m in range(2 if kind == "d" else 1):
                    freed(dve, "S", u, m)
                link(V.reciprocal(mx[:, 3:4], mx[:, 2:3]))
                p0 = Pb[:, 2 * (u % 2), 0:nk]
                if kind == "c":
                    V.tensor_scalar(p0, p0, mx[:, 3:4], None, ALU.mult).then_inc(probs_ready, 1)
                else:
                    p1 = Pb[:, 2 * (u % 2) + 1, 0:nk]
                    link(V.reciprocal(mx[:, 7:8], mx[:, 6:7]))
                    link(V.tensor_scalar(p1, p1, mx[:, 7:8], lam, ALU.mult, ALU.mult))
                    V.scalar_tensor_tensor(p0, p0, mx[:, 3:4], p1, ALU.mult, ALU.subtract).then_inc(probs_ready, 1)

            row_max(0)
            for u in range(len(ATTN)):
                if u + 1 < len(ATTN):
                    row_max(u + 1)
                normalise(u)
            for h in range(H):
                dve.wait_ge(head_rs, H + h + 1)
                V.scalar_tensor_tensor(cT[:, 4 + h, :], at["od"][:, h, :], at["lam"][:, 5:6], rs[:, :], ALU.mult, ALU.mult).then_inc(mixed, 1)
            project_out(1)
            norm(1, 1)
            experts(1)

        @block.tensor
        def _(pe):
            mm = nc.tensor.matmul

            def open_bank(*name):
                b, n = banks.at[name]
                if n > 1:
                    pe.wait_ge(bank_free[b], n - 1)
                return psum[b]

            def loaded(n):
                s, load = slot_of(n)
                pe.wait_ge(slot_loaded[s], 16 * load)
                return ring[:, s, :].rearrange("p (k n) -> p k n", k=KD)

            def modulation(layer):
                ps = open_bank("mod", layer)
                for blk in range(MOD_BLOCKS):
                    w = loaded(index[("mod", layer, blk)])
                    for m in range(4):
                        ch = 4 * blk + m
                        for k in range(KD):
                            ins = mm(ps[:, 2 * ch : 2 * ch + 2], w[:, k, P * m : P * m + P], condT[:, k, :], start=k == 0, stop=k == KD - 1)
                    if blk < MOD_BLOCKS - 1:
                        ins.then_inc(mod_blocks, 1)
                ins.then_inc(full_of("mod", layer), 1)

            def norm(layer, which):
                name = (f"norm{which + 1}", layer)
                ps = open_bank(*name)
                for k in range(KD):
                    pe.wait_ge(squares_ready, KD * (2 * layer + which) + k + 1)
                    ins = mm(ps[:, 0:T], ones, hT[:, k, :], start=k == 0, stop=k == KD - 1)
                ins.then_inc(full_of(*name), 1)

            def features_out(ps, w, m, src):
                for k in range(KD):
                    ins = mm(ps[:, 0:T], w[:, k, P * m : P * m + P], src[:, k, :], start=k == 0, stop=k == KD - 1)
                return ins

            def tokens_out(ps, w, i, src):
                for k in range(KD):
                    ins = mm(ps[:, :], src[:, k, P * i : P * i + P], w[:, k, :], start=k == 0, stop=k == KD - 1)
                return ins

            def experts(layer):
                pe.wait_ge(h_ready, 2 * KD * (2 * layer + 2))
                w_rt = pr("w_rt").rearrange("p (l k n) -> p l k n", l=DEPTH, k=KD)[:, layer]
                for i in range(NT):
                    ps = open_bank("rt", layer, i)
                    for k in range(KD):
                        ins = mm(ps[:, 0:20], hT[:, k, P * i : P * i + P], w_rt[:, k, :], start=k == 0, stop=k == KD - 1)
                    ins.then_inc(full_of("rt", layer, i), 1)
                for i in range(NT):
                    freed(pe, "rt", layer, i)
                with pe.Fori(0, NE // 2) as i:
                    for side in range(2):
                        e = i * 2 + side
                        w = [moe_block(side, kind) for kind in range(3)]
                        for f in range(NF):
                            for kind in range(2):
                                g = 2 * f + kind
                                bnk = MOE_GROUPS[g]
                                if f == 0:
                                    pe.wait_ge(moe_loaded(side, kind), i * 16 + 16 * (moe_loads(layer, side, kind) + 1))
                                pe.wait_ge(bank_free[bnk], moe_count(layer, g, e, MOE_GROUPS[:g].count(bnk)))
                                wk = w[kind].rearrange("p (k n) -> p k n", k=KD)
                                for k in range(KD):
                                    ins = mm(psum[bnk][:, 0:T], wk[:, k, P * f : P * f + P], hT[:, k, :], start=k == 0, stop=k == KD - 1)
                                ins.then_inc(bank_full[bnk], 1)
                        pe.wait_ge(moe_loaded(side, 2), i * 16 + 16 * (moe_loads(layer, side, 2) + 1))
                        wd = w[2].rearrange("p (f n) -> p f n", f=NF)
                        for f in (NF - 2, NF - 1):
                            pe.wait_ge(bank_free[MOE_GROUPS[2 * f + 1]], moe_count(layer, 2 * f + 1, e))
                        for dd in range(2 * NT):
                            g = 2 * NF + dd
                            bnk = MOE_GROUPS[g]
                            t, half = dd // 2, slice(HALF * (dd % 2), HALF * (dd % 2) + HALF)
                            pe.wait_ge(bank_free[bnk], moe_count(layer, g, e, MOE_GROUPS[:g].count(bnk)))
                            for f in range(NF):
                                ins = mm(psum[bnk][:, :], mo["hid"][:, f, P * t : P * t + P], wd[:, f, half], start=f == 0, stop=f == NF - 1)
                            ins.then_inc(bank_full[bnk], 1)
                y = cT[:, :, :].rearrange("p k t -> p (k t)").rearrange("p (i n) -> p i n", i=NT)
                for b in range(GATEUP_BANKS, BANKS):
                    pe.wait_ge(bank_free[b], moe_base[layer][b] + NE * MOE_USES[b])
                for k in range(KD):
                    ps = open_bank("yt", layer, k)
                    for i in range(NT):
                        ins = nc.tensor.transpose(ps[:, P * i : P * i + P], y[:, i, P * k : P * k + P], ident)
                    ins.then_inc(full_of("yt", layer, k), 1)

            def project_out(layer):
                pe.wait_ge(mixed, H * (layer + 1))
                if layer == 0:
                    pe.wait_ge(hyena_done, 4)
                else:
                    freed(pe, "O", len(ATTN) - 1)
                for j in range(KD):
                    w = loaded(index[("even_out" if layer == 0 else "odd_out", j // 4)])
                    ps = open_bank("out", layer, j)
                    features_out(ps, w, j % 4, cT).then_inc(full_of("out", layer, j), 1)

            pe.wait_ge(params_in, 16)
            pe.wait_ge(cond_ready, 1)
            pe.wait_ge(consts_in, 16)
            modulation(0)
            norm(0, 0)
            pe.wait_ge(hyc_in, 32)
            ps = open_bank("hf1")
            mm(ps[0:NHID, 0:T], hyp("w1", NFEAT), hyc("pos")[0:NFEAT], start=True, stop=True).then_inc(full_of("hf1"), 1)
            pe.wait_ge(sin_done, 1)
            ps = open_bank("hf2")
            mm(ps[0:NHID, 0:T], hyp("w2", NHID), hy["s"][0:NHID, :], start=True, stop=True).then_inc(full_of("hf2"), 1)
            pe.wait_ge(sin_done, 2)
            for i in range(NT):
                for half in range(2):
                    ps = open_bank("hf3", i, half)
                    mm(ps[:, :], hy["s"][0:NHID, P * i : P * i + P], hyp("w3", NHID)[:, HALF * half : HALF * half + HALF],
                       start=True, stop=True).then_inc(full_of("hf3", i, half), 1)
            pe.wait_ge(filter_ready, 2 * NT)
            for g, (seq, part, m) in enumerate(FILTER_DFT):
                ps = open_bank("G", g)
                tiles = seq_tiles[seq]
                src = hy["hm"] if part == "im" else hy["hp"]
                for n, i in enumerate(tiles):
                    ins = mm(ps[:, :], dft[seq][:, n, dft_columns(seq, part, m)], src[:, i, :], start=n == 0, stop=n == len(tiles) - 1)
                ins.then_inc(full_of("G", g), 1)
            pe.wait_ge(h_ready, 2 * KD)
            for name in EVEN_ORDER:
                w = loaded(index[("even", name)])
                for j in range(even_groups(name)):
                    ps = open_bank("even", name, j)
                    project = tokens_out if even_groups(name) == NT else features_out
                    project(ps, w, j, hT).then_inc(full_of("even", name, j), 1)
                if name == "hy2":
                    pe.wait_ge(z_ready, 4)
                    for i in range(NT):
                        ps = open_bank("zt", i)
                        for j in range(4):
                            ins = nc.tensor.transpose(ps[:, P * j : P * j + P], hy["u"][:, 4 + j, P * i : P * i + P], ident)
                        ins.then_inc(full_of("zt", i), 1)
                    for i in range(NT):
                        freed(pe, "zt", i)
                    for s, (seq, m) in enumerate(SIGNAL_DFT):
                        tiles = seq_tiles[seq]
                        for grp, part in (("Ur", "re"), ("Ui", "imp")):
                            ps = open_bank(grp, s)
                            for n, i in enumerate(tiles):
                                ins = mm(ps[:, :], dft[seq][:, n, dft_columns(seq, part, m)], z_tm[:, i, :], start=n == 0, stop=n == len(tiles) - 1)
                            ins.then_inc(full_of(grp, s), 1)
                    pe.wait_ge(spec_ready, 3)
                    for ch in range(4):
                        ps = open_bank("inv", ch)
                        cc = slice(P * ch, P * ch + P)
                        for n, (z, f) in enumerate(((0, 0), (2, 1), (1, 2), (3, 3))):
                            mm(ps[:, LAT], Z[:, z, cc], inv_lat[:, f, :], start=n == 0, stop=n == 3)
                        for f in range(2):
                            ins = mm(ps[:, CTX], Z[:, 4 + f, cc], inv_ctx[:, f, :], start=f == 0, stop=f == 1)
                        ins.then_inc(full_of("inv", ch), 1)
            for stage, u in SCAN_ORDER:
                d, i = UNITS[u]
                b, cols = u % 2, slice(P * i, P * i + P)
                hd = [slice(P * h, P * h + P) for h in range(H)]
                if stage == "decays":
                    pe.wait_ge(lf_ready, NT * d + i + 1)
                    lf, kk = sc[f"lf{d}"][:, i, :], sc[f"k{d}"][:, i, :]
                    tri = con[:, CONSTS.at[f"mid{d}"][0] : CONSTS.at[f"mid{d}"][0] + 2 * P]
                    for pair, g in enumerate(("b01", "b23")):
                        ps = open_bank("scan", u, g)
                        for x in range(2):
                            ins = mm(ps[:, 2 * P * x : 2 * P * x + 2 * P], lf[:, hd[2 * pair + x]], tri, start=True, stop=True)
                        ins.then_inc(full_of("scan", u, g), 1)
                    ps = open_bank("scan", u, "kT")
                    for h in range(H):
                        ins = nc.tensor.transpose(ps[:, hd[h]], kk[:, hd[h]], ident)
                    ins.then_inc(full_of("scan", u, "kT"), 1)
                    ps = open_bank("scan", u, "rl")
                    mm(ps[:, :], c(f"last{d}"), lf, start=True, stop=True).then_inc(full_of("scan", u, "rl"), 1)
                elif stage == "products":
                    pe.wait_ge(qk_scaled, 3 * u + 1)
                    freed(pe, "scan", u, "kT")
                    ps = open_bank("scan", u, "sc")
                    for h in range(H):
                        ins = mm(ps[:, hd[h]], sc["en"][:, b, h, :], sc["ep"][:, b, h, :], start=True, stop=True)
                    ins.then_inc(full_of("scan", u, "sc"), 1)
                    pe.wait_ge(qk_scaled, 3 * u + 2)
                    pe.wait_ge(vx_ready, NBLK * (u + 1))
                    for h in range(H):
                        ps = open_bank("scan", u, f"U{h}")
                        mm(ps[:, :], sc["el"][:, b, h, :], sc["vx"][:, h].rearrange("p j n -> p (j n)"),
                           start=True, stop=True).then_inc(full_of("scan", u, f"U{h}"), 1)
                else:
                    pe.wait_ge(qk_scaled, 3 * u + 3)
                    freed(pe, "scan", u, "sc")
                    if u < 4:
                        pe.wait_ge(states_ready, u + 1)
                    else:
                        freed(pe, "scan", u, "U3")
                        freed(pe, "scan", u - 2, "U3")
                    ps = open_bank("scan", u, "o")
                    order = list(range(NBLK - 1, -1, -1) if d else range(NBLK))
                    for h in range(H):
                        ins = mm(ps[:, hd[h]], sc["v"][:, i, hd[h]], sc[f"P{d}"][:, h, :], start=True, stop=False)
                        for n, j in enumerate(order):
                            S = state_before(u, n, h)
                            if S is not None:
                                t = slice(BLK * j, BLK * j + BLK)
                                ins = mm(ps[:, P * h + BLK * j : P * h + BLK * j + BLK], S, sc["ei"][:, b, h, t], start=False, stop=n == NBLK - 1)
                    ins.then_inc(full_of("scan", u, "o"), 1)
            pe.wait_ge(head_squares, 1)
            sq = sc["vx"].rearrange("p h j n -> p (h j n)")[:, 0 : H * T].rearrange("p (h n) -> p h n", h=H)
            for h in range(H):
                ps = open_bank("on", h)
                mm(ps[:, 0:T], ones, sq[:, h, :], start=True, stop=True).then_inc(full_of("on", h), 1)
            project_out(0)
            norm(0, 1)
            experts(0)
            modulation(1)
            norm(1, 0)
            pe.wait_ge(h_ready, 3 * 2 * KD)
            for name in ODD_ORDER:
                w = loaded(index[("odd", name)])
                for i in range(NT):
                    ps = open_bank("odd", name, i)
                    tokens_out(ps, w, i, hT).then_inc(full_of("odd", name, i), 1)
            for b, (name, n) in enumerate((("qc", 4), ("kv", 2), ("qd", 4), ("kd", 4))):
                pe.wait_ge(roped, b + 1)
                for i in range(NT):
                    ps = open_bank("tr", name, i)
                    for h in range(n):
                        ins = nc.tensor.transpose(ps[:, P * h : P * h + P], at[f"raw{b}"][:, i, P * h : P * h + P], ident)
                    ins.then_inc(full_of("tr", name, i), 1)
            pe.wait_ge(caches_in, 64)
            for name in ("qc", "kv", "qd", "kd"):
                for i in range(NT):
                    freed(pe, "tr", name, i)
            for i in range(NT):
                freed(pe, "odd", "vd", i)
            for u in range(len(ATTN) + 2):
                if u < len(ATTN):
                    kind, h, i = ATTN[u]
                    cols, keys = slice(P * i, P * i + P), slice(0, P) if i == 0 else slice(P, 4 * P)
                    nk = keys.stop - keys.start
                    for m in range(2 if kind == "d" else 1):
                        q = at["qcT"] if kind == "c" else at[f"qd{m}"]
                        k_all = at["kcT"][:, h // 2, keys] if kind == "c" else at["kdT"][:, h, keys]
                        ps = open_bank("S", u, m)
                        mm(ps[:, 0:nk], q[:, h, cols], k_all, start=True, stop=True).then_inc(full_of("S", u, m), 1)
                if 0 < u <= len(ATTN):
                    nt = 1 if ATTN[u - 1][2] == 0 else 3
                    pe.wait_ge(probs_ready, u)
                    ps = open_bank("PT", u - 1)
                    for n in range(nt):
                        ins = nc.tensor.transpose(ps[:, P * n : P * n + P], at["Pb"][:, 2 * ((u - 1) % 2), P * n : P * n + P], ident)
                    ins.then_inc(full_of("PT", u - 1), 1)
                if u > 1:
                    kind, h, i = ATTN[u - 2]
                    slots = (0,) if i == 0 else (1, 2, 3)
                    freed(pe, "PT", u - 2)
                    ps = open_bank("O", u - 2)
                    for n, s in enumerate(slots):
                        v = at["vc"][:, s, P * (h // 2) : P * (h // 2) + P] if kind == "c" else at["vd"][:, s, P * h : P * h + P]
                        ins = mm(ps[:, 0:P], v, at["PT"][:, (u - 2) % 2, P * n : P * n + P], start=n == 0, stop=n == len(slots) - 1)
                    ins.then_inc(full_of("O", u - 2), 1)
            pe.wait_ge(head_squares, 2)
            sq = at["raw0"].rearrange("p i n -> p (i n)").rearrange("p (h n) -> p h n", h=H)
            for h in range(H):
                ps = open_bank("sn", h)
                mm(ps[:, 0:T], ones, sq[:, h, :], start=True, stop=True).then_inc(full_of("sn", h), 1)
            project_out(1)
            norm(1, 1)
            experts(1)


def _constants():
    con = np.zeros((P, CONSTS.total), np.float32)

    def put(name, a):
        start, width = CONSTS.at[name]
        con[: a.shape[0], start : start + width] = a.reshape(a.shape[0], width)

    put("ident", np.eye(P))
    put("ones", np.ones((P, P)))
    put("eps", np.full((P, 1), EPS))
    put("iota16", np.broadcast_to(np.arange(NE), (P, NE)))
    s, t = np.arange(P)[:, None], np.arange(P)[None, :]
    same = s // BLK == t // BLK
    middle = t // BLK * BLK + BLK // 2
    put("inc0", same & (s <= t))
    put("mid0", (same & (s <= t)) * 1.0 - (same & (s <= middle - 1)) * 1.0)
    put("last0", same & (s > t))
    put("inc1", same & (s >= t))
    put("mid1", (same & (s >= t)) * 1.0 - (same & (s >= middle)) * 1.0)
    put("last1", same & (s < t))
    row, col = np.arange(DEC) // 64, np.arange(DEC) % 64
    for name, dim in (("c", P), ("d", 64)):
        half = dim // 2
        inv = np.float32(10000.0) ** (-np.arange(0, half, 2, dtype=np.float32) / np.float32(half))
        ang = np.concatenate([row[:, None].astype(np.float32) * inv, col[:, None].astype(np.float32) * inv], -1)
        for fn, f in (("cos", np.cos), ("sin", np.sin)):
            put(fn + name, f(ang).reshape(2, P, half).transpose(1, 0, 2))
    hyc = np.zeros((P, HYCONST.total), np.float32)

    def puth(name, a):
        start, width = HYCONST.at[name]
        hyc[: a.shape[0], start : start + width] = a.reshape(a.shape[0], width)

    pos, win = [], []
    deltas = np.abs(np.linspace(math.log(1e-2) / 1.5, math.log(1e-2) / 0.3, HALF, dtype=np.float32))
    for n in (SEQ, DEC):
        tt = np.linspace(0.0, 1.0, n, dtype=np.float32)[:, None]
        w = (np.float32(2.0 * math.pi) * np.arange(n, dtype=np.float32) / np.float32(n)).astype(np.float32)
        f = np.linspace(1e-4, 15, 16, dtype=np.float32)
        ang = (w[:, None] * f[None, :]).astype(np.float32)
        pos.append(np.concatenate([tt, np.cos(ang), -np.sin(ang)], -1).T)
        win.append(np.exp(-tt * deltas[None, :]))
    puth("pos", np.concatenate(pos, 1))
    puth("window", np.concatenate(win, 0).reshape(NT, P, HALF).transpose(1, 0, 2))
    for name, n in (("lat", DEC), ("ctx", SEQ)):
        t, f = np.arange(n)[:, None], np.arange(n)[None, :]
        re, im = np.cos(np.pi * t * f / n), -np.sin(np.pi * t * f / n)
        nyquist = (-1.0) ** np.arange(n)
        imp, re2 = im[:, :P].copy(), re[:, :P].copy()
        imp[:, 0], re2[:, 0] = nyquist, nyquist
        m = np.concatenate([re, im, imp, re2], 1)
        puth("dft_" + name, m.reshape(n // P, P, -1).transpose(1, 0, 2))
        f, t = np.arange(n)[:, None], np.arange(n)[None, :]
        ire, iim = np.cos(np.pi * t * f / n) / n, -np.sin(np.pi * t * f / n) / n
        ire[0] = 0.5 / n
        iim[0] = 0.5 * (-1.0) ** np.arange(n) / n
        puth("inv_" + name, np.concatenate([ire, iim], 0).reshape(2 * n // P, P, n).transpose(1, 0, 2))
    return con, hyc


def _blocks(w):
    n = w.shape[1] // HALF
    return w.reshape(KD, P, n, HALF).transpose(2, 1, 0, 3).reshape(n, P, KD * HALF)


def _columns(v):
    return np.ascontiguousarray(v.reshape(-1, P).T)


def kernel(**a):
    import concourse.bacc as bacc
    from concourse.bass_utils import run_bass_kernel_spmd

    a = {k: np.asarray(v) for k, v in a.items()}
    par = np.zeros((P, PARAMS.total), np.float32)

    def put(name, v):
        start, width = PARAMS.at[name]
        par[: v.shape[0], start : start + width] = v.reshape(v.shape[0], width)

    rows = lambda v: np.broadcast_to(v.reshape(1, -1), (P, v.size))
    put("cond", np.stack([_columns(a["c_ctx"]), _columns(a["c"][0])], -1))
    put("b_mod", _columns(a["b_mod"]))
    put("n1", _columns(a["norm1_g"]))
    put("n2", _columns(a["norm2_g"]))
    put("conv_w", _columns(a["hy_conv_w"][0]))
    put("conv_b", _columns(a["hy_conv_b"][0]))
    put("hgrn_g", _columns(a["hgrn_norm_g"][0]))
    put("subln_g", _columns(a["d_subln_g"][0]))
    for to, of in (("hb1", "hy_b1"), ("hf1", "hy_freq1"), ("hb2", "hy_b2"), ("hf2", "hy_freq2")):
        put(to, a[of][0].reshape(-1, 1))
    put("hy_bias", _columns(a["hy_bias"][0]))
    put("lower", rows(a["hgrn_lower"]))
    for to, of in (("cq", "c_qnorm_g"), ("ck", "c_knorm_g"), ("dq", "d_qnorm_g"), ("dk", "d_knorm_g")):
        put(to, rows(a[of][0]))
    put("lam", rows(np.concatenate([a["d_lambda_q1"][0], a["d_lambda_k1"][0], a["d_lambda_q2"][0], a["d_lambda_k2"][0]])))
    put("b_rt", rows(np.concatenate([a["moe_b_grp"], a["moe_b_rt"]], -1)))
    w_rt = np.concatenate([a["moe_w_grp"], a["moe_w_rt"]], -1)
    put("w_rt", w_rt.reshape(DEPTH, KD, P, 20).transpose(2, 0, 1, 3).reshape(P, -1))
    hypar = np.zeros((P, HYPAR.total), np.float32)
    for name, v in (("w1", a["hy_w1"][0]), ("w2", a["hy_w2"][0]), ("w3", a["hy_w3"][0])):
        start, width = HYPAR.at[name]
        hypar[: v.shape[0], start : start + width] = v
    con, hyc = _constants()
    x = np.concatenate([a["x_prompt"][0], a["x_sample"][0]], 0)
    mods = [_blocks(w) for w in a["w_mod"]]
    even, odd = _blocks(a["even_w_in"][0]), _blocks(a["odd_w_in"][0])
    proj = np.concatenate([mods[0], even[[EVEN_COLUMN[n] for n in EVEN_ORDER]], _blocks(a["even_w_out"][0]),
                           mods[1], odd, _blocks(a["odd_w_out"][0])], 0)
    moe = np.empty((DEPTH, NE, 3, P, KD * HALF), np.float32)
    for kind, name in enumerate(("moe_w_gate", "moe_w_up")):
        moe[:, :, kind] = a[name].reshape(DEPTH, NE, KD, P, FE).transpose(0, 1, 3, 2, 4).reshape(DEPTH, NE, P, -1)
    moe[:, :, 2] = a["moe_w_down"].reshape(DEPTH, NE, NF, P, D).transpose(0, 1, 3, 2, 4).reshape(DEPTH, NE, P, -1)
    arrays = {
        "params": par, "hypar": hypar, "consts": con, "hyconst": hyc,
        "x": np.ascontiguousarray(x.T.reshape(KD, P, T).transpose(1, 0, 2)),
        "s0": np.ascontiguousarray(a["state_hgrn"][0, 0].transpose(2, 0, 1, 3)),
        "ck": np.ascontiguousarray(a["cache_c_k"][0, 0].transpose(2, 0, 1)),
        "cv": np.ascontiguousarray(a["cache_c_v"][0, 0].transpose(1, 0, 2)).reshape(P, -1),
        "dk": np.ascontiguousarray(a["cache_d_k"][0, 0].transpose(2, 0, 1)),
        "dv": np.ascontiguousarray(a["cache_d_v"][0, 0].transpose(1, 0, 2)).reshape(P, -1),
        "proj": proj, "moe": moe.reshape(DEPTH * NE * 3, P, KD * HALF),
    }
    outs = {"y": (P, KD, T), "state": (2, P, H, P), "ock": (P, 2 * P), "ocv": (P, 2 * P), "odk": (P, HALF), "odv": (P, HALF)}
    nc = bacc.Bacc("TRN2", target_bir_lowering=False, num_devices=1)
    args = [nc.dram_tensor("in_" + n, v.shape, F32, kind="ExternalInput").ap() for n, v in arrays.items()]
    args += [nc.dram_tensor("out_" + n, s, F32, kind="ExternalOutput").ap() for n, s in outs.items()]
    trunk_kernel(nc, *args)
    r = run_bass_kernel_spmd(nc, [{"in_" + n: v for n, v in arrays.items()}], core_ids=[0]).results[0]
    y = np.asarray(r["out_y"]).transpose(2, 1, 0).reshape(T, D)
    heads = lambda n, k: np.asarray(r["out_" + n]).reshape(SEQ, k, P).transpose(1, 0, 2)[None, None]
    return (y[None, :SEQ], y[None, SEQ:], np.asarray(r["out_state"]).transpose(0, 2, 1, 3)[None, None],
            heads("ock", 2), heads("ocv", 2), heads("odk", H), heads("odv", H))
```

```python
import math
from contextlib import ExitStack

import concourse.bass as bass
import numpy as np
from concourse import mybir
from concourse.alu_op_type import AluOpType as ALU

ACT = mybir.ActivationFunctionType
F32 = mybir.dt.float32
U32 = mybir.dt.uint32
AX_X = mybir.AxisListType.X

P = 128
D = 1024
KD = D // P
SEQ, DEC = 128, 256
T = SEQ + DEC
NT = T // P
CTX, LAT = slice(0, SEQ), slice(SEQ, T)
SEGS = (CTX, LAT)
DEPTH = 2
EPS = 1e-6
H = 4
BLK = 32
NBLK = P // BLK
HALF = 512
NHID = 64
NFEAT = 33
NE = 16
NG = 4
EPG = 4
FE = 512
NF = FE // P
NPAIR = NE // 2
CAP = P // 2
OVER = (T - 1) // CAP
FOLD = 96
LAM_INIT = 0.8 - 0.6 * math.exp(-0.3)
MAGIC = 1.5 * 2.0**23
TWO_PI_HI = 6.28125
TWO_PI_LO = 2 * math.pi - 6.28125
PI_BELOW = 3.1415925
BANKS = 8
PROJ_SLOTS = 3

MOD_BLOCKS = 6 * D // HALF
MOD_FIRST = 2 * D // HALF
MODS = [("mod", layer, b) for layer in range(DEPTH) for b in range(MOD_BLOCKS)]
EVEN_COLUMN = {"q": 0, "ff": 1, "fb": 2, "v": 3, "g": 4, "hy0": 5, "hy1": 6, "hy2": 7}
ODD_ORDER = ["qc", "kv", "qd", "kd", "vd"]
UNITS = [(0, 0), (0, 1), (0, 2), (1, 0), (1, 2), (1, 1)]


def even_groups(name):
    return NT if name in ("v", "ff", "fb") else 4


def project(name):
    return [("even", name, j) for j in range(even_groups(name))]


def out_half(layer, half):
    return [("out", layer, half, j) for j in range(KD)]


def scans_with(fillers):
    stages = [("decays", 0)]
    for u in range(len(UNITS)):
        stages += ([("decays", u + 1)] if u + 1 < len(UNITS) else []) + [("products", u), ("outputs", u)]
    share = {"decays": 1, "products": 2, "outputs": 1}
    length = {"even": 4, "out": 2, "mod": 2}
    left = sum(length[f[0]] for f in fillers)
    gaps = sum(share[stage[0]] for stage in stages)
    steps, fillers, owed = [], list(fillers), 0.0
    per_gap = left / gaps
    for stage in stages:
        steps.append(stage)
        owed += per_gap * share[stage[0]]
        while fillers and owed >= length[fillers[0][0]] / 2:
            owed -= length[fillers[0][0]]
            steps.append(fillers.pop(0))
    return steps + fillers


STEPS0 = [
    ("hf1",), ("sum1",), MODS[0], ("hf2",), *MODS[1:MOD_FIRST], ("apply1",),
    *project("hy0"), ("hf3",), *MODS[4:6], ("G",),
    *project("hy1"), *MODS[6:8],
    *project("hy2"), *MODS[8:10],
    *project("q"), ("zt",), ("even", "v", 0), ("dft",), ("even", "v", 1), ("even", "v", 2), *MODS[10:11], ("inv",),
    *project("ff"), *MODS[11:13],
    *scans_with(project("fb") + MODS[13:15] + project("g") + MODS[15:18] + out_half(0, 1) + MODS[18:21]),
    MODS[21], ("head",), *MODS[22:24], *out_half(0, 0),
]


def block_of(step):
    return step if step[0] == "mod" else step[:3] if step[0] == "out" else step[:2]


LAYER0 = list(dict.fromkeys(block_of(step) for step in STEPS0 if step[0] in ("mod", "even", "out")))
LAYER1 = [("odd", n) for n in ODD_ORDER] + [("out", 1, half) for half in range(2)]
STREAM = LAYER0 + LAYER1
LAYER_BLOCKS = [len(LAYER0), len(LAYER1)]


class Columns:

    def __init__(self, widths):
        self.at, self.total = {}, 0
        for name, width in widths:
            self.at[name] = (self.total, width)
            self.total += width

    def of(self, tensor, name, parts=P):
        start, width = self.at[name]
        return tensor[0:parts, start : start + width]


PARAMS = Columns([
    ("cond", KD * 2), ("b_mod", DEPTH * 48), ("n1", DEPTH * KD), ("n2", DEPTH * KD),
    ("conv_w", 3 * 12), ("conv_b", 12), ("hgrn_g", 1), ("subln_g", 1),
    ("hb1", 1), ("hf1", 1), ("hb2", 1), ("hf2", 1), ("hy_bias", 4),
    ("lower", 2 * HALF), ("cq", P), ("ck", P), ("dq", 64), ("dk", 64),
    ("lam", 4 * 64), ("b_rt", DEPTH * 20), ("w_rt", DEPTH * KD * BLK),
])
HYPAR = Columns([("w1", NHID), ("w2", NHID), ("w3", 2 * HALF)])
CONSTS = Columns([
    ("ident", P), ("ones", P), ("eps", 1), ("iota16", NE),
    ("mid0", P), ("inc0", P), ("mid1", P), ("inc1", P), ("last0", P), ("last1", P),
    ("fold", FOLD), ("upto", P), ("iota128", P), ("slot_id", 1), ("before", NPAIR * (NPAIR + 1)),
    ("cosc", 2 * 64), ("sinc", 2 * 64), ("cosd", 2 * 32), ("sind", 2 * 32),
])
HYCONST = Columns([
    ("pos", T), ("window", NT * HALF), ("dft_lat", 2 * 768), ("dft_ctx", 512),
    ("inv_lat", 4 * DEC), ("inv_ctx", 2 * SEQ),
])


class Banks:

    def __init__(self):
        self.at, self.used, self.next = {}, [0] * BANKS, 0

    def take(self, *name):
        bank = self.next
        self.next = (bank + 1) % BANKS
        self.used[bank] += 1
        self.at[name] = (bank, self.used[bank])


GATE_BANK, UP_BANK, GATHER_BANK, SCATTER_BANK, HIDT_BANK = 0, 1, 2, 4, 7
ATTN = [("c", h, i) for h in range(H) for i in range(NT)] + [("d", h, i) for h in range(H) for i in range(NT)]
SCAN_GROUPS = {"decays": ("b01", "b23", "kT", "rl"), "products": ("sc", "U0", "U1", "U2", "U3"), "outputs": ("o",)}
FILTER_DFT = [("lat", "re", 0), ("lat", "re", 1), ("lat", "im", 0), ("lat", "im", 1), ("lat", "re2", 0),
              ("ctx", "re", 0), ("ctx", "im", 0), ("ctx", "re2", 0)]
SIGNAL_DFT = [("lat", 0), ("lat", 1), ("ctx", 0)]


def groups_of(step):
    kind, u = step[0], step[-1]
    if kind == "mod":
        return [("ada", *step[1:]), ("adt", *step[1:])]
    if kind in ("decays", "products", "outputs"):
        return [("scan", u, g) for g in SCAN_GROUPS[kind]]
    return {
        "sum1": [("norm1", 0)], "hf3": [("hf3", i, half) for i in range(NT) for half in range(2)], "apply1": [],
        "G": [("G", g) for g in range(len(FILTER_DFT))], "zt": [("zt", i) for i in range(NT)],
        "dft": [(g, s) for s in range(len(SIGNAL_DFT)) for g in ("Ur", "Ui")], "inv": [("inv", ch) for ch in range(4)],
        "head": [("on", h) for h in range(H)],
    }.get(kind, [step])


def plan_banks():
    banks = Banks()
    for layer in range(DEPTH):
        if layer == 0:
            for step in STEPS0:
                for group in groups_of(step):
                    banks.take(*group)
        else:
            banks.take("norm1", layer)
            for name in ODD_ORDER:
                for i in range(NT):
                    banks.take("odd", name, i)
            for name in ("qc", "kv", "qd", "kd"):
                for i in range(NT):
                    banks.take("tr", name, i)
            order = []
            for u in range(len(ATTN) + 2):
                if u < len(ATTN):
                    order += [("S", u, m) for m in range(2 if ATTN[u][0] == "d" else 1)]
                if 0 < u <= len(ATTN):
                    order.append(("PT", u - 1))
                if u > 1:
                    order.append(("O", u - 2))
            for name in order:
                banks.take(*name)
            for h in range(H):
                banks.take("sn", h)
            for half in range(2):
                for j in range(KD):
                    banks.take("out", 1, half, j)
        banks.take("norm2", layer)
        banks.take("rk", layer)
        banks.take("rt", layer)
        for i in range(NT):
            for half in range(2):
                banks.take("ht", layer, i, half)
        banks.take("cum", layer)
        for n in range(4):
            banks.take("pb", layer, n)
        for k in range(KD):
            banks.take("yt", layer, k)
    return banks


def trunk_kernel(nc, params_d, hypar_d, consts_d, hyconst_d, x_d, s0_d, ck_d, cv_d, dk_d, dv_d,
                 proj_d, moe_d, y_d, state_d, ock_d, ocv_d, odk_d, odv_d):
    banks = plan_banks()
    with ExitStack() as ctx:
        def sb(name, shape, dt=F32):
            return ctx.enter_context(nc.sbuf_tensor(name, shape, dt))

        def sem(name):
            return ctx.enter_context(nc.semaphore(name))

        xT = sb("xT", [P, KD, T])
        hT = sb("hT", [P, KD, T])
        cT = sb("cT", [P, KD, T])
        par = sb("par", [P, PARAMS.total])
        con = sb("con", [P, CONSTS.total])
        ring = sb("ring", [P, PROJ_SLOTS, KD * HALF])
        mod = sb("mod", [P, DEPTH, 48, 2])
        gs = sb("gs", [P, DEPTH, 2, KD, 2])
        condT = sb("condT", [P, KD, BLK])
        ada = sb("ada", [P, 2, HALF])
        rs = sb("rs", [P, T])
        lnt = sb("lnt", [P, T])
        stats = sb("stats", [P, 64])
        arena_cols = 25048
        arena = sb("arena", [P, arena_cols])
        psum = [ctx.enter_context(nc.psum_tensor(f"bank{b}", [P, HALF], F32)) for b in range(BANKS)]

        def carve(shapes):
            out, at = {}, 0
            for name, shape in shapes:
                n = int(np.prod(shape))
                view = arena[:, at : at + n]
                if len(shape) == 2:
                    view = view.rearrange("p (a b) -> p a b", a=shape[0])
                elif len(shape) == 3:
                    view = view.rearrange("p (a b c) -> p a b c", a=shape[0], b=shape[1])
                out[name] = view
                at += n
            assert at <= arena_cols, at
            return out

        hy = carve([("hyc", (HYCONST.total,)), ("hyp", (HYPAR.total,)), ("G", (8, HALF)),
                    ("u", (12, T)), ("hp", (NT, HALF)), ("hm", (NT, HALF)),
                    ("a", (HALF,)), ("b", (HALF,)), ("n", (T,)), ("s", (T,))])
        hz = carve([("hyc", (HYCONST.total,)), ("hyp", (HYPAR.total,)), ("G", (8, HALF)),
                    ("u", (12, T)), ("z_tm", (NT, HALF)), ("Z", (6, HALF)),
                    ("t1", (HALF,)), ("t2", (HALF,))])
        z_tm, Z = hz["z_tm"], hz["Z"]
        sc = carve([("lf0", (NT, HALF)), ("lf1", (NT, HALF)), ("k0", (NT, HALF)), ("k1", (NT, HALF)), ("g", (H, T)),
                    ("vx", (H, NBLK, P)), ("S", (H, (NBLK - 1) * P)), ("s0", (2, H, P)), ("carry", (4, H, P)),
                    ("ep", (2, H, P)), ("en", (2, H, P)), ("ei", (2, H, P)), ("el", (2, H, P)),
                    ("P0", (H, P)), ("P1", (H, P)), ("decay", (2, H, NBLK)), ("spare", (arena_cols - 22560,)),
                    ("q", (H, T)), ("v", (NT, HALF))])
        at = carve([("vc", (4, 2 * P)), ("vd", (4, HALF)), ("qcT", (H, T)), ("kcT", (2, 4 * P)),
                    ("qd0", (H, T)), ("qd1", (H, T)), ("kdT", (H, 4 * P)), ("raw0", (NT, HALF)),
                    ("raw1", (NT, HALF)), ("raw2", (NT, HALF)), ("raw3", (NT, HALF)),
                    ("t", (4, HALF)), ("t2", (4, HALF)), ("ss", (4, 24)), ("lt", (4, 24)), ("lam", (8,)),
                    ("od", (H, T)), ("Pb", (4, T)), ("PT", (2, T)), ("mx", (2, 8))])
        mo = carve([("ring", (3, KD * HALF)), ("h", (NT, D)), ("hS", (KD, P)), ("sg", (FE,)), ("hid", (FE,)),
                    ("hidT", (NF, P)), ("yS", (2, HALF)), ("sel", (NT, P)), ("sel1", (NT, P)), ("GT", (T,)), ("GT1", (T,)),
                    ("bc", (4, T)), ("diag", (4, T)), ("rk", (T,)), ("iota", (P,)), ("slot", (1,)), ("prime", (16,)),
                    ("lg", (NT, 20)), ("l8", (NT, 8)), ("m8", (NT, 8)), ("i8", (NT, 8)), ("f8", (NT, 8)),
                    ("oh", (NT, NG)), ("ml", (NT, NE)), ("w", (NT, 8)), ("e4", (NT, NG)),
                    ("g1", (NT, NE)), ("eq0", (NT, NE)), ("eq1", (NT, NE)), ("A", (NT, NE)), ("B", (NT + 1, NE)),
                    ("rank", (NT, NE)), ("floor", (NT, NE)), ("tiles", (NE,)), ("pairs", (NPAIR,)),
                    ("pp", (NPAIR + 1, NPAIR)), ("first", (NPAIR + 1,)), ("firsti", (NPAIR + 1,)), ("base", (NE,)), ("pos", (4, NT))])

        params_in, consts_in, x_in = sem("params_in"), sem("consts_in"), sem("x_in")
        filter_in, hyconst_in = sem("filter_in"), sem("hyconst_in")
        s0_in, caches_in = sem("s0_in"), sem("caches_in")
        slot_loaded = [sem(f"slot_loaded{s}") for s in range(2 * PROJ_SLOTS)]
        bank_full = [sem(f"bank_full{b}") for b in range(BANKS)]
        bank_free = [sem(f"bank_free{b}") for b in range(BANKS)]
        dve_link, act_link, pool_link = sem("dve_link"), sem("act_link"), sem("pool_link")
        cond_ready, mod_ready, lb_diff, lb_exp = sem("cond_ready"), sem("mod_ready"), sem("lb_diff"), sem("lb_exp")
        squares_ready, rs_ready, scaled, h_ready = sem("squares_ready"), sem("rs_ready"), sem("scaled"), sem("h_ready")
        sin_arg, sin_done, filter_ready = sem("sin_arg"), sem("sin_done"), sem("filter_ready")
        conv_bias, z_ready, spec_ready, hyena_done = sem("conv_bias"), sem("z_ready"), sem("spec_ready"), sem("hyena_done")
        f_ready, lf_ready, zeroed, vx_ready = sem("f_ready"), sem("lf_ready"), sem("zeroed"), sem("vx_ready")
        exps_ready, qk_scaled, probs_masked, states_ready = sem("exps_ready"), sem("qk_scaled"), sem("probs_masked"), sem("states_ready")
        head_squares, head_rs, mixed = sem("head_squares"), sem("head_rs"), sem("mixed")
        ss_ready, qk_rs, normed, roped = sem("ss_ready"), sem("qk_rs"), sem("normed"), sem("roped")
        lam_dots, lam_exps, pads_zero = sem("lam_dots"), sem("lam_exps"), sem("pads_zero")
        neg_max, probs_ready = sem("neg_max"), sem("probs_ready")
        route_max, route_exp, assigned, diag_ready, table_ready = (
            sem("route_max"), sem("route_exp"), sem("assigned"), sem("diag_ready"), sem("table_ready"))
        loop_names = ("selected", "gathered", "hS_ready", "gate_full", "up_full", "sg_ready", "hid_ready", "hidT_full",
                      "hidT_ready", "down_full", "yS_ready", "GT_ready", "scattered", "summed", "primed")
        loops = [{n: sem(f"{n}{layer}") for n in loop_names} for layer in range(DEPTH)]
        state_out, cache_out, y_out = sem("state_out"), sem("cache_out"), sem("y_out")

        def full(eng, *name):
            b, n = banks.at[name]
            eng.wait_ge(bank_full[b], n)

        def bank(*name):
            return psum[banks.at[name][0]]

        def freed(eng, *name):
            b, n = banks.at[name]
            eng.wait_ge(bank_free[b], n)

        def free_of(*name):
            return bank_free[banks.at[name][0]]

        def full_of(*name):
            return bank_full[banks.at[name][0]]

        def residual(eng, adds, k=KD - 1):
            layer = (adds - 1) // 2
            if adds % 2:
                freed(eng, "out", layer, 0 if layer == 0 else 1, k)
            else:
                freed(eng, "yt", layer, k)

        MOD_ALL = [entry[1:] for entry in MODS]

        def mods_needed(layer, which):
            return MOD_ALL.index((layer, MOD_FIRST - 1 if which == 0 else 5 * D // HALF - 1)) + 1

        def keeps(u):
            return UNITS[u] not in ((0, 2), (1, 1))

        def carry_of(u):
            return sum(keeps(w) for w in range(u))

        def state_before(u, n, h):
            d, i = UNITS[u]
            if n:
                return sc["S"][:, h, P * (n - 1) : P * n]
            return None if i == 0 else sc["s0"][:, d, h, :] if keeps(u) else sc["carry"][:, carry_of(u - 1), h, :]

        c = lambda name: CONSTS.of(con, name)
        pr = lambda name, parts=P: PARAMS.of(par, name, parts)
        ident, ones, eps = c("ident"), c("ones"), c("eps")
        n1 = pr("n1").rearrange("p (l k) -> p l k", l=DEPTH)
        n2 = pr("n2").rearrange("p (l k) -> p l k", l=DEPTH)
        hyc = lambda name: HYCONST.of(hy["hyc"], name)
        hyp = lambda name, parts: HYPAR.of(hy["hyp"], name, parts)
        dft = {"lat": hyc("dft_lat").rearrange("p (k n) -> p k n", k=2),
               "ctx": hyc("dft_ctx").rearrange("p (k n) -> p k n", k=1)}
        seq_tiles = {"ctx": [0], "lat": [1, 2]}
        n_freq = {"ctx": 1, "lat": 2}
        inv_lat = hyc("inv_lat").rearrange("p (f t) -> p f t", f=4)
        inv_ctx = hyc("inv_ctx").rearrange("p (f t) -> p f t", f=2)
        window = hyc("window").rearrange("p (i n) -> p i n", i=NT)
        conv_w = pr("conv_w").rearrange("p (t c) -> p t c", t=3)
        lower = pr("lower").rearrange("p (r n) -> p r n", r=2)
        lb, omlb = lower[:, 0, :], lower[:, 1, :]

        def dft_columns(seq, part, m):
            n = n_freq[seq] * P
            start = {"re": m * P, "im": n + m * P, "imp": 2 * n if m == 0 else n + m * P, "re2": 2 * n + P}[part]
            return slice(start, start + P)

        def slot_of(n):
            layer = 0 if n < LAYER_BLOCKS[0] else 1
            first = 0 if layer == 0 else LAYER_BLOCKS[0]
            s = (n - first) % PROJ_SLOTS
            earlier = sum(1 for m in range(first) if m % PROJ_SLOTS == s) + (NE // 2 if layer else 0)
            return s, earlier + (n - first) // PROJ_SLOTS + 1

        index = {name: n for n, name in enumerate(STREAM)}

        def last_group(name):
            if name[0] == "mod":
                return ("ada", name[1], name[2])
            if name[0] == "even":
                return ("even", name[1], even_groups(name[1]) - 1)
            if name[0] == "odd":
                return ("odd", name[1], NT - 1)
            return (*name, KD - 1)

        def moe_block(side, kind):
            return (mo["ring"] if side else ring)[:, kind, :]

        def moe_loaded(side, kind):
            return slot_loaded[PROJ_SLOTS * side + kind]

        def moe_loads(layer, side, kind):
            if side:
                return layer * NE // 2
            return sum(slot_of(n)[0] == kind for n in range(sum(LAYER_BLOCKS[: layer + 1]))) + layer * NE // 2

        def first_tile(eng, pair):
            return eng.value_load(mo["firsti"][0:1, bass.ds(pair, 1)].bitcast(mybir.dt.int32), min_val=0, max_val=NPAIR * (OVER + 1))

        block = ctx.enter_context(nc.Block())

        @block.sync
        def _(sp):
            sp.dma_start(par[:, :], params_d).then_inc(params_in, 16)
            sp.dma_start(con[:, :], consts_d).then_inc(consts_in, 16)
            sp.dma_start(hy["hyc"][:, 0:T], hyconst_d[:, 0:T]).then_inc(filter_in, 16)
            sp.dma_start(hy["hyp"], hypar_d).then_inc(filter_in, 16)
            sp.dma_start(xT[:, :, :], x_d).then_inc(x_in, 16)

            def load_blocks(first, count, wait_slot=None):
                for n in range(first, first + count):
                    s, _ = slot_of(n)
                    if n == first + s and wait_slot:
                        wait_slot(s)
                    before = n - PROJ_SLOTS
                    if before >= first:
                        full(sp, *last_group(STREAM[before]))
                    sp.dma_start(ring[:, s, :], proj_d[n]).then_inc(slot_loaded[s], 16)
                    if n == MOD_FIRST:
                        sp.dma_start(hy["hyc"][:, T:], hyconst_d[:, T:]).then_inc(hyconst_in, 16)

            def load_experts(layer):
                end = sum(LAYER_BLOCKS[: layer + 1])
                for n in range(end - PROJ_SLOTS, end):
                    full(sp, *last_group(STREAM[n]))

                def load(pair, kind, side):
                    at_block = pair * 6 + (layer * NE * 3 + 3 * side + kind)
                    sp.dma_start(moe_block(side, kind),
                                 moe_d[bass.ds(at_block, 1)].rearrange("o p n -> p (o n)")).then_inc(moe_loaded(side, kind), 16)

                for kind in range(3):
                    load(0, kind, 0)
                sp.wait_ge(mixed, H * (layer + 1))
                if layer == 0:
                    sp.wait_ge(state_out, 32)
                else:
                    sp.wait_ge(cache_out, 64)
                for kind in range(3):
                    load(0, kind, 1)
                sems = loops[layer]
                sp.wait_ge(table_ready, layer + 1)
                with sp.Fori(1, NPAIR) as i:
                    first = first_tile(sp, i) + 1
                    for kind in range(3):
                        if kind == 0:
                            sp.wait_ge(sems["gate_full"], first - 1)
                        elif kind == 1:
                            sp.wait_ge(sems["up_full"], first - 1)
                        else:
                            sp.wait_ge(sems["down_full"], first * 2 - 1)
                        for side in range(2):
                            load(i, kind, side)
                return first_tile(sp, NPAIR) + 1

            load_blocks(0, LAYER_BLOCKS[0])
            end = load_experts(0)

            def experts_done(kind):
                if kind == 2:
                    sp.wait_ge(loops[0]["down_full"], end * 2 - 1)
                else:
                    sp.wait_ge(loops[0][("gate_full", "up_full")[kind]], end - 1)

            load_blocks(LAYER_BLOCKS[0], LAYER_BLOCKS[1], experts_done)
            load_experts(1)
            for k in range(KD):
                freed(sp, "yt", 1, k)
                sp.dma_start(y_d[:, k, :], xT[:, k, :]).then_inc(y_out, 16)
            sp.wait_ge(y_out, 16 * KD)

        @block.gpsimd
        def _(pool):
            nc.gpsimd.memset(condT[:, :, :], 0.0).then_inc(zeroed, 1)
            pool.wait_ge(hyena_done, 4)
            nc.gpsimd.memset(sc["vx"], 0.0).then_inc(zeroed, 1)
            nc.gpsimd.memset(sc["P0"], 0.0).then_inc(zeroed, 1)
            nc.gpsimd.memset(sc["P1"], 0.0).then_inc(zeroed, 1)
            pool.dma_start(sc["s0"], s0_d).then_inc(s0_in, 16)
            pool.wait_ge(zeroed, 4)
            for u, (d, i) in enumerate(UNITS):
                freed(pool, "even", "v", i)
                if u:
                    full(pool, "scan", u - 1, f"U{H - 1}")
                for j in range(NBLK):
                    rows = slice(BLK * j, BLK * j + BLK)
                    nc.gpsimd.tensor_copy(
                        sc["vx"][rows, :, j, :], sc["v"][rows, i, :].rearrange("p (h n) -> p h n", h=H)
                    ).then_inc(vx_ready, 1)
                if u and UNITS[u - 1][1] == 0:
                    for h in range(H):
                        freed(pool, "scan", u - 1, f"U{h}")
                    pool.dma_start(state_d[UNITS[u - 1][0]], sc["carry"][:, carry_of(u - 1)]).then_inc(state_out, 16)
            pool.wait_ge(state_out, 32)
            freed(pool, "yt", 0, KD - 1)
            nc.gpsimd.memset(at["qd0"][64:P], 0.0).then_inc(pads_zero, 1)
            nc.gpsimd.memset(at["qd1"][0:64], 0.0).then_inc(pads_zero, 1)
            for dst, src in ((at["kcT"][:, :, P : 2 * P], ck_d), (at["kdT"][:, :, P : 2 * P], dk_d),
                             (at["vc"][:, 1, :], cv_d), (at["vd"][:, 1, :], dv_d)):
                pool.dma_start(dst, src).then_inc(caches_in, 16)
            pool.wait_ge(normed, 2)
            pool.dma_start(ock_d, at["raw1"][:, 0, 0 : 2 * P]).then_inc(cache_out, 16)
            freed(pool, "odd", "kv", 0)
            pool.dma_start(ocv_d, at["vc"][:, 0, :]).then_inc(cache_out, 16)
            pool.wait_ge(normed, 4)
            pool.dma_start(odk_d, at["raw3"][:, 0, :]).then_inc(cache_out, 16)
            freed(pool, "odd", "vd", 0)
            pool.dma_start(odv_d, at["vd"][:, 0, :]).then_inc(cache_out, 16)
            pool.wait_ge(cache_out, 64)

        @block.scalar
        def _(act):
            links = [0]

            def link(ins):
                links[0] += 1
                ins.then_inc(act_link, 1)
                act.wait_ge(act_link, links[0])

            def norm_sums(layer, which):
                count = 2 * layer + which
                for k in range(KD):
                    if count:
                        residual(act, count, k)
                    nc.scalar.activation(hT[:, k, :], xT[:, k, :], ACT.Square).then_inc(squares_ready, 1)
                name = (f"norm{which + 1}", layer)
                full(act, *name)
                nc.scalar.activation(lnt[:, :], bank(*name)[:, 0:T], ACT.Ln, bias=eps, scale=1.0 / D).then_inc(free_of(*name), 1)
                freed(act, *name)
                nc.scalar.activation(rs[:, :], lnt[:, :], ACT.Exp, scale=-0.5).then_inc(rs_ready, 1)

            def norm_shift(layer, which):
                count = 2 * layer + which
                act.wait_ge(mod_ready, mods_needed(layer, which))
                for k in range(KD):
                    for s, seg in enumerate(SEGS):
                        act.wait_ge(scaled, count * 2 * KD + 2 * k + s + 1)
                        nc.scalar.activation(hT[:, k, seg], hT[:, k, seg], ACT.Identity,
                                             bias=mod[:, layer, 24 * which + k, s : s + 1]).then_inc(h_ready, 1)

            def norm(layer, which):
                norm_sums(layer, which)
                norm_shift(layer, which)

            def head_norm(count, groups, src, sq):
                nc.scalar.activation(sq, src, ACT.Square).then_inc(head_squares, 1)
                for h in range(H):
                    full(act, groups, h)
                    if h:
                        act.wait_ge(head_rs, H * count + h)
                    nc.scalar.activation(lnt[:, :], bank(groups, h)[:, 0:T], ACT.Ln, bias=eps, scale=1.0 / P).then_inc(free_of(groups, h), 1)
                    freed(act, groups, h)
                    if h:
                        act.wait_ge(mixed, H * count + h)
                    nc.scalar.activation(rs[:, :], lnt[:, :], ACT.Exp, scale=-0.5).then_inc(head_rs, 1)

            mods_done = [0]

            def modulation(layer, b):
                if mods_done[0] >= 2:
                    full(act, "adt", *MOD_ALL[mods_done[0] - 2])
                full(act, "ada", layer, b)
                nc.scalar.activation(ada[:, mods_done[0] % 2, :], bank("ada", layer, b)[:, :], ACT.Copy).then_inc(free_of("ada", layer, b), 1)
                mods_done[0] += 1

            def experts(layer):
                sems = loops[layer]
                full(act, "rk", layer)
                nc.scalar.activation(mo["rk"], bank("rk", layer)[:, 0:T], ACT.Copy).then_inc(free_of("rk", layer), 1)
                act.wait_ge(*((state_out, 32) if layer == 0 else (cache_out, 64)))
                for i in range(NT):
                    for half in range(2):
                        full(act, "ht", layer, i, half)
                        nc.scalar.activation(mo["h"][:, i, HALF * half : HALF * half + HALF], bank("ht", layer, i, half)[:, :],
                                             ACT.Copy).then_inc(free_of("ht", layer, i, half), 1)
                act.wait_ge(route_max, 2 * layer + 1)
                nc.scalar.activation(mo["e4"], mo["e4"], ACT.Exp).then_inc(route_exp, 1)
                act.wait_ge(route_max, 2 * layer + 2)
                nc.scalar.activation(mo["w"][:, :, 0:1], mo["w"][:, :, 0:1], ACT.Exp).then_inc(route_exp, 1)
                for n in range(4):
                    full(act, "pb", layer, n)
                    nc.scalar.activation(mo["bc"][:, n, :], bank("pb", layer, n)[:, 0:T], ACT.Copy).then_inc(free_of("pb", layer, n), 1)
                act.wait_ge(table_ready, layer + 1)
                act.wait_ge(sems["primed"], 1)

                def gathered(half, tile):
                    act.wait_ge(sems["gathered"], tile * 2 + (half - 1))
                    nc.scalar.activation(mo["hS"][:, 4 * half : 4 * half + 4, :],
                                         psum[GATHER_BANK + half][:, :].rearrange("p (k n) -> p k n", k=4),
                                         ACT.Copy).then_inc(sems["hS_ready"], 1)

                for half in range(2):
                    gathered(half, 1)
                with act.Fori(0, NPAIR) as i:
                    with act.Fori(first_tile(act, i), first_tile(act, i + 1)) as tile:
                        g = tile + 1
                        act.wait_ge(sems["hid_ready"], g)
                        act.wait_ge(sems["gate_full"], g)
                        nc.scalar.activation(mo["sg"], psum[GATE_BANK][:, :], ACT.Silu).then_inc(sems["sg_ready"], 1)
                        act.wait_ge(sems["down_full"], g * 2 - 1)
                        act.wait_ge(sems["hidT_full"], g + 1)
                        nc.scalar.activation(mo["hidT"], psum[HIDT_BANK][:, :].rearrange("p (f n) -> p f n", f=NF),
                                             ACT.Copy).then_inc(sems["hidT_ready"], 1)
                        act.wait_ge(sems["scattered"], g * 6)
                        for half in range(2):
                            act.wait_ge(sems["down_full"], g * 2 + half)
                            nc.scalar.activation(mo["yS"][:, half, :], psum[half][:, :], ACT.Copy).then_inc(sems["yS_ready"], 1)
                        act.wait_ge(sems["up_full"], g)
                        for half in range(2):
                            gathered(half, g + 1)

            def projected(name, j):
                full(act, "even", name, j)
                ps = bank("even", name, j)
                if name.startswith("hy"):
                    ch = 4 * int(name[2]) + j
                    nc.scalar.activation(hy["u"][:, ch, :], ps[:, 0:T], ACT.Identity, bias=pr("conv_b")[:, ch : ch + 1],
                                         scale=conv_w[:, 1, ch : ch + 1]).then_inc(conv_bias, 1)
                elif name == "q" or name == "g":
                    nc.scalar.activation(sc[name][:, j, :], ps[:, 0:T], ACT.Silu).then_inc(free_of("even", name, j), 1)
                elif name == "v":
                    nc.scalar.activation(sc["v"][:, j, :], ps[:, :], ACT.Copy).then_inc(free_of("even", name, j), 1)
                else:
                    act.wait_ge(hyena_done, 4)
                    d = 0 if name == "ff" else 1
                    nc.scalar.activation(sc[f"k{d}"][:, j, :], ps[:, :], ACT.Sigmoid).then_inc(free_of("even", name, j), 1)
                    if j == NT - 1:
                        for i in range(NT):
                            act.wait_ge(f_ready, NT * d + i + 1)
                            lf = sc[f"lf{d}"][:, i, :]
                            nc.scalar.activation(lf, lf, ACT.Ln).then_inc(lf_ready, 1)

            act.wait_ge(params_in, 16)
            act.wait_ge(zeroed, 1)
            nc.scalar.activation(condT[:, :, 0:2], pr("cond").rearrange("p (k s) -> p k s", s=2), ACT.Silu).then_inc(cond_ready, 1)
            act.wait_ge(lb_diff, 1)
            nc.scalar.activation(omlb, omlb, ACT.Exp).then_inc(lb_exp, 1)
            act.wait_ge(x_in, 16)
            act.wait_ge(consts_in, 16)
            for step in STEPS0:
                kind, u = step[0], step[-1]
                if kind in ("hf1", "hf2"):
                    act.wait_ge(sin_arg, int(kind[2]))
                    nc.scalar.activation(hy["s"][0:NHID, :], hy["n"][0:NHID, :], ACT.Sin).then_inc(sin_done, 1)
                elif kind == "sum1":
                    norm_sums(0, 0)
                elif kind == "apply1":
                    norm_shift(0, 0)
                elif kind == "mod":
                    modulation(*step[1:])
                elif kind == "G":
                    for g in range(len(FILTER_DFT)):
                        full(act, "G", g)
                        nc.scalar.activation(hy["G"][:, g, :], bank("G", g)[:, :], ACT.Copy).then_inc(free_of("G", g), 1)
                elif kind == "even":
                    projected(*step[1:])
                elif kind == "zt":
                    for i in range(NT):
                        full(act, "zt", i)
                        if i == 0:
                            full(act, "G", len(FILTER_DFT) - 1)
                        nc.scalar.activation(z_tm[:, i, :], bank("zt", i)[:, :], ACT.Copy).then_inc(free_of("zt", i), 1)
                elif kind == "decays":
                    if u >= 2:
                        full(act, "scan", u - 2, "o")
                    b = u % 2
                    for pair, g in enumerate(("b01", "b23")):
                        full(act, "scan", u, g)
                        ps = bank("scan", u, g)[:, :].rearrange("p (h c n) -> p h c n", h=2, c=2)
                        hs = slice(2 * pair, 2 * pair + 2)
                        nc.scalar.activation(sc["ep"][:, b, hs, :], ps[:, :, 0, :], ACT.Exp).then_inc(exps_ready, 1)
                        nc.scalar.activation(sc["en"][:, b, hs, :], ps[:, :, 0, :], ACT.Exp, scale=-1.0).then_inc(exps_ready, 1)
                        nc.scalar.activation(sc["ei"][:, b, hs, :], ps[:, :, 1, :], ACT.Exp).then_inc(free_of("scan", u, g), 1)
                    full(act, "scan", u, "rl")
                    nc.scalar.activation(sc["el"][:, b], bank("scan", u, "rl")[:, :].rearrange("p (h n) -> p h n", h=H),
                                         ACT.Exp).then_inc(free_of("scan", u, "rl"), 1)
                elif kind == "head":
                    for w in range(len(UNITS)):
                        freed(act, "scan", w, "o")
                    head_norm(0, "on", cT[:, 0:H, :], sc["vx"].rearrange("p h j n -> p (h j n)")[:, 0 : H * T].rearrange("p (h n) -> p h n", h=H))
            norm(0, 1)
            experts(0)
            norm(1, 0)
            for b, name in enumerate(ODD_ORDER):
                for i in range(NT):
                    full(act, "odd", name, i)
                    ps = bank("odd", name, i)
                    done = free_of("odd", name, i)
                    slot = (0, 2, 3)[i]
                    if name == "vd":
                        nc.scalar.activation(at["vd"][:, slot, :], ps[:, :], ACT.Copy).then_inc(done, 1)
                    elif name == "kv":
                        nc.scalar.activation(at["raw1"][:, i, 0 : 2 * P], ps[:, 0 : 2 * P], ACT.Copy)
                        nc.scalar.activation(at["vc"][:, slot, :], ps[:, 2 * P :], ACT.Copy).then_inc(done, 1)
                    else:
                        nc.scalar.activation(at[f"raw{b}"][:, i, :], ps[:, :], ACT.Copy).then_inc(done, 1)
                    if name == "vd" and i == 0:
                        act.wait_ge(lam_dots, 1)
                        nc.scalar.activation(at["lam"][:, 2:4], at["lam"][:, 0:2], ACT.Exp).then_inc(lam_exps, 1)
            for b, n in enumerate((4, 2, 8, 8)):
                act.wait_ge(ss_ready, b + 1)
                link(nc.scalar.activation(at["lt"][:, b, 0 : NT * n], at["ss"][:, b, 0 : NT * n], ACT.Ln, bias=eps,
                                          scale=1.0 / (P if b < 2 else 64)))
                nc.scalar.activation(at["ss"][:, b, 0 : NT * n], at["lt"][:, b, 0 : NT * n], ACT.Exp, scale=-0.5).then_inc(qk_rs, 1)
            act.wait_ge(pads_zero, 2)
            for b, name in enumerate(("qc", "kv", "qd", "kd")):
                for i in range(NT):
                    full(act, "tr", name, i)
                    ps = bank("tr", name, i)[:, :].rearrange("p (h n) -> p h n", h=H)
                    done = free_of("tr", name, i)
                    cols, slot = slice(P * i, P * i + P), (0, 2, 3)[i]
                    keys = slice(P * slot, P * slot + P)
                    if name == "qc":
                        nc.scalar.activation(at["qcT"][:, :, cols], ps, ACT.Copy).then_inc(done, 1)
                    elif name == "kv":
                        nc.scalar.activation(at["kcT"][:, :, keys], ps[:, 0:2, :], ACT.Copy).then_inc(done, 1)
                    elif name == "qd":
                        nc.scalar.activation(at["qd0"][0:64, :, cols], ps[0:64], ACT.Copy)
                        nc.scalar.activation(at["qd1"][64:P, :, cols], ps[64:P], ACT.Copy).then_inc(done, 1)
                    else:
                        nc.scalar.activation(at["kdT"][:, :, keys], ps, ACT.Copy).then_inc(done, 1)
            maps_done = 0
            for u in range(len(ATTN) + 2):
                if u < len(ATTN):
                    kind, h, i = ATTN[u]
                    nk = P if i == 0 else 3 * P
                    for m in range(2 if kind == "d" else 1):
                        maps_done += 1
                        act.wait_ge(neg_max, maps_done)
                        if u >= 2:
                            full(act, "PT", u - 2)
                        col = 4 * m
                        nc.scalar.activation(at["Pb"][:, 2 * (u % 2) + m, 0:nk], bank("S", u, m)[:, 0:nk], ACT.Exp,
                                             bias=at["mx"][:, u % 2, col + 1 : col + 2],
                                             scale=(P if kind == "c" else 64) ** -0.5,
                                             accum_out=at["mx"][:, u % 2, col + 2 : col + 3]).then_inc(free_of("S", u, m), 1)
                if 0 < u <= len(ATTN):
                    i = ATTN[u - 1][2]
                    nk = P if i == 0 else 3 * P
                    full(act, "PT", u - 1)
                    if u >= 3:
                        full(act, "O", u - 3)
                    nc.scalar.activation(at["PT"][:, (u - 1) % 2, 0:nk], bank("PT", u - 1)[:, 0:nk], ACT.Copy).then_inc(free_of("PT", u - 1), 1)
                if u > 1:
                    kind, h, i = ATTN[u - 2]
                    cols = slice(P * i, P * i + P)
                    full(act, "O", u - 2)
                    dst = cT[:, h, cols] if kind == "c" else at["od"][:, h, cols]
                    nc.scalar.activation(dst, bank("O", u - 2)[:, 0:P], ACT.Copy).then_inc(free_of("O", u - 2), 1)
            freed(act, "O", len(ATTN) - 1)
            head_norm(1, "sn", at["od"], at["raw0"].rearrange("p i n -> p (i n)").rearrange("p (h n) -> p h n", h=H))
            norm(1, 1)
            experts(1)

        @block.vector
        def _(dve):
            links = [0]

            def link(ins):
                links[0] += 1
                ins.then_inc(dve_link, 1)
                dve.wait_ge(dve_link, links[0])

            V = nc.vector

            def modulation(layer, b):
                full(dve, "adt", layer, b)
                b_mod = pr("b_mod").rearrange("p (l n) -> p l n", l=DEPTH)[:, layer, 4 * b : 4 * b + 4]
                V.tensor_tensor(mod[:, layer, 4 * b : 4 * b + 4, :],
                                bank("adt", layer, b)[:, 0 : 4 * FOLD].rearrange("p (n s) -> p n s", n=4)[:, :, 0:2],
                                b_mod.unsqueeze(2).to_broadcast([P, 4, 2]), ALU.add).then_inc(free_of("adt", layer, b), 1)
                freed(dve, "adt", layer, b)
                which, chunk = b // 6, 4 * b - 24 * (b // 6)
                if KD <= chunk < 2 * KD:
                    k = slice(chunk - KD, chunk - KD + 4)
                    gain = (n1, n2)[which][:, layer, k].unsqueeze(2).to_broadcast([P, 4, 2])
                    V.scalar_tensor_tensor(gs[:, layer, which, k, :], mod[:, layer, 4 * b : 4 * b + 4, :], 1.0, gain,
                                           ALU.add, ALU.mult).then_inc(mod_ready, 1)
                else:
                    V.memset(stats[:, 0:1], 0.0).then_inc(mod_ready, 1)
                dve.wait_ge(mod_ready, MOD_ALL.index((layer, b)) + 1)

            def norm(layer, which):
                count = 2 * layer + which
                dve.wait_ge(rs_ready, count + 1)
                if count == 0:
                    dve.wait_ge(x_in, 16)
                else:
                    residual(dve, count)
                for k in range(KD):
                    for s, seg in enumerate(SEGS):
                        ins = V.scalar_tensor_tensor(hT[:, k, seg], xT[:, k, seg], gs[:, layer, which, k, s : s + 1],
                                                     rs[:, seg], ALU.mult, ALU.mult)
                        ins.then_inc(scaled, 1)

            def sine_argument(name):
                if name == "hf1":
                    dve.wait_ge(filter_in, 32)
                else:
                    dve.wait_ge(sin_done, 1)
                a, n, t = hy["a"][0:NHID, 0:T], hy["n"][0:NHID, :], hy["b"][0:NHID, 0:T]
                full(dve, name)
                V.tensor_scalar(a, bank(name)[0:NHID, 0:T], pr("hb" + name[2], NHID), pr(name, NHID),
                                ALU.add, ALU.mult).then_inc(free_of(name), 1)
                freed(dve, name)
                link(V.tensor_scalar(t, a, 1.0 / (2 * math.pi), MAGIC, ALU.mult, ALU.add))
                link(V.tensor_scalar(t, t, MAGIC, None, ALU.subtract))
                link(V.scalar_tensor_tensor(a, t, -TWO_PI_HI, a, ALU.mult, ALU.add))
                link(V.scalar_tensor_tensor(a, t, -TWO_PI_LO, a, ALU.mult, ALU.add))
                V.tensor_scalar(n, a, PI_BELOW, -PI_BELOW, ALU.min, ALU.max).then_inc(sin_arg, 1)

            def filters():
                for i in range(NT):
                    full(dve, "hf3", i, 0)
                    V.tensor_tensor(hy["a"], bank("hf3", i, 0)[:, :], window[:, i, :], ALU.mult).then_inc(free_of("hf3", i, 0), 1)
                    full(dve, "hf3", i, 1)
                    V.tensor_tensor(hy["b"], bank("hf3", i, 1)[:, :], window[:, i, :], ALU.mult).then_inc(free_of("hf3", i, 1), 1)
                    freed(dve, "hf3", i, 0)
                    freed(dve, "hf3", i, 1)
                    V.tensor_tensor(hy["hp"][:, i, :], hy["a"], hy["b"], ALU.add).then_inc(filter_ready, 1)
                    V.tensor_tensor(hy["hm"][:, i, :], hy["a"], hy["b"], ALU.subtract).then_inc(filter_ready, 1)
                    dve.wait_ge(filter_ready, 2 * i + 2)

            def short_conv(name, j):
                ch = 4 * int(name[2]) + j
                dve.wait_ge(conv_bias, ch + 1)
                ps, u = bank("even", name, j), hy["u"]
                for tap, shift in ((0, -1), (2, 1)):
                    for seg in SEGS:
                        a, b = seg.start, seg.stop
                        dst = slice(a + 1, b) if shift < 0 else slice(a, b - 1)
                        src = slice(a, b - 1) if shift < 0 else slice(a + 1, b)
                        ins = V.scalar_tensor_tensor(u[:, ch, dst], ps[:, src], conv_w[:, tap, ch : ch + 1], u[:, ch, dst],
                                                     ALU.mult, ALU.add)
                        if tap == 2 and seg is LAT:
                            ins.then_inc(free_of("even", name, j), 1)
                        elif tap == 0 and seg is LAT:
                            link(ins)

            def spectra():
                G = hy["G"]
                for s, (seq, m) in enumerate(SIGNAL_DFT):
                    re = FILTER_DFT.index((seq, "re", m))
                    im = FILTER_DFT.index((seq, "im", m))
                    re2 = FILTER_DFT.index((seq, "re2", m)) if m == 0 else re
                    full(dve, "Ur", s)
                    full(dve, "Ui", s)
                    Ur, Ui = bank("Ur", s)[:, :], bank("Ui", s)[:, :]
                    for g in (re, im, re2):
                        freed(dve, "G", g)
                    V.tensor_tensor(hz["t1"], Ur, G[:, re, :], ALU.mult)
                    link(V.tensor_tensor(hz["t2"], Ui, G[:, im, :], ALU.mult))
                    link(V.tensor_tensor(Z[:, 2 * s, :], hz["t1"], hz["t2"], ALU.subtract))
                    V.tensor_tensor(hz["t1"], Ur, G[:, im, :], ALU.mult).then_inc(free_of("Ur", s), 1)
                    V.tensor_tensor(hz["t2"], Ui, G[:, re2, :], ALU.mult).then_inc(free_of("Ui", s), 1)
                    freed(dve, "Ur", s)
                    freed(dve, "Ui", s)
                    V.tensor_tensor(Z[:, 2 * s + 1, :], hz["t1"], hz["t2"], ALU.add).then_inc(spec_ready, 1)
                    dve.wait_ge(spec_ready, s + 1)

            def forget(d, i):
                lf, kk = sc[f"lf{d}"][:, i, :], sc[f"k{d}"][:, i, :]
                freed(dve, "even", "fb" if d else "ff", i)
                link(V.tensor_tensor(lf, kk, omlb, ALU.mult))
                link(V.tensor_tensor(lf, lf, lb, ALU.add))
                V.tensor_scalar(kk, lf, -1.0, 1.0, ALU.mult, ALU.add).then_inc(f_ready, 1)

            def scan_scale(u):
                d, i = UNITS[u]
                b, cols = u % 2, slice(P * i, P * i + P)
                ep, en, ei, el = (sc[n][:, b] for n in ("ep", "en", "ei", "el"))
                q = sc["q"][:, :, cols]
                dve.wait_ge(exps_ready, 4 * u + 4)
                freed(dve, "scan", u, "b01")
                freed(dve, "scan", u, "b23")
                if u >= 2:
                    for h in range(H):
                        freed(dve, "scan", u - 2, f"U{h}")
                ends = ei.rearrange("p h (j t) -> p h j t", t=BLK)[:, :, :, (0 if d else BLK - 1)]
                link(V.tensor_copy(sc["decay"][:, b], ends))
                V.tensor_tensor(ep, ep, q, ALU.mult).then_inc(qk_scaled, 1)
                full(dve, "scan", u, "kT")
                V.tensor_tensor(en, bank("scan", u, "kT")[:, :].rearrange("p (h n) -> p h n", h=H), en, ALU.mult).then_inc(free_of("scan", u, "kT"), 1)
                freed(dve, "scan", u, "rl")
                kk = sc[f"k{d}"][:, i, :].rearrange("p (h n) -> p h n", h=H)
                V.tensor_tensor(el, el, kk, ALU.mult).then_inc(qk_scaled, 1)
                V.tensor_tensor(ei, ei, q, ALU.mult).then_inc(qk_scaled, 1)

            def scan_states(u):
                d, i = UNITS[u]
                b = u % 2
                full(dve, "scan", u, "sc")
                if u == 0:
                    dve.wait_ge(zeroed, 4)
                else:
                    full(dve, "scan", u - 1, "o")
                mask = c(f"inc{d}").bitcast(U32).unsqueeze(1).to_broadcast([P, H, P])
                V.copy_predicated(sc[f"P{d}"], mask, bank("scan", u, "sc")[:, :].rearrange("p (h n) -> p h n", h=H)).then_inc(free_of("scan", u, "sc"), 1)
                for h in range(H):
                    full(dve, "scan", u, f"U{h}")
                if i:
                    dve.wait_ge(s0_in, 16)
                order = list(range(NBLK - 1, -1, -1) if d else range(NBLK))
                steps = NBLK if keeps(u) else NBLK - 1
                for n, j in enumerate(order[:steps]):
                    for h in range(H):
                        dst = sc["carry"][:, carry_of(u), h, :] if n == NBLK - 1 else sc["S"][:, h, P * n : P * n + P]
                        U = bank("scan", u, f"U{h}")[:, P * j : P * j + P]
                        src = state_before(u, n, h)
                        if src is None:
                            ins = V.tensor_copy(dst, U)
                        else:
                            ins = V.scalar_tensor_tensor(dst, src, sc["decay"][:, b, h, j : j + 1], U, ALU.mult, ALU.add)
                        if n == steps - 1:
                            ins.then_inc(free_of("scan", u, f"U{h}"), 1)
                    if n == NBLK - 2 and keeps(u):
                        ins.then_inc(states_ready, 1)
                        dve.wait_ge(states_ready, carry_of(u) + 1)
                    elif n < steps - 1:
                        link(ins)

            def scan_output(u):
                i = UNITS[u][1]
                cols = slice(P * i, P * i + P)
                full(dve, "scan", u, "o")
                first = i not in [UNITS[w][1] for w in range(u)]
                ps = bank("scan", u, "o")[:, :].rearrange("p (h n) -> p h n", h=H)
                o = cT[:, 0:H, cols]
                if first:
                    V.tensor_copy(o, ps).then_inc(free_of("scan", u, "o"), 1)
                else:
                    w = [x for x in range(u) if UNITS[x][1] == i][0]
                    freed(dve, "scan", w, "o")
                    V.tensor_tensor(o, o, ps, ALU.add).then_inc(free_of("scan", u, "o"), 1)

            def add_out(layer, half, j):
                if half == layer:
                    freed(dve, "out", layer, 1 - half, j)
                full(dve, "out", layer, half, j)
                for s, seg in enumerate(SEGS):
                    ins = V.scalar_tensor_tensor(xT[:, j, seg], bank("out", layer, half, j)[:, seg],
                                                 mod[:, layer, 2 * KD + j, s : s + 1], xT[:, j, seg], ALU.mult, ALU.add)
                ins.then_inc(free_of("out", layer, half, j), 1)

            def route(layer):
                b_rt = pr("b_rt").rearrange("p (l n) -> p l n", l=DEPTH)[:, layer]
                lg, l8, m8, i8, f8, oh, ml = (mo[n] for n in ("lg", "l8", "m8", "i8", "f8", "oh", "ml"))
                w, e4, g1, eq0, eq1, A, B = (mo[n] for n in ("w", "e4", "g1", "eq0", "eq1", "A", "B"))
                rank, floor, pos = mo["rank"], mo["floor"], mo["pos"]
                iota = c("iota16")
                link(V.memset(l8, -3.0e38))
                full(dve, "rt", layer)
                V.tensor_tensor(lg, bank("rt", layer)[:, 0 : NT * FOLD].rearrange("p (i n) -> p i n", i=NT)[:, :, 0:20],
                                b_rt.unsqueeze(1).to_broadcast([P, NT, 20]), ALU.add).then_inc(free_of("rt", layer), 1)
                freed(dve, "rt", layer)
                link(V.tensor_copy(l8[:, :, 0:NG], lg[:, :, 0:NG]))
                for i in range(NT):
                    link(V.max(m8[:, i, :], l8[:, i, :]))
                    link(V.max_index(i8[:, i, :].bitcast(U32), m8[:, i, :], l8[:, i, :]))
                link(V.tensor_copy(f8, i8.bitcast(U32)))
                V.tensor_tensor(e4, lg[:, :, 0:NG], m8[:, :, 0:1].to_broadcast([P, NT, NG]), ALU.subtract).then_inc(route_max, 1)
                link(V.tensor_tensor(oh, iota[:, 0:NG].unsqueeze(1).to_broadcast([P, NT, NG]), f8[:, :, 0:1].to_broadcast([P, NT, NG]), ALU.is_equal))
                g14 = g1.rearrange("p i (g e) -> p (i g) e", g=NG)
                oh4 = oh.rearrange("p i g -> p (i g)").unsqueeze(2).to_broadcast([P, NT * NG, EPG])
                link(V.tensor_scalar(g14, oh4, 1.0e30, 1.0e30, ALU.mult, ALU.subtract))
                link(V.tensor_tensor(ml, lg[:, :, NG:20], g1, ALU.add))
                for i in range(NT):
                    link(V.max(m8[:, i, :], ml[:, i, :]))
                    link(V.max_index(i8[:, i, :].bitcast(U32), m8[:, i, :], ml[:, i, :]))
                link(V.tensor_copy(f8, i8.bitcast(U32)))
                V.tensor_tensor(w[:, :, 0:1], m8[:, :, 1:2], m8[:, :, 0:1], ALU.subtract).then_inc(route_max, 1)
                it = iota.unsqueeze(1).to_broadcast([P, NT, NE])
                link(V.tensor_tensor(eq0, it, f8[:, :, 0:1].to_broadcast([P, NT, NE]), ALU.is_equal))
                link(V.tensor_tensor(eq1, it, f8[:, :, 1:2].to_broadcast([P, NT, NE]), ALU.is_equal))
                link(V.tensor_tensor(A, eq0, eq1, ALU.add))
                link(V.memset(B[:, 0, :], 0.0))
                for i in range(NT - 1):
                    link(V.tensor_tensor(B[:, i + 1, :], B[:, i, :], A[:, i, :], ALU.add))
                V.tensor_tensor(B[:, NT, :], B[:, NT - 1, :], A[:, NT - 1, :], ALU.add).then_inc(assigned, 1)
                dve.wait_ge(route_exp, 2 * layer + 1)
                link(V.tensor_reduce(w[:, :, 1:2], e4, AX_X, ALU.add))
                dve.wait_ge(route_exp, 2 * layer + 2)
                link(V.tensor_scalar(w[:, :, 2:3], w[:, :, 0:1], 1.0, None, ALU.add))
                link(V.tensor_tensor(w[:, :, 3:4], w[:, :, 1:2], w[:, :, 2:3], ALU.mult))
                link(V.reciprocal(w[:, :, 4:5], w[:, :, 3:4]))
                link(V.tensor_tensor(w[:, :, 5:6], w[:, :, 4:5], w[:, :, 0:1], ALU.mult))
                link(V.tensor_copy(pos[:, 2, :].unsqueeze(2), w[:, :, 4:5]))
                link(V.tensor_copy(pos[:, 3, :].unsqueeze(2), w[:, :, 5:6]))
                full(dve, "cum", layer)
                cum = bank("cum", layer)
                link(V.tensor_scalar(rank, cum[:, 0 : NT * NE].rearrange("p (i e) -> p i e", i=NT), 1.0, None, ALU.subtract))
                total, tiles = mo["base"], mo["tiles"]
                V.tensor_copy(total, cum[:, NT * NE : (NT + 1) * NE]).then_inc(free_of("cum", layer), 1)
                freed(dve, "cum", layer)
                link(V.memset(tiles, 1.0))
                link(V.memset(floor, 0.0))
                for j in range(1, OVER + 1):
                    V.scalar_tensor_tensor(tiles, total, float(CAP * j), tiles, ALU.is_gt, ALU.add)
                    link(V.scalar_tensor_tensor(floor, rank, float(CAP * j), floor, ALU.is_ge, ALU.add))
                two = tiles.rearrange("p (a b) -> p a b", b=2)
                link(V.tensor_tensor(mo["pairs"].unsqueeze(2), two[:, :, 0:1], two[:, :, 1:2], ALU.max))
                link(V.tensor_tensor(mo["pp"], mo["pairs"].unsqueeze(1).to_broadcast([P, NPAIR + 1, NPAIR]),
                                     c("before").rearrange("p (a b) -> p a b", b=NPAIR), ALU.mult))
                link(V.tensor_reduce(mo["first"], mo["pp"], AX_X, ALU.add))
                V.tensor_copy(mo["firsti"].bitcast(mybir.dt.int32), mo["first"]).then_inc(table_ready, 1)
                base = mo["base"].rearrange("p (a b) -> p a b", b=2)
                dve.wait_ge(table_ready, layer + 1)
                link(V.tensor_scalar(base, mo["first"][:, 0:NPAIR].unsqueeze(2).to_broadcast([P, NPAIR, 2]), float(P), float(P), ALU.mult, ALU.add))
                link(V.tensor_scalar(base[:, :, 1:2], base[:, :, 1:2], float(CAP), None, ALU.add))
                link(V.scalar_tensor_tensor(rank, floor, float(P - CAP), rank, ALU.mult, ALU.add))
                link(V.tensor_tensor(rank, rank, mo["base"].unsqueeze(1).to_broadcast([P, NT, NE]), ALU.add))
                for n, eq in enumerate((eq0, eq1)):
                    link(V.tensor_tensor(eq, eq, rank, ALU.mult))
                    link(V.tensor_reduce(pos[:, n, :], eq, AX_X, ALU.add))
                for n in range(4):
                    V.tensor_tensor(mo["diag"][:, n, :].rearrange("p (i t) -> p i t", i=NT), ident.unsqueeze(1).to_broadcast([P, NT, P]),
                                    pos[:, n, :].unsqueeze(2).to_broadcast([P, NT, P]), ALU.mult).then_inc(diag_ready, 1)

            def experts(layer):
                y = cT[:, :, :].rearrange("p k t -> p (k t)").rearrange("p (i n) -> p i n", i=NT)
                sems = loops[layer]
                if layer == 0:
                    dve.wait_ge(state_out, 32)
                else:
                    dve.wait_ge(cache_out, 64)
                full(dve, "out", layer, layer, KD - 1)
                link(V.memset(y, 0.0))
                route(layer)
                V.memset(mo["yS"][:, 0, :], 0.0).then_inc(sems["yS_ready"], 1)
                V.memset(mo["yS"][:, 1, :], 0.0).then_inc(sems["yS_ready"], 1)
                V.memset(mo["GT"], 0.0).then_inc(sems["GT_ready"], 1)
                for n, (name, count) in enumerate((("hid_ready", 1), ("hidT_full", 1), ("hidT_ready", 1), ("down_full", 1), ("summed", 3))):
                    for m in range(count):
                        V.memset(mo["prime"][:, 3 * n + m : 3 * n + m + 1], 0.0).then_inc(sems[name], 1)
                V.tensor_copy(mo["slot"], c("slot_id"))
                V.tensor_copy(mo["iota"], c("iota128")).then_inc(sems["primed"], 1)
                dve.wait_ge(sems["primed"], 1)
                sel, sel1, iota = mo["sel"], mo["sel1"], mo["iota"]
                loop_links = sems["primed"]

                def select(tile):
                    it = iota.unsqueeze(1).to_broadcast([P, NT, P])
                    n = tile * 6
                    V.tensor_tensor(sel1, it, mo["pos"][:, 0, :].unsqueeze(2).to_broadcast([P, NT, P]), ALU.is_equal).then_inc(loop_links, 1)
                    V.tensor_tensor(sel, it, mo["pos"][:, 1, :].unsqueeze(2).to_broadcast([P, NT, P]), ALU.is_equal).then_inc(loop_links, 1)
                    dve.wait_ge(loop_links, n - 6 + 1 + 2)
                    V.tensor_scalar(iota, iota, float(P), None, ALU.add).then_inc(loop_links, 1)
                    V.tensor_tensor(sel, sel, sel1, ALU.add).then_inc(sems["selected"], 1)
                    dve.wait_ge(sems["selected"], tile)
                    dve.wait_ge(loop_links, n - 6 + 1 + 3)

                select(1)
                with dve.Fori(0, NPAIR) as i:
                    with dve.Fori(first_tile(dve, i), first_tile(dve, i + 1)) as tile:
                        g = tile + 1
                        n = g * 6
                        dve.wait_ge(sems["gathered"], g * 2)
                        bc, GT, GT1, slot = mo["bc"], mo["GT"], mo["GT1"], mo["slot"]
                        V.scalar_tensor_tensor(GT1, bc[:, 0, :], slot, bc[:, 2, :], ALU.is_equal, ALU.mult).then_inc(loop_links, 1)
                        dve.wait_ge(loop_links, n - 6 + 1 + 4)
                        dve.wait_ge(sems["hidT_full"], g)
                        dve.wait_ge(sems["up_full"], g)
                        dve.wait_ge(sems["sg_ready"], g)
                        V.tensor_tensor(mo["hid"], psum[UP_BANK][:, :], mo["sg"], ALU.mult).then_inc(sems["hid_ready"], 1)
                        for m in range(6):
                            t, half = m // 2, slice(HALF * (m % 2), HALF * (m % 2) + HALF)
                            dve.wait_ge(sems["scattered"], n - 6 + m + 1)
                            dve.wait_ge(sems["summed"], n - 6 + m + 3)
                            V.tensor_tensor(y[:, t, half], psum[SCATTER_BANK + m % 3][:, :], y[:, t, half], ALU.add).then_inc(sems["summed"], 1)
                        V.scalar_tensor_tensor(GT, bc[:, 1, :], slot, bc[:, 3, :], ALU.is_equal, ALU.mult).then_inc(loop_links, 1)
                        dve.wait_ge(loop_links, n - 6 + 1 + 5)
                        V.tensor_scalar(slot, slot, float(P), None, ALU.add).then_inc(loop_links, 1)
                        V.tensor_tensor(GT, GT, GT1, ALU.add).then_inc(sems["GT_ready"], 1)
                        dve.wait_ge(sems["GT_ready"], g + 1)
                        dve.wait_ge(loop_links, n + 1)
                        select(g + 1)
                end = first_tile(dve, NPAIR) + 1
                n = end * 6
                for m in range(6):
                    t, half = m // 2, slice(HALF * (m % 2), HALF * (m % 2) + HALF)
                    dve.wait_ge(sems["scattered"], n - 6 + m + 1)
                    dve.wait_ge(sems["summed"], n - 6 + m + 3)
                    V.tensor_tensor(y[:, t, half], psum[SCATTER_BANK + m % 3][:, :], y[:, t, half], ALU.add).then_inc(sems["summed"], 1)
                gate = mod[:, layer, 5 * KD : 6 * KD]
                for k in range(KD):
                    full(dve, "yt", layer, k)
                    for s, seg in enumerate(SEGS):
                        ins = V.scalar_tensor_tensor(xT[:, k, seg], bank("yt", layer, k)[:, seg], gate[:, k, s : s + 1], xT[:, k, seg],
                                                     ALU.mult, ALU.add)
                    ins.then_inc(free_of("yt", layer, k), 1)

            dve.wait_ge(params_in, 16)
            V.tensor_tensor(omlb, omlb, lb, ALU.subtract).then_inc(lb_diff, 1)
            dve.wait_ge(lb_exp, 1)
            link(V.tensor_scalar(omlb, omlb, 1.0, None, ALU.add))
            link(V.reciprocal(lb, omlb))
            link(V.tensor_scalar(omlb, lb, -1.0, 1.0, ALU.mult, ALU.add))
            for step in STEPS0:
                kind, u = step[0], step[-1]
                if kind in ("hf1", "hf2"):
                    sine_argument(kind)
                elif kind == "mod":
                    modulation(*step[1:])
                elif kind == "apply1":
                    norm(0, 0)
                elif kind == "hf3":
                    dve.wait_ge(hyconst_in, 16)
                    filters()
                elif kind == "even" and step[1].startswith("hy"):
                    short_conv(*step[1:])
                    if step[1] == "hy2":
                        freed(dve, *step)
                        V.tensor_tensor(hy["u"][:, 4 + u, :], hy["u"][:, 4 + u, :], hy["u"][:, 8 + u, :], ALU.mult).then_inc(z_ready, 1)
                elif kind == "even" and step[1] in ("ff", "fb"):
                    forget(("ff", "fb").index(step[1]), u)
                elif kind == "dft":
                    spectra()
                elif kind == "inv":
                    for j in range(4):
                        full(dve, "inv", j)
                        V.scalar_tensor_tensor(hy["u"][:, 8 + j, :], hy["u"][:, 4 + j, :], pr("hy_bias")[:, j : j + 1], bank("inv", j)[:, 0:T],
                                               ALU.mult, ALU.add).then_inc(free_of("inv", j), 1)
                        freed(dve, "inv", j)
                        V.tensor_tensor(cT[:, 4 + j, :], hy["u"][:, 8 + j, :], hy["u"][:, j, :], ALU.mult).then_inc(hyena_done, 1)
                    dve.wait_ge(hyena_done, 4)
                elif kind == "decays":
                    if u == 0:
                        for j in range(H):
                            freed(dve, "even", "q", j)
                    scan_scale(u)
                elif kind == "products":
                    scan_states(u)
                elif kind == "outputs":
                    scan_output(u)
                elif kind == "out":
                    add_out(*step[1:])
                elif kind == "head":
                    for h in range(H):
                        freed(dve, "even", "g", h)
                        dve.wait_ge(head_rs, h + 1)
                        link(V.scalar_tensor_tensor(cT[:, h, :], cT[:, h, :], pr("hgrn_g"), rs[:, :], ALU.mult, ALU.mult))
                        V.tensor_tensor(cT[:, h, :], cT[:, h, :], sc["g"][:, h, :], ALU.mult).then_inc(mixed, 1)
            norm(0, 1)
            experts(0)
            norm(1, 0)
            link(V.tensor_tensor_reduce(out=at["t"][:, 0, 0:64], in0=pr("lam")[:, 0:64], in1=pr("lam")[:, 64:128], scale=1.0, scalar=0.0,
                                        op0=ALU.mult, op1=ALU.add, accum_out=at["lam"][:, 0:1]))
            V.tensor_tensor_reduce(out=at["t"][:, 0, 0:64], in0=pr("lam")[:, 128:192], in1=pr("lam")[:, 192:256], scale=1.0, scalar=0.0,
                                   op0=ALU.mult, op1=ALU.add, accum_out=at["lam"][:, 1:2]).then_inc(lam_dots, 1)
            dve.wait_ge(lam_dots, 1)
            norms = (("qc", 4, P, "cq", "cosc", "sinc"), ("kv", 2, P, "ck", "cosc", "sinc"),
                     ("qd", 8, 64, "dq", "cosd", "sind"), ("kd", 8, 64, "dk", "cosd", "sind"))
            for b, (name, n, d, gain, cos, sin) in enumerate(norms):
                for i in range(NT):
                    freed(dve, "odd", name, i)
                x = at[f"raw{b}"][:, :, 0 : n * d]
                t = at["t"][:, 0:NT, 0 : n * d]
                link(V.tensor_tensor(t, x, x, ALU.mult))
                for i in range(NT):
                    ins = V.tensor_reduce(at["ss"][:, b, n * i : n * i + n], t[:, i, :].rearrange("p (h d) -> p h d", h=n), AX_X, ALU.add)
                ins.then_inc(ss_ready, 1)
                dve.wait_ge(ss_ready, b + 1)
            for b, (name, n, d, gain, cos, sin) in enumerate(norms):
                dve.wait_ge(qk_rs, b + 1)
                raw = at[f"raw{b}"]
                g = pr(gain).unsqueeze(1).to_broadcast([P, n, d])
                for i in range(NT):
                    x = raw[:, i, 0 : n * d].rearrange("p (h d) -> p h d", h=n)
                    link(V.tensor_tensor(x, x, at["ss"][:, b, n * i : n * i + n].unsqueeze(2).to_broadcast([P, n, d]), ALU.mult))
                    ins = V.tensor_tensor(x, x, g, ALU.mult)
                    if i == 0:
                        ins.then_inc(normed, 1)
                        dve.wait_ge(normed, b + 1)
                    else:
                        link(ins)
                for i in range(1, NT):
                    x = raw[:, i, 0 : n * d].rearrange("p (h r two) -> p h r two", h=n, two=2)
                    x1, x2 = x[:, :, :, 0], x[:, :, :, 1]
                    cs = c(cos).rearrange("p (i r) -> p i r", i=2)[:, i - 1].unsqueeze(1).to_broadcast([P, n, d // 2])
                    sn = c(sin).rearrange("p (i r) -> p i r", i=2)[:, i - 1].unsqueeze(1).to_broadcast([P, n, d // 2])
                    t = [at["t"][:, m, 0 : n * d // 2].rearrange("p (h r) -> p h r", h=n) for m in range(4)]
                    V.tensor_tensor(t[0], x1, cs, ALU.mult)
                    V.tensor_tensor(t[1], x2, sn, ALU.mult)
                    V.tensor_tensor(t[2], x1, sn, ALU.mult)
                    link(V.tensor_tensor(t[3], x2, cs, ALU.mult))
                    V.tensor_tensor(x1, t[0], t[1], ALU.subtract)
                    ins = V.tensor_tensor(x2, t[2], t[3], ALU.add)
                    if i == 1:
                        link(ins)
                    else:
                        ins.then_inc(roped, 1)
                        dve.wait_ge(roped, b + 1)
            dve.wait_ge(lam_exps, 1)
            lam = at["lam"][:, 4:5]
            link(V.tensor_tensor(lam, at["lam"][:, 2:3], at["lam"][:, 3:4], ALU.subtract))
            link(V.tensor_scalar(lam, lam, LAM_INIT, None, ALU.add))
            link(V.tensor_scalar(at["lam"][:, 5:6], pr("subln_g"), 1.0 - LAM_INIT, None, ALU.mult))

            def row_max(u):
                kind, h, i = ATTN[u]
                nk = P if i == 0 else 3 * P
                for m in range(2 if kind == "d" else 1):
                    full(dve, "S", u, m)
                    if u >= 2:
                        dve.wait_ge(probs_ready, u - 1)
                    mx = at["mx"][:, u % 2, 4 * m : 4 * m + 4]
                    link(V.tensor_reduce(mx[:, 0:1], bank("S", u, m)[:, 0:nk], AX_X, ALU.max))
                    V.tensor_scalar(mx[:, 1:2], mx[:, 0:1], -((P if kind == "c" else 64) ** -0.5), None, ALU.mult).then_inc(neg_max, 1)

            def normalise(u):
                kind, h, i = ATTN[u]
                nk = P if i == 0 else 3 * P
                mx, Pb = at["mx"][:, u % 2, :], at["Pb"]
                for m in range(2 if kind == "d" else 1):
                    freed(dve, "S", u, m)
                link(V.reciprocal(mx[:, 3:4], mx[:, 2:3]))
                p0 = Pb[:, 2 * (u % 2), 0:nk]
                if kind == "c":
                    V.tensor_scalar(p0, p0, mx[:, 3:4], None, ALU.mult).then_inc(probs_ready, 1)
                else:
                    p1 = Pb[:, 2 * (u % 2) + 1, 0:nk]
                    link(V.reciprocal(mx[:, 7:8], mx[:, 6:7]))
                    link(V.tensor_scalar(p1, p1, mx[:, 7:8], lam, ALU.mult, ALU.mult))
                    V.scalar_tensor_tensor(p0, p0, mx[:, 3:4], p1, ALU.mult, ALU.subtract).then_inc(probs_ready, 1)

            row_max(0)
            for u in range(len(ATTN)):
                if u + 1 < len(ATTN):
                    row_max(u + 1)
                normalise(u)
            for h in range(H):
                dve.wait_ge(head_rs, H + h + 1)
                V.scalar_tensor_tensor(cT[:, 4 + h, :], at["od"][:, h, :], at["lam"][:, 5:6], rs[:, :], ALU.mult, ALU.mult).then_inc(mixed, 1)
            for half in range(2):
                for j in range(KD):
                    add_out(1, half, j)
            norm(1, 1)
            experts(1)

        @block.tensor
        def _(pe):
            mm = nc.tensor.matmul

            def open_bank(*name):
                b, n = banks.at[name]
                if n > 1:
                    pe.wait_ge(bank_free[b], n - 1)
                return psum[b]

            def loaded(n):
                s, load = slot_of(n)
                pe.wait_ge(slot_loaded[s], 16 * load)
                return ring[:, s, :].rearrange("p (k n) -> p k n", k=KD)

            def modulation(layer, b):
                w = loaded(index[("mod", layer, b)])
                ps = open_bank("ada", layer, b)
                for k in range(KD):
                    rows = slice(BLK * (k % 4), BLK * (k % 4) + BLK)
                    ins = mm(ps[rows, :], condT[:, k, :], w[:, k, :], start=k < 4, stop=k >= 4)
                ins.then_inc(full_of("ada", layer, b), 1)
                n = MOD_ALL.index((layer, b))
                freed(pe, "ada", layer, b)
                ps = open_bank("adt", layer, b)
                for m in range(4):
                    ins = mm(ps[:, FOLD * m : FOLD * m + FOLD], ada[:, n % 2, P * m : P * m + P], c("fold"), start=True, stop=True)
                ins.then_inc(full_of("adt", layer, b), 1)

            def norm(layer, which):
                name = (f"norm{which + 1}", layer)
                ps = open_bank(*name)
                for k in range(KD):
                    pe.wait_ge(squares_ready, KD * (2 * layer + which) + k + 1)
                    ins = mm(ps[:, 0:T], ones, hT[:, k, :], start=k == 0, stop=k == KD - 1)
                ins.then_inc(full_of(*name), 1)

            def features_out(ps, w, m, src):
                for k in range(KD):
                    ins = mm(ps[:, 0:T], w[:, k, P * m : P * m + P], src[:, k, :], start=k == 0, stop=k == KD - 1)
                return ins

            def tokens_out(ps, w, i, src):
                for k in range(KD):
                    ins = mm(ps[:, :], src[:, k, P * i : P * i + P], w[:, k, :], start=k == 0, stop=k == KD - 1)
                return ins

            def experts(layer):
                pe.wait_ge(h_ready, 2 * KD * (2 * layer + 2))
                sems = loops[layer]
                w_rt = pr("w_rt").rearrange("p (l k n) -> p l k n", l=DEPTH, k=KD)[:, layer]
                ps = open_bank("rk", layer)
                for k in range(KD):
                    rows = slice(BLK * (k % 4), BLK * (k % 4) + BLK)
                    ins = mm(ps[rows, 0:T], w_rt[:, k, :], hT[:, k, :], start=k < 4, stop=k >= 4)
                ins.then_inc(full_of("rk", layer), 1)
                freed(pe, "rk", layer)
                ps = open_bank("rt", layer)
                for i in range(NT):
                    ins = mm(ps[:, FOLD * i : FOLD * i + FOLD], mo["rk"][:, P * i : P * i + P], c("fold"), start=True, stop=True)
                ins.then_inc(full_of("rt", layer), 1)
                for i in range(NT):
                    for half in range(2):
                        ps = open_bank("ht", layer, i, half)
                        for k in range(4):
                            ins = nc.tensor.transpose(ps[:, P * k : P * k + P], hT[:, 4 * half + k, P * i : P * i + P], ident)
                        ins.then_inc(full_of("ht", layer, i, half), 1)
                pe.wait_ge(assigned, layer + 1)
                ps = open_bank("cum", layer)
                flat = lambda t: t.rearrange("p i e -> p (i e)")
                mm(ps[:, 0 : NT * NE], c("upto"), flat(mo["A"]), start=True, stop=False)
                mm(ps[:, 0 : NT * NE], ones, flat(mo["B"])[:, 0 : NT * NE], start=False, stop=True)
                mm(ps[:, NT * NE : (NT + 1) * NE], ones, mo["B"][:, NT, :], start=True, stop=True).then_inc(full_of("cum", layer), 1)
                for n in range(4):
                    pe.wait_ge(diag_ready, 4 * layer + n + 1)
                    ps = open_bank("pb", layer, n)
                    mm(ps[:, 0:T], ones, mo["diag"][:, n, :], start=True, stop=True).then_inc(full_of("pb", layer, n), 1)
                for i in range(NT):
                    for half in range(2):
                        freed(pe, "ht", layer, i, half)
                for n in range(4):
                    freed(pe, "pb", layer, n)
                pe.wait_ge(table_ready, layer + 1)
                pe.wait_ge(sems["primed"], 1)

                def gather(tile):
                    pe.wait_ge(sems["selected"], tile)
                    for k in range(KD):
                        for i in range(NT):
                            ins = mm(psum[GATHER_BANK + k // 4][:, P * (k % 4) : P * (k % 4) + P], mo["h"][:, i, P * k : P * k + P],
                                     mo["sel"][:, i, :], start=i == 0, stop=i == NT - 1)
                        if k % 4 == 3:
                            ins.then_inc(sems["gathered"], 1)

                def scatter(g, parts):
                    for m in parts:
                        pe.wait_ge(sems["summed"], g * 6 + (m - 5))
                        mm(psum[SCATTER_BANK + m % 3][:, :], mo["GT"][:, P * (m // 2) : P * (m // 2) + P], mo["yS"][:, m % 2, :],
                           start=True, stop=True).then_inc(sems["scattered"], 1)

                def weights_loaded(pair, kind):
                    for side in range(2):
                        pe.wait_ge(moe_loaded(side, kind), pair * 16 + 16 * (moe_loads(layer, side, kind) + 1))

                gather(1)
                with pe.Fori(0, NPAIR) as i:
                    with pe.Fori(first_tile(pe, i), first_tile(pe, i + 1)) as tile:
                        g = tile + 1
                        w = [[moe_block(side, kind) for side in range(2)] for kind in range(3)]
                        for kind, done in ((0, "gate_full"), (1, "up_full")):
                            pe.wait_ge(sems["yS_ready"], g * 2 + (kind - 1))
                            weights_loaded(i, kind)
                            for k in range(KD):
                                if kind == 0 and k % 4 == 0:
                                    pe.wait_ge(sems["hS_ready"], g * 2 + (k // 4 - 1))
                                for side in range(2):
                                    rows = slice(CAP * side, CAP * side + CAP)
                                    ins = mm(psum[kind][rows, :], mo["hS"][:, k, rows],
                                             w[kind][side].rearrange("p (k n) -> p k n", k=KD)[:, k, :], start=k == 0, stop=k == KD - 1)
                            ins.then_inc(sems[done], 1)
                        pe.wait_ge(sems["GT_ready"], g)
                        pe.wait_ge(sems["yS_ready"], g * 2)
                        scatter(g, (0, 1, 2))
                        pe.wait_ge(sems["hid_ready"], g + 1)
                        pe.wait_ge(sems["hidT_ready"], g)
                        for f in range(NF):
                            ins = nc.tensor.transpose(psum[HIDT_BANK][:, P * f : P * f + P], mo["hid"][:, P * f : P * f + P], ident)
                        ins.then_inc(sems["hidT_full"], 1)
                        scatter(g, (3, 4, 5))
                        pe.wait_ge(sems["hidT_ready"], g + 1)
                        weights_loaded(i, 2)
                        for half in range(2):
                            for f in range(NF):
                                for side in range(2):
                                    rows = slice(CAP * side, CAP * side + CAP)
                                    wd = w[2][side].rearrange("p (f n) -> p f n", f=NF)
                                    ins = mm(psum[half][rows, :], mo["hidT"][:, f, rows], wd[:, f, HALF * half : HALF * half + HALF],
                                             start=f == 0, stop=f == NF - 1)
                            ins.then_inc(sems["down_full"], 1)
                        gather(g + 1)
                end = first_tile(pe, NPAIR) + 1
                pe.wait_ge(sems["yS_ready"], end * 2)
                pe.wait_ge(sems["GT_ready"], end)
                pe.wait_ge(sems["hS_ready"], end * 2)
                scatter(end, range(6))
                pe.wait_ge(sems["summed"], end * 6 + 3)
                y = cT[:, :, :].rearrange("p k t -> p (k t)").rearrange("p (i n) -> p i n", i=NT)
                for k in range(KD):
                    ps = open_bank("yt", layer, k)
                    for i in range(NT):
                        ins = nc.tensor.transpose(ps[:, P * i : P * i + P], y[:, i, P * k : P * k + P], ident)
                    ins.then_inc(full_of("yt", layer, k), 1)

            def hyena(kind):
                if kind == "hf1":
                    pe.wait_ge(filter_in, 32)
                    ps = open_bank("hf1")
                    mm(ps[0:NHID, 0:T], hyp("w1", NFEAT), hyc("pos")[0:NFEAT], start=True, stop=True).then_inc(full_of("hf1"), 1)
                elif kind == "hf2":
                    pe.wait_ge(sin_done, 1)
                    ps = open_bank("hf2")
                    mm(ps[0:NHID, 0:T], hyp("w2", NHID), hy["s"][0:NHID, :], start=True, stop=True).then_inc(full_of("hf2"), 1)
                elif kind == "hf3":
                    pe.wait_ge(sin_done, 2)
                    for i in range(NT):
                        for half in range(2):
                            ps = open_bank("hf3", i, half)
                            mm(ps[:, :], hy["s"][0:NHID, P * i : P * i + P], hyp("w3", NHID)[:, HALF * half : HALF * half + HALF],
                               start=True, stop=True).then_inc(full_of("hf3", i, half), 1)
                elif kind == "G":
                    pe.wait_ge(hyconst_in, 16)
                    pe.wait_ge(filter_ready, 2 * NT)
                    for g, (seq, part, m) in enumerate(FILTER_DFT):
                        ps = open_bank("G", g)
                        tiles = seq_tiles[seq]
                        src = hy["hm"] if part == "im" else hy["hp"]
                        for n, i in enumerate(tiles):
                            ins = mm(ps[:, :], dft[seq][:, n, dft_columns(seq, part, m)], src[:, i, :], start=n == 0, stop=n == len(tiles) - 1)
                        ins.then_inc(full_of("G", g), 1)
                elif kind == "zt":
                    pe.wait_ge(z_ready, 4)
                    for i in range(NT):
                        ps = open_bank("zt", i)
                        for j in range(4):
                            ins = nc.tensor.transpose(ps[:, P * j : P * j + P], hy["u"][:, 4 + j, P * i : P * i + P], ident)
                        ins.then_inc(full_of("zt", i), 1)
                elif kind == "dft":
                    for i in range(NT):
                        freed(pe, "zt", i)
                    for s, (seq, m) in enumerate(SIGNAL_DFT):
                        tiles = seq_tiles[seq]
                        for grp, part in (("Ur", "re"), ("Ui", "imp")):
                            ps = open_bank(grp, s)
                            for n, i in enumerate(tiles):
                                ins = mm(ps[:, :], dft[seq][:, n, dft_columns(seq, part, m)], z_tm[:, i, :], start=n == 0, stop=n == len(tiles) - 1)
                            ins.then_inc(full_of(grp, s), 1)
                else:
                    pe.wait_ge(spec_ready, 3)
                    for ch in range(4):
                        ps = open_bank("inv", ch)
                        cc = slice(P * ch, P * ch + P)
                        for n, (z, f) in enumerate(((0, 0), (2, 1), (1, 2), (3, 3))):
                            mm(ps[:, LAT], Z[:, z, cc], inv_lat[:, f, :], start=n == 0, stop=n == 3)
                        for f in range(2):
                            ins = mm(ps[:, CTX], Z[:, 4 + f, cc], inv_ctx[:, f, :], start=f == 0, stop=f == 1)
                        ins.then_inc(full_of("inv", ch), 1)

            def heads_of(h):
                return slice(P * h, P * h + P)

            def scan_decays(u):
                d, i = UNITS[u]
                pe.wait_ge(lf_ready, NT * d + i + 1)
                lf, kk = sc[f"lf{d}"][:, i, :], sc[f"k{d}"][:, i, :]
                tri = con[:, CONSTS.at[f"mid{d}"][0] : CONSTS.at[f"mid{d}"][0] + 2 * P]
                for pair, g in enumerate(("b01", "b23")):
                    ps = open_bank("scan", u, g)
                    for x in range(2):
                        ins = mm(ps[:, 2 * P * x : 2 * P * x + 2 * P], lf[:, heads_of(2 * pair + x)], tri, start=True, stop=True)
                    ins.then_inc(full_of("scan", u, g), 1)
                ps = open_bank("scan", u, "kT")
                for h in range(H):
                    ins = nc.tensor.transpose(ps[:, heads_of(h)], kk[:, heads_of(h)], ident)
                ins.then_inc(full_of("scan", u, "kT"), 1)
                ps = open_bank("scan", u, "rl")
                mm(ps[:, :], c(f"last{d}"), lf, start=True, stop=True).then_inc(full_of("scan", u, "rl"), 1)

            def scan_products(u):
                b = u % 2
                pe.wait_ge(qk_scaled, 3 * u + 1)
                freed(pe, "scan", u, "kT")
                ps = open_bank("scan", u, "sc")
                for h in range(H):
                    ins = mm(ps[:, heads_of(h)], sc["en"][:, b, h, :], sc["ep"][:, b, h, :], start=True, stop=True)
                ins.then_inc(full_of("scan", u, "sc"), 1)
                pe.wait_ge(qk_scaled, 3 * u + 2)
                pe.wait_ge(vx_ready, NBLK * (u + 1))
                for h in range(H):
                    ps = open_bank("scan", u, f"U{h}")
                    mm(ps[:, :], sc["el"][:, b, h, :], sc["vx"][:, h].rearrange("p j n -> p (j n)"),
                       start=True, stop=True).then_inc(full_of("scan", u, f"U{h}"), 1)

            def scan_outputs(u):
                d, i = UNITS[u]
                b = u % 2
                pe.wait_ge(qk_scaled, 3 * u + 3)
                freed(pe, "scan", u, "sc")
                if keeps(u):
                    pe.wait_ge(states_ready, carry_of(u) + 1)
                else:
                    for w in (u - 1, u):
                        for h in range(H):
                            freed(pe, "scan", w, f"U{h}")
                ps = open_bank("scan", u, "o")
                order = list(range(NBLK - 1, -1, -1) if d else range(NBLK))
                for h in range(H):
                    ins = mm(ps[:, heads_of(h)], sc["v"][:, i, heads_of(h)], sc[f"P{d}"][:, h, :], start=True, stop=False)
                    for n, j in enumerate(order):
                        S = state_before(u, n, h)
                        if S is not None:
                            t = slice(BLK * j, BLK * j + BLK)
                            ins = mm(ps[:, P * h + BLK * j : P * h + BLK * j + BLK], S, sc["ei"][:, b, h, t], start=False, stop=n == NBLK - 1)
                ins.then_inc(full_of("scan", u, "o"), 1)

            def out_part(layer, half, j):
                w = ring[:, slot_of(index[("out", layer, half)])[0], :].rearrange("p (k n) -> p k n", k=4)
                if j == 0:
                    loaded(index[("out", layer, half)])
                    if layer == 0 and half == 1:
                        pe.wait_ge(hyena_done, 4)
                    elif layer == 1 and half == 0:
                        freed(pe, "O", len(ATTN) // 2 - 1)
                    else:
                        pe.wait_ge(mixed, H * (layer + 1))
                ps = open_bank("out", layer, half, j)
                for k in range(4):
                    ins = mm(ps[:, 0:T], w[:, k, P * j : P * j + P], cT[:, 4 * half + k, :], start=k == 0, stop=k == 3)
                ins.then_inc(full_of("out", layer, half, j), 1)

            pe.wait_ge(params_in, 16)
            pe.wait_ge(cond_ready, 1)
            pe.wait_ge(consts_in, 16)
            for step in STEPS0:
                kind, u = step[0], step[-1]
                if kind == "sum1":
                    norm(0, 0)
                elif kind == "mod":
                    modulation(*step[1:])
                elif kind == "even":
                    _, name, j = step
                    w = loaded(index[("even", name)])
                    pe.wait_ge(h_ready, 2 * KD)
                    ps = open_bank("even", name, j)
                    projection = tokens_out if even_groups(name) == NT else features_out
                    projection(ps, w, j, hT).then_inc(full_of("even", name, j), 1)
                elif kind == "out":
                    out_part(*step[1:])
                elif kind == "decays":
                    scan_decays(u)
                elif kind == "products":
                    scan_products(u)
                elif kind == "outputs":
                    scan_outputs(u)
                elif kind == "head":
                    pe.wait_ge(head_squares, 1)
                    sq = sc["vx"].rearrange("p h j n -> p (h j n)")[:, 0 : H * T].rearrange("p (h n) -> p h n", h=H)
                    for h in range(H):
                        ps = open_bank("on", h)
                        mm(ps[:, 0:T], ones, sq[:, h, :], start=True, stop=True).then_inc(full_of("on", h), 1)
                elif kind != "apply1":
                    hyena(kind)
            norm(0, 1)
            experts(0)
            norm(1, 0)
            pe.wait_ge(h_ready, 3 * 2 * KD)
            for name in ODD_ORDER:
                w = loaded(index[("odd", name)])
                for i in range(NT):
                    ps = open_bank("odd", name, i)
                    tokens_out(ps, w, i, hT).then_inc(full_of("odd", name, i), 1)
            for b, (name, n) in enumerate((("qc", 4), ("kv", 2), ("qd", 4), ("kd", 4))):
                pe.wait_ge(roped, b + 1)
                for i in range(NT):
                    ps = open_bank("tr", name, i)
                    for h in range(n):
                        ins = nc.tensor.transpose(ps[:, P * h : P * h + P], at[f"raw{b}"][:, i, P * h : P * h + P], ident)
                    ins.then_inc(full_of("tr", name, i), 1)
            pe.wait_ge(caches_in, 64)
            for name in ("qc", "kv", "qd", "kd"):
                for i in range(NT):
                    freed(pe, "tr", name, i)
            for i in range(NT):
                freed(pe, "odd", "vd", i)
            for u in range(len(ATTN) + 2):
                if u < len(ATTN):
                    kind, h, i = ATTN[u]
                    cols, keys = slice(P * i, P * i + P), slice(0, P) if i == 0 else slice(P, 4 * P)
                    nk = keys.stop - keys.start
                    for m in range(2 if kind == "d" else 1):
                        q = at["qcT"] if kind == "c" else at[f"qd{m}"]
                        k_all = at["kcT"][:, h // 2, keys] if kind == "c" else at["kdT"][:, h, keys]
                        ps = open_bank("S", u, m)
                        mm(ps[:, 0:nk], q[:, h, cols], k_all, start=True, stop=True).then_inc(full_of("S", u, m), 1)
                if 0 < u <= len(ATTN):
                    nt = 1 if ATTN[u - 1][2] == 0 else 3
                    pe.wait_ge(probs_ready, u)
                    ps = open_bank("PT", u - 1)
                    for n in range(nt):
                        ins = nc.tensor.transpose(ps[:, P * n : P * n + P], at["Pb"][:, 2 * ((u - 1) % 2), P * n : P * n + P], ident)
                    ins.then_inc(full_of("PT", u - 1), 1)
                if u > 1:
                    kind, h, i = ATTN[u - 2]
                    slots = (0,) if i == 0 else (1, 2, 3)
                    freed(pe, "PT", u - 2)
                    ps = open_bank("O", u - 2)
                    for n, s in enumerate(slots):
                        v = at["vc"][:, s, P * (h // 2) : P * (h // 2) + P] if kind == "c" else at["vd"][:, s, P * h : P * h + P]
                        ins = mm(ps[:, 0:P], v, at["PT"][:, (u - 2) % 2, P * n : P * n + P], start=n == 0, stop=n == len(slots) - 1)
                    ins.then_inc(full_of("O", u - 2), 1)
            pe.wait_ge(head_squares, 2)
            sq = at["raw0"].rearrange("p i n -> p (i n)").rearrange("p (h n) -> p h n", h=H)
            for h in range(H):
                ps = open_bank("sn", h)
                mm(ps[:, 0:T], ones, sq[:, h, :], start=True, stop=True).then_inc(full_of("sn", h), 1)
            for half in range(2):
                for j in range(KD):
                    out_part(1, half, j)
            norm(1, 1)
            experts(1)


def _constants():
    con = np.zeros((P, CONSTS.total), np.float32)

    def put(name, a):
        start, width = CONSTS.at[name]
        con[: a.shape[0], start : start + width] = a.reshape(a.shape[0], width)

    put("ident", np.eye(P))
    put("ones", np.ones((P, P)))
    put("eps", np.full((P, 1), EPS))
    put("iota16", np.broadcast_to(np.arange(NE), (P, NE)))
    put("fold", np.arange(P)[:, None] % BLK == np.arange(FOLD)[None, :])
    put("upto", np.arange(P)[:, None] <= np.arange(P)[None, :])
    put("iota128", np.broadcast_to(P + np.arange(P), (P, P)))
    put("slot_id", P + np.arange(P).reshape(P, 1))
    put("before", np.broadcast_to(np.arange(NPAIR)[None, :] < np.arange(NPAIR + 1)[:, None], (P, NPAIR + 1, NPAIR)))
    s, t = np.arange(P)[:, None], np.arange(P)[None, :]
    same = s // BLK == t // BLK
    middle = t // BLK * BLK + BLK // 2
    put("inc0", same & (s <= t))
    put("mid0", (same & (s <= t)) * 1.0 - (same & (s <= middle - 1)) * 1.0)
    put("last0", same & (s > t))
    put("inc1", same & (s >= t))
    put("mid1", (same & (s >= t)) * 1.0 - (same & (s >= middle)) * 1.0)
    put("last1", same & (s < t))
    row, col = np.arange(DEC) // 64, np.arange(DEC) % 64
    for name, dim in (("c", P), ("d", 64)):
        half = dim // 2
        inv = np.float32(10000.0) ** (-np.arange(0, half, 2, dtype=np.float32) / np.float32(half))
        ang = np.concatenate([row[:, None].astype(np.float32) * inv, col[:, None].astype(np.float32) * inv], -1)
        for fn, f in (("cos", np.cos), ("sin", np.sin)):
            put(fn + name, f(ang).reshape(2, P, half).transpose(1, 0, 2))
    hyc = np.zeros((P, HYCONST.total), np.float32)

    def puth(name, a):
        start, width = HYCONST.at[name]
        hyc[: a.shape[0], start : start + width] = a.reshape(a.shape[0], width)

    pos, win = [], []
    deltas = np.abs(np.linspace(math.log(1e-2) / 1.5, math.log(1e-2) / 0.3, HALF, dtype=np.float32))
    for n in (SEQ, DEC):
        tt = np.linspace(0.0, 1.0, n, dtype=np.float32)[:, None]
        w = (np.float32(2.0 * math.pi) * np.arange(n, dtype=np.float32) / np.float32(n)).astype(np.float32)
        f = np.linspace(1e-4, 15, 16, dtype=np.float32)
        ang = (w[:, None] * f[None, :]).astype(np.float32)
        pos.append(np.concatenate([tt, np.cos(ang), -np.sin(ang)], -1).T)
        win.append(np.exp(-tt * deltas[None, :]))
    puth("pos", np.concatenate(pos, 1))
    puth("window", np.concatenate(win, 0).reshape(NT, P, HALF).transpose(1, 0, 2))
    for name, n in (("lat", DEC), ("ctx", SEQ)):
        t, f = np.arange(n)[:, None], np.arange(n)[None, :]
        re, im = np.cos(np.pi * t * f / n), -np.sin(np.pi * t * f / n)
        nyquist = (-1.0) ** np.arange(n)
        imp, re2 = im[:, :P].copy(), re[:, :P].copy()
        imp[:, 0], re2[:, 0] = nyquist, nyquist
        m = np.concatenate([re, im, imp, re2], 1)
        puth("dft_" + name, m.reshape(n // P, P, -1).transpose(1, 0, 2))
        f, t = np.arange(n)[:, None], np.arange(n)[None, :]
        ire, iim = np.cos(np.pi * t * f / n) / n, -np.sin(np.pi * t * f / n) / n
        ire[0] = 0.5 / n
        iim[0] = 0.5 * (-1.0) ** np.arange(n) / n
        puth("inv_" + name, np.concatenate([ire, iim], 0).reshape(2 * n // P, P, n).transpose(1, 0, 2))
    return con, hyc


def _blocks(w):
    n = w.shape[1] // HALF
    return w.reshape(KD, P, n, HALF).transpose(2, 1, 0, 3).reshape(n, P, KD * HALF)


def _columns(v):
    return np.ascontiguousarray(v.reshape(-1, P).T)


def kernel(**a):
    import concourse.bacc as bacc
    from concourse.bass_utils import run_bass_kernel_spmd

    a = {k: np.asarray(v) for k, v in a.items()}
    par = np.zeros((P, PARAMS.total), np.float32)

    def put(name, v):
        start, width = PARAMS.at[name]
        par[: v.shape[0], start : start + width] = v.reshape(v.shape[0], width)

    rows = lambda v: np.broadcast_to(v.reshape(1, -1), (P, v.size))
    put("cond", np.stack([_columns(a["c_ctx"]), _columns(a["c"][0])], -1))
    put("b_mod", _columns(a["b_mod"]))
    put("n1", _columns(a["norm1_g"]))
    put("n2", _columns(a["norm2_g"]))
    put("conv_w", _columns(a["hy_conv_w"][0]))
    put("conv_b", _columns(a["hy_conv_b"][0]))
    put("hgrn_g", _columns(a["hgrn_norm_g"][0]))
    put("subln_g", _columns(a["d_subln_g"][0]))
    for to, of in (("hb1", "hy_b1"), ("hf1", "hy_freq1"), ("hb2", "hy_b2"), ("hf2", "hy_freq2")):
        put(to, a[of][0].reshape(-1, 1))
    put("hy_bias", _columns(a["hy_bias"][0]))
    put("lower", rows(a["hgrn_lower"]))
    for to, of in (("cq", "c_qnorm_g"), ("ck", "c_knorm_g"), ("dq", "d_qnorm_g"), ("dk", "d_knorm_g")):
        put(to, rows(a[of][0]))
    put("lam", rows(np.concatenate([a["d_lambda_q1"][0], a["d_lambda_k1"][0], a["d_lambda_q2"][0], a["d_lambda_k2"][0]])))
    put("b_rt", rows(np.concatenate([a["moe_b_grp"], a["moe_b_rt"]], -1)))
    w_rt = np.concatenate([a["moe_w_grp"], a["moe_w_rt"]], -1)
    w_rt = np.pad(w_rt, ((0, 0), (0, 0), (0, BLK - 20)))
    put("w_rt", w_rt.reshape(DEPTH, KD, P, BLK).transpose(2, 0, 1, 3).reshape(P, -1))
    hypar = np.zeros((P, HYPAR.total), np.float32)
    for name, v in (("w1", a["hy_w1"][0]), ("w2", a["hy_w2"][0]), ("w3", a["hy_w3"][0])):
        start, width = HYPAR.at[name]
        hypar[: v.shape[0], start : start + width] = v
    con, hyc = _constants()
    x = np.concatenate([a["x_prompt"][0], a["x_sample"][0]], 0)
    mods = [_blocks(w) for w in a["w_mod"]]
    even, odd = _blocks(a["even_w_in"][0]), _blocks(a["odd_w_in"][0])
    w_outs = [a[n][0].reshape(2, KD // 2, P, D).transpose(0, 2, 1, 3).reshape(2, P, -1) for n in ("even_w_out", "odd_w_out")]
    proj = np.stack([mods[n[1]][n[2]] if n[0] == "mod" else even[EVEN_COLUMN[n[1]]] if n[0] == "even"
                     else odd[ODD_ORDER.index(n[1])] if n[0] == "odd" else w_outs[n[1]][n[2]] for n in STREAM])
    moe = np.empty((DEPTH, NE, 3, P, KD * HALF), np.float32)
    for kind, name in enumerate(("moe_w_gate", "moe_w_up")):
        moe[:, :, kind] = a[name].reshape(DEPTH, NE, KD, P, FE).transpose(0, 1, 3, 2, 4).reshape(DEPTH, NE, P, -1)
    moe[:, :, 2] = a["moe_w_down"].reshape(DEPTH, NE, NF, P, D).transpose(0, 1, 3, 2, 4).reshape(DEPTH, NE, P, -1)
    arrays = {
        "params": par, "hypar": hypar, "consts": con, "hyconst": hyc,
        "x": np.ascontiguousarray(x.T.reshape(KD, P, T).transpose(1, 0, 2)),
        "s0": np.ascontiguousarray(a["state_hgrn"][0, 0].transpose(2, 0, 1, 3)),
        "ck": np.ascontiguousarray(a["cache_c_k"][0, 0].transpose(2, 0, 1)),
        "cv": np.ascontiguousarray(a["cache_c_v"][0, 0].transpose(1, 0, 2)).reshape(P, -1),
        "dk": np.ascontiguousarray(a["cache_d_k"][0, 0].transpose(2, 0, 1)),
        "dv": np.ascontiguousarray(a["cache_d_v"][0, 0].transpose(1, 0, 2)).reshape(P, -1),
        "proj": proj, "moe": moe.reshape(DEPTH * NE * 3, P, KD * HALF),
    }
    outs = {"y": (P, KD, T), "state": (2, P, H, P), "ock": (P, 2 * P), "ocv": (P, 2 * P), "odk": (P, HALF), "odv": (P, HALF)}
    nc = bacc.Bacc("TRN2", target_bir_lowering=False, num_devices=1)
    args = [nc.dram_tensor("in_" + n, v.shape, F32, kind="ExternalInput").ap() for n, v in arrays.items()]
    args += [nc.dram_tensor("out_" + n, s, F32, kind="ExternalOutput").ap() for n, s in outs.items()]
    trunk_kernel(nc, *args)
    r = run_bass_kernel_spmd(nc, [{"in_" + n: v for n, v in arrays.items()}], core_ids=[0]).results[0]
    y = np.asarray(r["out_y"]).transpose(2, 1, 0).reshape(T, D)
    heads = lambda n, k: np.asarray(r["out_" + n]).reshape(SEQ, k, P).transpose(1, 0, 2)[None, None]
    return (y[None, :SEQ], y[None, SEQ:], np.asarray(r["out_state"]).transpose(0, 2, 1, 3)[None, None],
            heads("ock", 2), heads("ocv", 2), heads("odk", H), heads("odv", H))
```

```python
import math
from contextlib import ExitStack

import concourse.bass as bass
import numpy as np
from concourse import mybir
from concourse.alu_op_type import AluOpType as ALU

ACT = mybir.ActivationFunctionType
F32 = mybir.dt.float32
F32R = mybir.dt.float32r
U32 = mybir.dt.uint32
AX_X = mybir.AxisListType.X

P = 128
D = 1024
KD = D // P
SEQ, DEC = 128, 256
T = SEQ + DEC
NT = T // P
CTX, LAT = slice(0, SEQ), slice(SEQ, T)
SEGS = (CTX, LAT)
DEPTH = 2
EPS = 1e-6
H = 4
BLK = 32
NBLK = P // BLK
HALF = 512
NHID = 64
NFEAT = 33
NE = 16
NG = 4
EPG = 4
FE = 512
NF = FE // P
NPAIR = NE // 2
CAP = P // 2
OVER = (T - 1) // CAP
FOLD = 96
LAM_INIT = 0.8 - 0.6 * math.exp(-0.3)
MAGIC = 1.5 * 2.0**23
TWO_PI_HI = 6.28125
TWO_PI_LO = 2 * math.pi - 6.28125
PI_BELOW = 3.1415925
BANKS = 8
ACT_CHUNKS = 5
PROJ_SLOTS = 3

MOD_BLOCKS = 6 * D // HALF
MOD_FIRST = 2 * D // HALF
MODS = [("mod", layer, b) for layer in range(DEPTH) for b in range(MOD_BLOCKS)]
EVEN_COLUMN = {"q": 0, "ff": 1, "fb": 2, "v": 3, "g": 4, "hy0": 5, "hy1": 6, "hy2": 7}
UNITS = [(0, 0), (0, 1), (0, 2), (1, 0), (1, 2), (1, 1)]


def even_groups(name):
    return NT if name in ("v", "ff", "fb") else 4


def project(name):
    return [("even", name, j) for j in range(even_groups(name))]


def out_half(layer, half):
    return [("out", layer, half, j) for j in range(KD)]


def scans_with(fillers):
    stages = [("decays", 0)]
    for u in range(len(UNITS)):
        stages += ([("decays", u + 1)] if u + 1 < len(UNITS) else []) + ([("scale_heads", UNITS[u - 1][1])] if u > 3 else [])
        stages += [("products", u), ("outputs", u)] + ([("square_heads", UNITS[u][1])] if u > 2 else [])
    share = {"decays": 1, "products": 2, "outputs": 1, "square_heads": 0, "scale_heads": 0}
    length = {"even": 4, "out": 2, "mod": 2}
    left = sum(length[f[0]] for f in fillers)
    gaps = sum(share[stage[0]] for stage in stages)
    steps, fillers, owed = [], list(fillers), 0.0
    per_gap = left / gaps
    for stage in stages:
        steps.append(stage)
        owed += per_gap * share[stage[0]]
        while fillers and owed >= length[fillers[0][0]] / 2:
            owed -= length[fillers[0][0]]
            steps.append(fillers.pop(0))
    return steps + fillers


STEPS0 = [
    ("hf1",), ("sum1",), MODS[0], ("hf2",), *MODS[1:MOD_FIRST], ("apply1",),
    *project("hy0"), ("hf3",), *MODS[4:6], ("G",),
    *project("hy1"), *MODS[6:8],
    *project("hy2"), *MODS[8:10],
    *project("q"), ("zt",), ("even", "v", 0), ("dft",), ("even", "v", 1), ("even", "v", 2), *MODS[10:11], ("inv",),
    *project("ff"), *MODS[11:13],
    *scans_with(project("fb") + MODS[13:15] + project("g") + MODS[15:22] + out_half(0, 1)[:5]),
    *out_half(0, 1)[5:7], ("scale_heads", UNITS[-1][1]), out_half(0, 1)[7], *out_half(0, 0),
]
LATE_MODS = MODS[22:]

ODD_COLUMN = {"qc": 0, "kv": 1, "qd": 2, "kd": 3, "vd": 4}
NORMED = ["qc", "kv", "qd", "kd"]
ATTN = [(kind, h, i) for kind in "cd" for h in range(H) for i in range(NT)]


def normed_projection(names):
    tiles = [(name, i) for name in names for i in range(NT)]
    return [(([("rope", *tiles[n - 1])] if n else []) + [("odd", *tile)], [("sums", *tile)]) for n, tile in enumerate(tiles)]


def attention():
    steps = []
    (kd0, kd0_sums), (kd1, kd1_sums), (kd2, kd2_sums) = normed_projection(["kd"])
    after = {
        0: [("rope", "qd", 2)] + kd0, 1: kd0_sums, 2: [("tr", "qd", 2)], 3: kd1, 4: kd1_sums, 5: kd2, 6: kd2_sums + [("tr", "kd", 0)],
        7: [("rope", "kd", 2), ("odd", "vd", 0)], 8: [("tr", "kd", 1)], 9: [("odd", "vd", 1), ("tr", "kd", 2)], 11: [("odd", "vd", 2)],
    }
    gqa_half = out_half(1, 0)
    for j in range(6):
        after[15 + 2 * j] = [gqa_half[j]]
    for h in range(H - 1):
        last = len(ATTN) // 2 + NT * h + NT + 2
        after[last] = after.get(last, []) + [("square_heads", h)]
        after[last + 1] = after.get(last + 1, []) + [("scale_heads", h)]
    for u in range(len(ATTN) + 3):
        steps += [("attend", u)] + after.get(u, [])
    return steps + [("square_heads", H - 1), gqa_half[6], ("scale_heads", H - 1), gqa_half[7]]


def first_projections():
    steps, tiles = [], []
    for projection, sums in normed_projection(["qc", "kv", "qd"]):
        tiles.append(sums[0][1:])
        steps += projection + sums + ([("tr", *tiles[-3])] if len(tiles) > 2 else [])
    return steps + [("lambda",), ("tr", *tiles[-2])]


STEPS1 = [*first_projections(), *attention(), *out_half(1, 1)]
STEPS = [STEPS0, STEPS1]


def block_of(step):
    return step if step[0] == "mod" else step[:3] if step[0] == "out" else step[:2]


BLOCKS = [list(dict.fromkeys(block_of(step) for step in steps if step[0] in ("mod", "even", "odd", "out"))) for steps in STEPS]
BLOCKS[0] += LATE_MODS
STREAM = BLOCKS[0] + BLOCKS[1]
LAYER_BLOCKS = [len(blocks) for blocks in BLOCKS]


class Columns:

    def __init__(self, widths):
        self.at, self.total = {}, 0
        for name, width in widths:
            self.at[name] = (self.total, width)
            self.total += width

    def of(self, tensor, name, parts=P):
        start, width = self.at[name]
        return tensor[0:parts, start : start + width]


PARAMS = Columns([
    ("cond", KD * 2), ("b_mod", DEPTH * 48), ("n1", DEPTH * KD), ("n2", DEPTH * KD),
    ("conv_w", 3 * 12), ("conv_b", 12), ("hgrn_g", 1), ("subln_g", 1),
    ("hb1", 1), ("hf1", 1), ("hb2", 1), ("hf2", 1), ("hy_bias", 4),
    ("lower", 2 * HALF), ("cq", P), ("ck", P), ("dq", 64), ("dk", 64),
    ("lam", 4 * 64), ("b_rt", DEPTH * 20), ("w_rt", DEPTH * KD * BLK),
])
HYPAR = Columns([("w1", NHID), ("w2", NHID), ("w3", 2 * HALF)])
CONSTS = Columns([
    ("ident", P), ("ones", P), ("eps", 1), ("iota16", NE),
    ("mid0", P), ("inc0", P), ("mid1", P), ("inc1", P), ("last0", P), ("last1", P),
    ("fold", FOLD), ("upto", P), ("iota128", P), ("slot_id", 1), ("before", NPAIR * (NPAIR + 1)), ("over", OVER), ("side", NE),
    ("cosc", 2 * 64), ("sinc", 2 * 64), ("cosd", 2 * 32), ("sind", 2 * 32),
])
HYCONST = Columns([
    ("pos", T), ("window", NT * HALF), ("dft_lat", 2 * 768), ("dft_ctx", 512),
    ("inv_lat", 4 * DEC), ("inv_ctx", 2 * SEQ),
])


class Banks:

    def __init__(self):
        self.at, self.used, self.next = {}, [0] * BANKS, 0

    def take(self, *name, bank=None):
        if bank is None:
            bank = self.next
            self.next = (bank + 1) % BANKS
        self.used[bank] += 1
        self.at[name] = (bank, self.used[bank])


GATE_BANK, UP_BANK, GATHER_BANK, SCATTER_BANK, HIDT_BANK = 0, 1, 2, 4, 7
SCAN_GROUPS = {"decays": ("b01", "b23", "kT", "rl"), "products": ("sc", "U0", "U1", "U2", "U3"), "outputs": ("o",)}
FILTER_DFT = [("lat", "re", 0), ("lat", "re", 1), ("lat", "im", 0), ("lat", "im", 1), ("lat", "re2", 0),
              ("ctx", "re", 0), ("ctx", "im", 0), ("ctx", "re2", 0)]
SIGNAL_DFT = [("lat", 0), ("lat", 1), ("ctx", 0)]


def maps(u):
    return range(2 if ATTN[u][0] == "d" else 1)


def groups_of(layer, step):
    kind, u = step[0], step[-1]
    if kind == "attend":
        return ([("S", u, m) for m in maps(u)] if u < len(ATTN) else []) + (
            [("PT", u - 2)] if 2 <= u < len(ATTN) + 2 else []) + ([("O", u - 3)] if u >= 3 else [])
    if kind == "mod":
        return [("ada", *step[1:]), ("adt", *step[1:])]
    if kind in ("decays", "products", "outputs"):
        return [("scan", u, g) for g in SCAN_GROUPS[kind]]
    if kind == "square_heads":
        return [] if layer == 0 else [("heads", u)]
    if kind == "scale_heads":
        return [("ot", u)] if layer == 0 else []
    return {
        "sum1": [("norm1", 0)], "hf3": [("hf3", i, half) for i in range(NT) for half in range(2)], "apply1": [],
        "G": [("G", g) for g in range(len(FILTER_DFT))], "zt": [("zt", i) for i in range(NT)],
        "dft": [(g, s) for s in range(len(SIGNAL_DFT)) for g in ("Ur", "Ui")], "inv": [("inv", ch) for ch in range(4)],
        "rope": [], "sums": [], "lambda": [],
    }.get(kind, [step])


def plan_banks():
    banks = Banks()
    for layer in range(DEPTH):
        if layer:
            banks.take("norm1", layer)
        for step in STEPS[layer]:
            for group in groups_of(layer, step):
                banks.take(*group)
        banks.take("norm2", layer)
        banks.take("rk", layer)
        banks.take("rt", layer)
        for i in range(NT):
            for half in range(2):
                banks.take("ht", layer, i, half)
        if layer == 0:
            for step in LATE_MODS:
                for group in groups_of(0, step):
                    banks.take(*group)
        banks.take("cum", layer)
        for n in range(4):
            banks.take("pb", layer, n, bank=SCATTER_BANK + n)
        for k in range(KD):
            banks.take("yt", layer, k)
    return banks


def trunk_kernel(nc, params_d, hypar_d, consts_d, hyconst_d, x_d, s0_d, ck_d, cv_d, dk_d, dv_d,
                 proj_d, moe_d, y_d, state_d, ock_d, ocv_d, odk_d, odv_d):
    banks = plan_banks()
    with ExitStack() as ctx:
        def sb(name, shape, dt=F32):
            return ctx.enter_context(nc.sbuf_tensor(name, shape, dt))

        def sem(name):
            return ctx.enter_context(nc.semaphore(name))

        xT = sb("xT", [P, KD, T])
        hT = sb("hT", [P, KD, T])
        cT = sb("cT", [P, KD, T])
        par = sb("par", [P, PARAMS.total])
        con = sb("con", [P, CONSTS.total])
        ring = sb("ring", [P, PROJ_SLOTS, KD * HALF])
        mod = sb("mod", [P, DEPTH, 48, 2])
        gs = sb("gs", [P, DEPTH, 2, KD, 2])
        condT = sb("condT", [P, KD, BLK])
        ada = sb("ada", [P, 2, HALF])
        rs = sb("rs", [P, T])
        lnt = sb("lnt", [P, T])
        arena_cols = 22616
        arena = sb("arena", [P, arena_cols])
        high, low = sb("high", [P, D], F32R), sb("low", [P, D], F32R)
        owner = sb("owner", [P, T], F32R)
        psum = [ctx.enter_context(nc.psum_tensor(f"bank{b}", [P, HALF], F32)) for b in range(BANKS)]

        def carve(shapes):
            out, at = {}, 0
            for name, shape in shapes:
                n = int(np.prod(shape))
                view = arena[:, at : at + n]
                if len(shape) == 2:
                    view = view.rearrange("p (a b) -> p a b", a=shape[0])
                elif len(shape) == 3:
                    view = view.rearrange("p (a b c) -> p a b c", a=shape[0], b=shape[1])
                out[name] = view
                at += n
            assert at <= arena_cols, at
            return out

        hy = carve([("hyc", (HYCONST.total,)), ("hyp", (HYPAR.total,)), ("G", (8, HALF)),
                    ("u", (12, T)), ("hp", (NT, HALF)), ("hm", (NT, HALF)),
                    ("a", (HALF,)), ("b", (HALF,)), ("n", (T,)), ("s", (T,))])
        hz = carve([("hyc", (HYCONST.total,)), ("hyp", (HYPAR.total,)), ("G", (8, HALF)),
                    ("u", (12, T)), ("z_tm", (NT, HALF)), ("Z", (6, HALF)),
                    ("t1", (HALF,)), ("t2", (HALF,))])
        z_tm, Z = hz["z_tm"], hz["Z"]
        sc = carve([("q", (H, T)), ("lf0", (NT, HALF)), ("lf1", (NT, HALF)), ("k0", (NT, HALF)), ("k1", (NT, HALF)), ("g", (H, T)),
                    ("vx", (H, NBLK, P)), ("S", (H, (NBLK - 1) * P)), ("s0", (2, H, P)), ("carry", (4, H, P)),
                    ("ep", (2, H, P)), ("en", (2, H, P)), ("ei", (2, H, P)), ("el", (2, H, P)),
                    ("P0", (H, P)), ("P1", (H, P)), ("decay", (2, H, NBLK)), ("mean", (NT, 2 * H)),
                    ("spare", (arena_cols - 22584,)), ("v", (NT, HALF))])
        at = carve([("vc", (4, 2 * P)), ("vd", (4, HALF)), ("qcT", (H, T)), ("kcT", (2, 4 * P)),
                    ("qd0", (H, T)), ("qd1", (H, T)), ("kdT", (H, 4 * P)), ("raw0", (NT, HALF)),
                    ("raw1", (NT, HALF)), ("raw2", (NT, HALF)), ("raw3", (NT, HALF)),
                    ("t", (4, HALF)), ("ss", (4, 24)), ("lt", (4, 24)), ("lam", (8,)),
                    ("Pb", (6, T)), ("PT", (2, T)), ("mx", (3, 8))])
        mo = carve([("ring", (3, KD * HALF)), ("hS", (KD, P)), ("sg", (FE,)), ("hid", (FE,)),
                    ("hidT", (NF, P)), ("weight", (1,)), ("sel", (NT, P)), ("sel1", (NT, P)), ("GT", (T,)), ("GT1", (T,)),
                    ("bc", (4, T)), ("diag", (4, T)), ("rk", (T,)), ("iota", (P,)), ("slot", (1,)), ("prime", (16,)),
                    ("lg", (NT, 20)), ("l8", (NT, 8)), ("m8", (NT, 8)), ("i8", (NT, 8)), ("f8", (NT, 8)),
                    ("oh", (NT, NG)), ("ml", (NT, NE)), ("w", (NT, 8)), ("e4", (NT, NG)),
                    ("g1", (NT, NE)), ("eq0", (NT, NE)), ("eq1", (NT, NE)), ("A", (NT, NE)), ("B", (NT + 1, NE)),
                    ("rank", (NT, NE)), ("floor", (NT + 1, NE)), ("pairs", (NPAIR,)),
                    ("pp", (NPAIR + 1, NPAIR)), ("first", (NPAIR + 1,)), ("firsti", (NPAIR + 1,)), ("base", (NE,)), ("pos", (4, NT))])
        weight = mo["weight"]
        h_rows = hT[:, :, :].rearrange("p k t -> p (k t)").rearrange("p (i n) -> p i n", i=NT)

        params_in, consts_in, x_in = sem("params_in"), sem("consts_in"), sem("x_in")
        filter_in, hyconst_in = sem("filter_in"), sem("hyconst_in")
        s0_in, caches_in = sem("s0_in"), sem("caches_in")
        slot_loaded = [sem(f"slot_loaded{s}") for s in range(2 * PROJ_SLOTS)]
        bank_full = [sem(f"bank_full{b}") for b in range(BANKS)]
        bank_free = [sem(f"bank_free{b}") for b in range(BANKS)]
        dve_link, act_link = sem("dve_link"), sem("act_link")
        cond_ready, mod_ready, lb_diff, lb_exp = sem("cond_ready"), sem("mod_ready"), sem("lb_diff"), sem("lb_exp")
        squares_ready, rs_ready, scaled = sem("squares_ready"), sem("rs_ready"), sem("scaled")
        h_by_act, h_by_dve = sem("h_by_act"), sem("h_by_dve")
        sin_arg, sin_done, filter_ready = sem("sin_arg"), sem("sin_done"), sem("filter_ready")
        conv_bias, z_ready, spec_ready, hyena_done = sem("conv_bias"), sem("z_ready"), sem("spec_ready"), sem("hyena_done")
        f_ready, lf_ready, zeroed, vx_ready = sem("f_ready"), sem("lf_ready"), sem("zeroed"), sem("vx_ready")
        exps_ready, qk_scaled, states_ready = sem("exps_ready"), sem("qk_scaled"), sem("states_ready")
        head_squares, head_rs, mixed = sem("head_squares"), sem("head_rs"), sem("mixed")
        ss_ready, qk_rs, normed, roped = sem("ss_ready"), sem("qk_rs"), sem("normed"), sem("roped")
        lam_dots, lam_exps, pads_zero = sem("lam_dots"), sem("lam_exps"), sem("pads_zero")
        neg_max, probs_ready = sem("neg_max"), sem("probs_ready")
        cleared, sums_zero = sem("cleared"), sem("sums_zero")
        route_max, route_exp, assigned, diag_ready, table_ready = (
            sem("route_max"), sem("route_exp"), sem("assigned"), sem("diag_ready"), sem("table_ready"))
        loop_names = ("selected", "gathered", "hS_ready", "gate_full", "up_full", "sg_ready", "hid_ready", "hidT_full",
                      "hidT_ready", "down_full", "owner_ready", "weighed", "high_ready", "split", "scattered", "summed", "primed")
        loops = [{n: sem(f"{n}{layer}") for n in loop_names} for layer in range(DEPTH)]
        state_out, cache_out, y_out = sem("state_out"), sem("cache_out"), sem("y_out")

        def full(eng, *name):
            b, n = banks.at[name]
            eng.wait_ge(bank_full[b], n)

        def bank(*name):
            return psum[banks.at[name][0]]

        def freed(eng, *name):
            b, n = banks.at[name]
            eng.wait_ge(bank_free[b], n)

        def free_of(*name):
            return bank_free[banks.at[name][0]]

        def full_of(*name):
            return bank_full[banks.at[name][0]]

        def features_mixed(eng, layer):
            if layer == 0:
                for i in range(NT):
                    freed(eng, "ot", i)
            else:
                eng.wait_ge(mixed, H)

        def residual(eng, adds, k=KD - 1):
            layer = (adds - 1) // 2
            if adds % 2:
                freed(eng, "out", layer, 0 if layer == 0 else 1, k)
            else:
                freed(eng, "yt", layer, k)

        MOD_ALL = [entry[1:] for entry in MODS]

        def mods_needed(layer, which):
            return MOD_ALL.index((layer, MOD_FIRST - 1 if which == 0 else 5 * D // HALF - 1)) + 1

        def keeps(u):
            return UNITS[u] not in ((0, 2), (1, 1))

        def carry_of(u):
            return sum(keeps(w) for w in range(u))

        def state_before(u, n, h):
            d, i = UNITS[u]
            if n:
                return sc["S"][:, h, P * (n - 1) : P * n]
            return None if i == 0 else sc["s0"][:, d, h, :] if keeps(u) else sc["carry"][:, carry_of(u - 1), h, :]

        c = lambda name: CONSTS.of(con, name)
        pr = lambda name, parts=P: PARAMS.of(par, name, parts)
        ident, ones, eps = c("ident"), c("ones"), c("eps")
        n1 = pr("n1").rearrange("p (l k) -> p l k", l=DEPTH)
        n2 = pr("n2").rearrange("p (l k) -> p l k", l=DEPTH)
        hyc = lambda name: HYCONST.of(hy["hyc"], name)
        hyp = lambda name, parts: HYPAR.of(hy["hyp"], name, parts)
        dft = {"lat": hyc("dft_lat").rearrange("p (k n) -> p k n", k=2),
               "ctx": hyc("dft_ctx").rearrange("p (k n) -> p k n", k=1)}
        seq_tiles = {"ctx": [0], "lat": [1, 2]}
        n_freq = {"ctx": 1, "lat": 2}
        inv_lat = hyc("inv_lat").rearrange("p (f t) -> p f t", f=4)
        inv_ctx = hyc("inv_ctx").rearrange("p (f t) -> p f t", f=2)
        window = hyc("window").rearrange("p (i n) -> p i n", i=NT)
        conv_w = pr("conv_w").rearrange("p (t c) -> p t c", t=3)
        lower = pr("lower").rearrange("p (r n) -> p r n", r=2)
        lb, omlb = lower[:, 0, :], lower[:, 1, :]

        def dft_columns(seq, part, m):
            n = n_freq[seq] * P
            start = {"re": m * P, "im": n + m * P, "imp": 2 * n if m == 0 else n + m * P, "re2": 2 * n + P}[part]
            return slice(start, start + P)

        def slot_of(n):
            layer = 0 if n < LAYER_BLOCKS[0] else 1
            first = 0 if layer == 0 else LAYER_BLOCKS[0]
            s = (n - first) % PROJ_SLOTS
            earlier = sum(1 for m in range(first) if m % PROJ_SLOTS == s) + (NE // 2 if layer else 0)
            return s, earlier + (n - first) // PROJ_SLOTS + 1

        index = {name: n for n, name in enumerate(STREAM)}

        def last_group(name):
            if name[0] == "mod":
                return ("ada", name[1], name[2])
            if name[0] == "even":
                return ("even", name[1], even_groups(name[1]) - 1)
            if name[0] == "odd":
                return ("odd", name[1], NT - 1)
            return (*name, KD - 1)

        def moe_block(side, kind):
            return (mo["ring"] if side else ring)[:, kind, :]

        def moe_loaded(side, kind):
            return slot_loaded[PROJ_SLOTS * side + kind]

        def moe_loads(layer, side, kind):
            if side:
                return layer * NE // 2
            return sum(slot_of(n)[0] == kind for n in range(sum(LAYER_BLOCKS[: layer + 1]))) + layer * NE // 2

        def first_tile(eng, pair):
            return eng.value_load(mo["firsti"][0:1, bass.ds(pair, 1)].bitcast(mybir.dt.int32), min_val=0, max_val=NPAIR * (OVER + 1))

        block = ctx.enter_context(nc.Block())

        @block.sync
        def _(sp):
            sp.dma_start(par[:, :], params_d).then_inc(params_in, 16)
            sp.dma_start(con[:, :], consts_d).then_inc(consts_in, 16)
            sp.dma_start(hy["hyc"][:, 0:T], hyconst_d[:, 0:T]).then_inc(filter_in, 16)
            sp.dma_start(hy["hyp"], hypar_d).then_inc(filter_in, 16)
            sp.dma_start(xT[:, :, :], x_d).then_inc(x_in, 16)

            def load_blocks(first, count, wait_slot=None):
                for n in range(first, first + count):
                    s, _ = slot_of(n)
                    if n == first + s and wait_slot:
                        wait_slot(s)
                    before = n - PROJ_SLOTS
                    if before >= first:
                        full(sp, *last_group(STREAM[before]))
                    sp.dma_start(ring[:, s, :], proj_d[n]).then_inc(slot_loaded[s], 16)
                    if n == MOD_FIRST:
                        sp.dma_start(hy["hyc"][:, T:], hyconst_d[:, T:]).then_inc(hyconst_in, 16)

            def load_experts(layer):
                end = sum(LAYER_BLOCKS[: layer + 1])
                last = {slot_of(n)[0]: STREAM[n] for n in range(end - PROJ_SLOTS, end)}

                def load(pair, kind, side):
                    at_block = pair * 6 + (layer * NE * 3 + 3 * side + kind)
                    sp.dma_start(moe_block(side, kind),
                                 moe_d[bass.ds(at_block, 1)].rearrange("o p n -> p (o n)")).then_inc(moe_loaded(side, kind), 16)

                def load_first(kind):
                    full(sp, *last_group(last[kind]))
                    load(0, kind, 0)

                order = sorted(range(3), key=lambda kind: STREAM.index(last[kind]))
                load_first(order[0])
                features_mixed(sp, layer)
                if layer == 0:
                    sp.wait_ge(state_out, 32)
                else:
                    sp.wait_ge(cache_out, 64)
                for kind in range(3):
                    load(0, kind, 1)
                for kind in sorted(order[1:]) if layer == 0 else order[1:]:
                    load_first(kind)
                sems = loops[layer]
                sp.wait_ge(table_ready, layer + 1)
                with sp.Fori(1, NPAIR) as i:
                    first = first_tile(sp, i) + 1
                    for kind in range(3):
                        if kind == 0:
                            sp.wait_ge(sems["gate_full"], first - 1)
                        elif kind == 1:
                            sp.wait_ge(sems["up_full"], first - 1)
                        else:
                            sp.wait_ge(sems["down_full"], first * 2 - 1)
                        for side in range(2):
                            load(i, kind, side)
                return first_tile(sp, NPAIR) + 1

            load_blocks(0, LAYER_BLOCKS[0])
            end = load_experts(0)

            def experts_done(kind):
                if kind == 2:
                    sp.wait_ge(loops[0]["down_full"], end * 2 - 1)
                else:
                    sp.wait_ge(loops[0][("gate_full", "up_full")[kind]], end - 1)

            load_blocks(LAYER_BLOCKS[0], LAYER_BLOCKS[1], experts_done)
            load_experts(1)
            for k in range(KD):
                freed(sp, "yt", 1, k)
                sp.dma_start(y_d[:, k, :], xT[:, k, :]).then_inc(y_out, 16)
            sp.wait_ge(y_out, 16 * KD)

        @block.gpsimd
        def _(pool):
            def set_up(layer):
                sems = loops[layer]
                full(pool, "out", layer, layer, KD - 1)
                nc.gpsimd.memset(mo["l8"], -3.0e38)
                nc.gpsimd.memset(mo["B"][:, 0, :], 0.0).then_inc(cleared, 1)
                starts = ("split",) * 2 + ("hid_ready", "hidT_full", "hidT_ready", "down_full") + ("summed",) * 3
                for n, name in enumerate(starts):
                    nc.gpsimd.memset(mo["prime"][:, n : n + 1], 0.0).then_inc(sems[name], 1)
                nc.gpsimd.tensor_copy(mo["slot"], c("slot_id"))
                nc.gpsimd.tensor_copy(mo["iota"], c("iota128"))
                nc.gpsimd.memset(cT[:, :, :], 0.0).then_inc(sums_zero, 1)
                pool.wait_ge(sums_zero, layer + 1)
                zeros = cT[:, :, :].rearrange("p k t -> p (k t)")
                nc.gpsimd.tensor_copy(owner[:, :], zeros[:, 0:T]).then_inc(sems["owner_ready"], 1)
                nc.gpsimd.tensor_copy(low[:, :], zeros[:, 0:D])
                nc.gpsimd.tensor_copy(high[:, :], zeros[:, 0:D]).then_inc(sems["primed"], 1)

            nc.gpsimd.memset(condT[:, :, :], 0.0).then_inc(zeroed, 1)
            pool.wait_ge(hyena_done, 4)
            nc.gpsimd.memset(sc["vx"], 0.0).then_inc(zeroed, 1)
            nc.gpsimd.memset(sc["P0"], 0.0).then_inc(zeroed, 1)
            nc.gpsimd.memset(sc["P1"], 0.0).then_inc(zeroed, 1)
            pool.dma_start(sc["s0"], s0_d).then_inc(s0_in, 16)
            pool.wait_ge(zeroed, 4)
            for u, (d, i) in enumerate(UNITS):
                freed(pool, "even", "v", i)
                if u:
                    full(pool, "scan", u - 1, f"U{H - 1}")
                for j in range(NBLK):
                    rows = slice(BLK * j, BLK * j + BLK)
                    nc.gpsimd.tensor_copy(
                        sc["vx"][rows, :, j, :], sc["v"][rows, i, :].rearrange("p (h n) -> p h n", h=H)
                    ).then_inc(vx_ready, 1)
                if u and UNITS[u - 1][1] == 0:
                    for h in range(H):
                        freed(pool, "scan", u - 1, f"U{h}")
                    pool.dma_start(state_d[UNITS[u - 1][0]], sc["carry"][:, carry_of(u - 1)]).then_inc(state_out, 16)
            pool.wait_ge(state_out, 32)
            set_up(0)
            freed(pool, "yt", 0, KD - 1)
            nc.gpsimd.memset(at["qd0"][64:P], 0.0).then_inc(pads_zero, 1)
            nc.gpsimd.memset(at["qd1"][0:64], 0.0).then_inc(pads_zero, 1)
            for dst, src in ((at["kcT"][:, :, P : 2 * P], ck_d), (at["kdT"][:, :, P : 2 * P], dk_d),
                             (at["vc"][:, 1, :], cv_d), (at["vd"][:, 1, :], dv_d)):
                pool.dma_start(dst, src).then_inc(caches_in, 16)
            pool.wait_ge(normed, 2)
            pool.dma_start(ock_d, at["raw1"][:, 0, 0 : 2 * P]).then_inc(cache_out, 16)
            freed(pool, "odd", "kv", 0)
            pool.dma_start(ocv_d, at["vc"][:, 0, :]).then_inc(cache_out, 16)
            pool.wait_ge(normed, 4)
            pool.dma_start(odk_d, at["raw3"][:, 0, :]).then_inc(cache_out, 16)
            freed(pool, "odd", "vd", 0)
            pool.dma_start(odv_d, at["vd"][:, 0, :]).then_inc(cache_out, 16)
            pool.wait_ge(cache_out, 64)
            set_up(1)

        @block.scalar
        def _(act):
            links = [0]

            def link(ins):
                links[0] += 1
                ins.then_inc(act_link, 1)
                act.wait_ge(act_link, links[0])

            def norm_sums(layer, which):
                count = 2 * layer + which
                for k in range(KD):
                    if count:
                        residual(act, count, k)
                    nc.scalar.activation(hT[:, k, :], xT[:, k, :], ACT.Square).then_inc(squares_ready, 1)
                name = (f"norm{which + 1}", layer)
                full(act, *name)
                nc.scalar.activation(lnt[:, :], bank(*name)[:, 0:T], ACT.Ln, bias=eps, scale=1.0 / D).then_inc(free_of(*name), 1)
                freed(act, *name)
                nc.scalar.activation(rs[:, :], lnt[:, :], ACT.Exp, scale=-0.5).then_inc(rs_ready, 1)

            def norm_shift(layer, which):
                count = 2 * layer + which
                act.wait_ge(mod_ready, mods_needed(layer, which))
                for k in range(ACT_CHUNKS):
                    act.wait_ge(scaled, count * KD + k + 1)
                    for s, seg in enumerate(SEGS):
                        nc.scalar.activation(hT[:, k, seg], hT[:, k, seg], ACT.Identity, bias=mod[:, layer, 24 * which + k, s : s + 1],
                                             scale=gs[:, layer, which, k, s : s + 1]).then_inc(h_by_act, 1)

            def norm(layer, which):
                norm_sums(layer, which)
                norm_shift(layer, which)

            def head_sums(h):
                full(act, "heads", h)
                if h:
                    act.wait_ge(mixed, h)
                nc.scalar.activation(lnt[:, :], bank("heads", h)[:, 0:T], ACT.Ln, bias=eps, scale=1.0 / P).then_inc(free_of("heads", h), 1)
                freed(act, "heads", h)
                nc.scalar.activation(rs[:, :], lnt[:, :], ACT.Exp, scale=-0.5).then_inc(head_rs, 1)

            mods_done = [0]

            def modulation(layer, b):
                if mods_done[0] >= 2:
                    full(act, "adt", *MOD_ALL[mods_done[0] - 2])
                full(act, "ada", layer, b)
                nc.scalar.activation(ada[:, mods_done[0] % 2, :], bank("ada", layer, b)[:, :], ACT.Copy).then_inc(free_of("ada", layer, b), 1)
                mods_done[0] += 1

            def experts(layer):
                sems = loops[layer]
                full(act, "rk", layer)
                nc.scalar.activation(mo["rk"], bank("rk", layer)[:, 0:T], ACT.Copy).then_inc(free_of("rk", layer), 1)
                act.wait_ge(*((state_out, 32) if layer == 0 else (cache_out, 64)))
                for i in range(NT):
                    for half in range(2):
                        full(act, "ht", layer, i, half)
                for i in range(NT):
                    for half in range(2):
                        nc.scalar.activation(h_rows[:, i, HALF * half : HALF * half + HALF], bank("ht", layer, i, half)[:, :],
                                             ACT.Copy).then_inc(free_of("ht", layer, i, half), 1)
                if layer == 0:
                    for step in LATE_MODS:
                        modulation(*step[1:])
                act.wait_ge(route_max, 2 * layer + 1)
                nc.scalar.activation(mo["e4"], mo["e4"], ACT.Exp).then_inc(route_exp, 1)
                act.wait_ge(route_max, 2 * layer + 2)
                nc.scalar.activation(mo["w"][:, :, 0:1], mo["w"][:, :, 0:1], ACT.Exp).then_inc(route_exp, 1)
                act.wait_ge(table_ready, layer + 1)
                act.wait_ge(sems["primed"], 1)

                def gathered(half, tile):
                    act.wait_ge(sems["gathered"], tile * 2 + (half - 1))
                    nc.scalar.activation(mo["hS"][:, 4 * half : 4 * half + 4, :],
                                         psum[GATHER_BANK + half][:, :].rearrange("p (k n) -> p k n", k=4),
                                         ACT.Copy).then_inc(sems["hS_ready"], 1)

                for half in range(2):
                    gathered(half, 1)
                for n in range(4):
                    full(act, "pb", layer, n)
                    nc.scalar.activation(mo["bc"][:, n, :], bank("pb", layer, n)[:, 0:T], ACT.Copy).then_inc(free_of("pb", layer, n), 1)
                with act.Fori(0, NPAIR) as i:
                    with act.Fori(first_tile(act, i), first_tile(act, i + 1)) as tile:
                        g = tile + 1
                        act.wait_ge(sems["hid_ready"], g)
                        act.wait_ge(sems["gate_full"], g)
                        nc.scalar.activation(mo["sg"], psum[GATE_BANK][:, :], ACT.Silu).then_inc(sems["sg_ready"], 1)
                        act.wait_ge(sems["down_full"], g * 2 - 1)
                        act.wait_ge(sems["hidT_full"], g + 1)
                        nc.scalar.activation(mo["hidT"], psum[HIDT_BANK][:, :].rearrange("p (f n) -> p f n", f=NF),
                                             ACT.Copy).then_inc(sems["hidT_ready"], 1)
                        act.wait_ge(sems["scattered"], g * 6)
                        act.wait_ge(sems["split"], g * 2)
                        act.wait_ge(sems["weighed"], g)
                        for half in range(2):
                            act.wait_ge(sems["down_full"], g * 2 + half)
                            nc.scalar.activation(high[:, HALF * half : HALF * half + HALF], psum[half][:, :], ACT.Identity,
                                                 scale=weight).then_inc(sems["high_ready"], 1)
                        act.wait_ge(sems["up_full"], g)
                        for half in range(2):
                            gathered(half, g + 1)

            def projected(name, j):
                full(act, "even", name, j)
                ps = bank("even", name, j)
                if name.startswith("hy"):
                    ch = 4 * int(name[2]) + j
                    nc.scalar.activation(hy["u"][:, ch, :], ps[:, 0:T], ACT.Identity, bias=pr("conv_b")[:, ch : ch + 1],
                                         scale=conv_w[:, 1, ch : ch + 1]).then_inc(conv_bias, 1)
                elif name == "q" or name == "g":
                    act.wait_ge(filter_ready, 2 * NT)
                    nc.scalar.activation(sc[name][:, j, :], ps[:, 0:T], ACT.Silu).then_inc(free_of("even", name, j), 1)
                elif name == "v":
                    nc.scalar.activation(sc["v"][:, j, :], ps[:, :], ACT.Copy).then_inc(free_of("even", name, j), 1)
                else:
                    act.wait_ge(hyena_done, 4)
                    d = 0 if name == "ff" else 1
                    nc.scalar.activation(sc[f"k{d}"][:, j, :], ps[:, :], ACT.Sigmoid).then_inc(free_of("even", name, j), 1)
                    if j == NT - 1:
                        for i in range(NT):
                            act.wait_ge(f_ready, NT * d + i + 1)
                            lf = sc[f"lf{d}"][:, i, :]
                            nc.scalar.activation(lf, lf, ACT.Ln).then_inc(lf_ready, 1)

            def odd_projected(name, i):
                full(act, "odd", name, i)
                ps = bank("odd", name, i)
                done = free_of("odd", name, i)
                slot = (0, 2, 3)[i]
                if name == "vd":
                    nc.scalar.activation(at["vd"][:, slot, :], ps[:, :], ACT.Copy).then_inc(done, 1)
                elif name == "kv":
                    nc.scalar.activation(at["raw1"][:, i, 0 : 2 * P], ps[:, 0 : 2 * P], ACT.Copy)
                    nc.scalar.activation(at["vc"][:, slot, :], ps[:, 2 * P :], ACT.Copy).then_inc(done, 1)
                else:
                    nc.scalar.activation(at[f"raw{NORMED.index(name)}"][:, i, :], ps[:, :], ACT.Copy).then_inc(done, 1)

            def transposed(name, i):
                act.wait_ge(pads_zero, 2)
                full(act, "tr", name, i)
                ps = bank("tr", name, i)[:, :].rearrange("p (h n) -> p h n", h=H)
                done = free_of("tr", name, i)
                cols, slot = slice(P * i, P * i + P), (0, 2, 3)[i]
                keys = slice(P * slot, P * slot + P)
                if name == "qc":
                    nc.scalar.activation(at["qcT"][:, :, cols], ps, ACT.Copy).then_inc(done, 1)
                elif name == "kv":
                    nc.scalar.activation(at["kcT"][:, :, keys], ps[:, 0:2, :], ACT.Copy).then_inc(done, 1)
                elif name == "qd":
                    nc.scalar.activation(at["qd0"][0:64, :, cols], ps[0:64], ACT.Copy)
                    nc.scalar.activation(at["qd1"][64:P, :, cols], ps[64:P], ACT.Copy).then_inc(done, 1)
                else:
                    nc.scalar.activation(at["kdT"][:, :, keys], ps, ACT.Copy).then_inc(done, 1)

            maps_done = [0]

            def attend(u):
                if 2 <= u < len(ATTN) + 2:
                    w = u - 2
                    nk = P if ATTN[w][2] == 0 else 3 * P
                    full(act, "PT", w)
                    if w >= 2:
                        full(act, "O", w - 2)
                    nc.scalar.activation(at["PT"][:, w % 2, 0:nk], bank("PT", w)[:, 0:nk], ACT.Copy).then_inc(free_of("PT", w), 1)
                if u >= 3:
                    kind, h, i = ATTN[u - 3]
                    cols = slice(P * i, P * i + P)
                    full(act, "O", u - 3)
                    dst = cT[:, h if kind == "c" else 4 + h, cols]
                    nc.scalar.activation(dst, bank("O", u - 3)[:, 0:P], ACT.Copy).then_inc(free_of("O", u - 3), 1)
                if u < len(ATTN):
                    kind, h, i = ATTN[u]
                    nk = P if i == 0 else 3 * P
                    for m in maps(u):
                        maps_done[0] += 1
                        act.wait_ge(neg_max, maps_done[0])
                        if u >= 3:
                            full(act, "PT", u - 3)
                        mx = at["mx"][:, u % 3, 4 * m : 4 * m + 4]
                        nc.scalar.activation(at["Pb"][:, 2 * (u % 3) + m, 0:nk], bank("S", u, m)[:, 0:nk], ACT.Exp, bias=mx[:, 1:2],
                                             scale=(P if kind == "c" else 64) ** -0.5, accum_out=mx[:, 2:3]).then_inc(free_of("S", u, m), 1)

            act.wait_ge(params_in, 16)
            act.wait_ge(zeroed, 1)
            nc.scalar.activation(condT[:, :, 0:2], pr("cond").rearrange("p (k s) -> p k s", s=2), ACT.Silu).then_inc(cond_ready, 1)
            act.wait_ge(lb_diff, 1)
            nc.scalar.activation(omlb, omlb, ACT.Exp).then_inc(lb_exp, 1)
            act.wait_ge(x_in, 16)
            act.wait_ge(consts_in, 16)
            for step in STEPS0:
                kind, u = step[0], step[-1]
                if kind in ("hf1", "hf2"):
                    act.wait_ge(sin_arg, int(kind[2]))
                    nc.scalar.activation(hy["s"][0:NHID, :], hy["n"][0:NHID, :], ACT.Sin).then_inc(sin_done, 1)
                elif kind == "sum1":
                    norm_sums(0, 0)
                elif kind == "apply1":
                    norm_shift(0, 0)
                elif kind == "mod":
                    modulation(*step[1:])
                elif kind == "G":
                    for g in range(len(FILTER_DFT)):
                        full(act, "G", g)
                        nc.scalar.activation(hy["G"][:, g, :], bank("G", g)[:, :], ACT.Copy).then_inc(free_of("G", g), 1)
                elif kind == "even":
                    projected(*step[1:])
                elif kind == "zt":
                    for i in range(NT):
                        full(act, "zt", i)
                        if i == 0:
                            full(act, "G", len(FILTER_DFT) - 1)
                        nc.scalar.activation(z_tm[:, i, :], bank("zt", i)[:, :], ACT.Copy).then_inc(free_of("zt", i), 1)
                elif kind == "decays":
                    if u >= 2:
                        full(act, "scan", u - 2, "o")
                    b = u % 2
                    for pair, g in enumerate(("b01", "b23")):
                        full(act, "scan", u, g)
                        ps = bank("scan", u, g)[:, :].rearrange("p (h c n) -> p h c n", h=2, c=2)
                        hs = slice(2 * pair, 2 * pair + 2)
                        nc.scalar.activation(sc["ep"][:, b, hs, :], ps[:, :, 0, :], ACT.Exp).then_inc(exps_ready, 1)
                        nc.scalar.activation(sc["en"][:, b, hs, :], ps[:, :, 0, :], ACT.Exp, scale=-1.0).then_inc(exps_ready, 1)
                        nc.scalar.activation(sc["ei"][:, b, hs, :], ps[:, :, 1, :], ACT.Exp).then_inc(free_of("scan", u, g), 1)
                    full(act, "scan", u, "rl")
                    nc.scalar.activation(sc["el"][:, b], bank("scan", u, "rl")[:, :].rearrange("p (h n) -> p h n", h=H),
                                         ACT.Exp).then_inc(free_of("scan", u, "rl"), 1)
                elif kind == "square_heads":
                    for w, (_, i) in enumerate(UNITS):
                        if i == u:
                            freed(act, "scan", w, "o")
                    mean = sc["mean"][:, u, :]
                    for h in range(H):
                        ins = nc.scalar.activation(sc["lf0"][:, 0, P * h : P * h + P], cT[:, h, P * u : P * u + P], ACT.Square,
                                                   accum_out=mean[:, h : h + 1])
                    link(ins)
                    link(nc.scalar.activation(mean[:, H:], mean[:, 0:H], ACT.Ln, bias=eps, scale=1.0 / P))
                    nc.scalar.activation(mean[:, 0:H], mean[:, H:], ACT.Exp, scale=-0.5).then_inc(head_rs, 1)
            norm(0, 1)
            experts(0)
            norm(1, 0)
            for step in STEPS1:
                kind, u = step[0], step[-1]
                if kind == "odd":
                    odd_projected(*step[1:])
                elif kind == "rope":
                    b, i = NORMED.index(step[1]), u
                    n = (4, 2, 8, 8)[b]
                    cols = slice(n * i, n * i + n)
                    act.wait_ge(ss_ready, NT * b + i + 1)
                    link(nc.scalar.activation(at["lt"][:, b, cols], at["ss"][:, b, cols], ACT.Ln, bias=eps, scale=1.0 / (P if b < 2 else 64)))
                    nc.scalar.activation(at["ss"][:, b, cols], at["lt"][:, b, cols], ACT.Exp, scale=-0.5).then_inc(qk_rs, 1)
                elif kind == "lambda":
                    act.wait_ge(lam_dots, 1)
                    nc.scalar.activation(at["lam"][:, 2:4], at["lam"][:, 0:2], ACT.Exp).then_inc(lam_exps, 1)
                elif kind == "tr":
                    transposed(*step[1:])
                elif kind == "attend":
                    attend(u)
                elif kind == "square_heads":
                    freed(act, "O", len(ATTN) // 2 + NT * u + NT - 1)
                    nc.scalar.activation(at["raw0"].rearrange("p i n -> p (i n)")[:, T * u : T * u + T], cT[:, 4 + u, :],
                                         ACT.Square).then_inc(head_squares, 1)
                elif kind == "scale_heads":
                    head_sums(u)
            norm(1, 1)
            experts(1)

        @block.vector
        def _(dve):
            links = [0]

            def link(ins):
                links[0] += 1
                ins.then_inc(dve_link, 1)
                dve.wait_ge(dve_link, links[0])

            V = nc.vector

            def modulation(layer, b):
                full(dve, "adt", layer, b)
                b_mod = pr("b_mod").rearrange("p (l n) -> p l n", l=DEPTH)[:, layer, 4 * b : 4 * b + 4]
                now = mod[:, layer, 4 * b : 4 * b + 4, :]
                V.tensor_reduce(now, bank("adt", layer, b)[:, :].rearrange("p (n g s) -> p n s g", n=4, g=4)[:, :, 0:2, :],
                                AX_X, ALU.add).then_inc(free_of("adt", layer, b), 1)
                freed(dve, "adt", layer, b)
                biased = V.tensor_tensor(now, now, b_mod.unsqueeze(2).to_broadcast([P, 4, 2]), ALU.add)
                which, chunk = b // 6, 4 * b - 24 * (b // 6)
                if KD <= chunk < 2 * KD:
                    link(biased)
                    k = slice(chunk - KD, chunk - KD + 4)
                    gain = (n1, n2)[which][:, layer, k].unsqueeze(2).to_broadcast([P, 4, 2])
                    V.scalar_tensor_tensor(gs[:, layer, which, k, :], mod[:, layer, 4 * b : 4 * b + 4, :], 1.0, gain,
                                           ALU.add, ALU.mult).then_inc(mod_ready, 1)
                else:
                    biased.then_inc(mod_ready, 1)
                dve.wait_ge(mod_ready, MOD_ALL.index((layer, b)) + 1)

            def norm(layer, which):
                count = 2 * layer + which
                dve.wait_ge(rs_ready, count + 1)
                if count == 0:
                    dve.wait_ge(x_in, 16)
                else:
                    residual(dve, count)
                for k in range(KD):
                    V.tensor_tensor(hT[:, k, :], xT[:, k, :], rs[:, :], ALU.mult).then_inc(scaled, 1)
                for k in range(ACT_CHUNKS, KD):
                    dve.wait_ge(scaled, count * KD + k + 1)
                    for s, seg in enumerate(SEGS):
                        V.tensor_scalar(hT[:, k, seg], hT[:, k, seg], gs[:, layer, which, k, s : s + 1],
                                        mod[:, layer, 24 * which + k, s : s + 1], ALU.mult, ALU.add).then_inc(h_by_dve, 1)

            def sine_argument(name):
                if name == "hf1":
                    dve.wait_ge(filter_in, 32)
                else:
                    dve.wait_ge(sin_done, 1)
                a, n, t = hy["a"][0:NHID, 0:T], hy["n"][0:NHID, :], hy["b"][0:NHID, 0:T]
                full(dve, name)
                V.tensor_scalar(a, bank(name)[0:NHID, 0:T], pr("hb" + name[2], NHID), pr(name, NHID),
                                ALU.add, ALU.mult).then_inc(free_of(name), 1)
                freed(dve, name)
                link(V.tensor_scalar(t, a, 1.0 / (2 * math.pi), MAGIC, ALU.mult, ALU.add))
                link(V.tensor_scalar(t, t, MAGIC, None, ALU.subtract))
                link(V.scalar_tensor_tensor(a, t, -TWO_PI_HI, a, ALU.mult, ALU.add))
                link(V.scalar_tensor_tensor(a, t, -TWO_PI_LO, a, ALU.mult, ALU.add))
                V.tensor_scalar(n, a, PI_BELOW, -PI_BELOW, ALU.min, ALU.max).then_inc(sin_arg, 1)

            def filters():
                for i in range(NT):
                    full(dve, "hf3", i, 0)
                    V.tensor_tensor(hy["a"], bank("hf3", i, 0)[:, :], window[:, i, :], ALU.mult).then_inc(free_of("hf3", i, 0), 1)
                    full(dve, "hf3", i, 1)
                    V.tensor_tensor(hy["b"], bank("hf3", i, 1)[:, :], window[:, i, :], ALU.mult).then_inc(free_of("hf3", i, 1), 1)
                    freed(dve, "hf3", i, 0)
                    freed(dve, "hf3", i, 1)
                    V.tensor_tensor(hy["hp"][:, i, :], hy["a"], hy["b"], ALU.add).then_inc(filter_ready, 1)
                    V.tensor_tensor(hy["hm"][:, i, :], hy["a"], hy["b"], ALU.subtract).then_inc(filter_ready, 1)
                    dve.wait_ge(filter_ready, 2 * i + 2)

            def short_conv(name, j):
                ch = 4 * int(name[2]) + j
                dve.wait_ge(conv_bias, ch + 1)
                ps, u = bank("even", name, j), hy["u"]
                for tap, shift in ((0, -1), (2, 1)):
                    for seg in SEGS:
                        a, b = seg.start, seg.stop
                        dst = slice(a + 1, b) if shift < 0 else slice(a, b - 1)
                        src = slice(a, b - 1) if shift < 0 else slice(a + 1, b)
                        ins = V.scalar_tensor_tensor(u[:, ch, dst], ps[:, src], conv_w[:, tap, ch : ch + 1], u[:, ch, dst],
                                                     ALU.mult, ALU.add)
                        if tap == 2 and seg is LAT:
                            ins.then_inc(free_of("even", name, j), 1)
                        elif tap == 0 and seg is LAT:
                            link(ins)

            def spectra():
                G = hy["G"]
                for s, (seq, m) in enumerate(SIGNAL_DFT):
                    re = FILTER_DFT.index((seq, "re", m))
                    im = FILTER_DFT.index((seq, "im", m))
                    re2 = FILTER_DFT.index((seq, "re2", m)) if m == 0 else re
                    full(dve, "Ur", s)
                    full(dve, "Ui", s)
                    Ur, Ui = bank("Ur", s)[:, :], bank("Ui", s)[:, :]
                    for g in (re, im, re2):
                        freed(dve, "G", g)
                    V.tensor_tensor(hz["t1"], Ur, G[:, re, :], ALU.mult)
                    link(V.tensor_tensor(hz["t2"], Ui, G[:, im, :], ALU.mult))
                    link(V.tensor_tensor(Z[:, 2 * s, :], hz["t1"], hz["t2"], ALU.subtract))
                    V.tensor_tensor(hz["t1"], Ur, G[:, im, :], ALU.mult).then_inc(free_of("Ur", s), 1)
                    V.tensor_tensor(hz["t2"], Ui, G[:, re2, :], ALU.mult).then_inc(free_of("Ui", s), 1)
                    freed(dve, "Ur", s)
                    freed(dve, "Ui", s)
                    V.tensor_tensor(Z[:, 2 * s + 1, :], hz["t1"], hz["t2"], ALU.add).then_inc(spec_ready, 1)
                    dve.wait_ge(spec_ready, s + 1)

            def forget(d, i):
                lf, kk = sc[f"lf{d}"][:, i, :], sc[f"k{d}"][:, i, :]
                freed(dve, "even", "fb" if d else "ff", i)
                link(V.tensor_tensor(lf, kk, omlb, ALU.mult))
                link(V.tensor_tensor(lf, lf, lb, ALU.add))
                V.tensor_scalar(kk, lf, -1.0, 1.0, ALU.mult, ALU.add).then_inc(f_ready, 1)

            def scan_scale(u):
                d, i = UNITS[u]
                b, cols = u % 2, slice(P * i, P * i + P)
                ep, en, ei, el = (sc[n][:, b] for n in ("ep", "en", "ei", "el"))
                q = sc["q"][:, :, cols]
                dve.wait_ge(exps_ready, 4 * u + 4)
                freed(dve, "scan", u, "b01")
                freed(dve, "scan", u, "b23")
                if u >= 2:
                    for h in range(H):
                        freed(dve, "scan", u - 2, f"U{h}")
                ends = ei.rearrange("p h (j t) -> p h j t", t=BLK)[:, :, :, (0 if d else BLK - 1)]
                link(V.tensor_copy(sc["decay"][:, b], ends))
                V.tensor_tensor(ep, ep, q, ALU.mult).then_inc(qk_scaled, 1)
                full(dve, "scan", u, "kT")
                V.tensor_tensor(en, bank("scan", u, "kT")[:, :].rearrange("p (h n) -> p h n", h=H), en, ALU.mult).then_inc(free_of("scan", u, "kT"), 1)
                freed(dve, "scan", u, "rl")
                kk = sc[f"k{d}"][:, i, :].rearrange("p (h n) -> p h n", h=H)
                V.tensor_tensor(el, el, kk, ALU.mult).then_inc(qk_scaled, 1)
                V.tensor_tensor(ei, ei, q, ALU.mult).then_inc(qk_scaled, 1)

            def scan_states(u):
                d, i = UNITS[u]
                b = u % 2
                full(dve, "scan", u, "sc")
                if u == 0:
                    dve.wait_ge(zeroed, 4)
                else:
                    full(dve, "scan", u - 1, "o")
                mask = c(f"inc{d}").bitcast(U32).unsqueeze(1).to_broadcast([P, H, P])
                V.copy_predicated(sc[f"P{d}"], mask, bank("scan", u, "sc")[:, :].rearrange("p (h n) -> p h n", h=H)).then_inc(free_of("scan", u, "sc"), 1)
                for h in range(H):
                    full(dve, "scan", u, f"U{h}")
                if i:
                    dve.wait_ge(s0_in, 16)
                order = list(range(NBLK - 1, -1, -1) if d else range(NBLK))
                steps = NBLK if keeps(u) else NBLK - 1
                for n, j in enumerate(order[:steps]):
                    for h in range(H):
                        dst = sc["carry"][:, carry_of(u), h, :] if n == NBLK - 1 else sc["S"][:, h, P * n : P * n + P]
                        U = bank("scan", u, f"U{h}")[:, P * j : P * j + P]
                        src = state_before(u, n, h)
                        if src is None:
                            ins = V.tensor_copy(dst, U)
                        else:
                            ins = V.scalar_tensor_tensor(dst, src, sc["decay"][:, b, h, j : j + 1], U, ALU.mult, ALU.add)
                        if n == steps - 1:
                            ins.then_inc(free_of("scan", u, f"U{h}"), 1)
                    if n == NBLK - 2 and keeps(u):
                        ins.then_inc(states_ready, 1)
                        dve.wait_ge(states_ready, carry_of(u) + 1)
                    elif n < steps - 1:
                        link(ins)

            def scan_output(u):
                i = UNITS[u][1]
                cols = slice(P * i, P * i + P)
                full(dve, "scan", u, "o")
                first = i not in [UNITS[w][1] for w in range(u)]
                ps = bank("scan", u, "o")[:, :].rearrange("p (h n) -> p h n", h=H)
                o = cT[:, 0:H, P * i : P * i + P]
                if first:
                    V.tensor_copy(o, ps).then_inc(free_of("scan", u, "o"), 1)
                else:
                    w = [x for x in range(u) if UNITS[x][1] == i][0]
                    freed(dve, "scan", w, "o")
                    V.tensor_tensor(o, o, ps, ALU.add).then_inc(free_of("scan", u, "o"), 1)

            def add_out(layer, half, j):
                if half == layer:
                    freed(dve, "out", layer, 1 - half, j)
                full(dve, "out", layer, half, j)
                for s, seg in enumerate(SEGS):
                    ins = V.scalar_tensor_tensor(xT[:, j, seg], bank("out", layer, half, j)[:, seg],
                                                 mod[:, layer, 2 * KD + j, s : s + 1], xT[:, j, seg], ALU.mult, ALU.add)
                ins.then_inc(free_of("out", layer, half, j), 1)

            def route(layer):
                b_rt = pr("b_rt").rearrange("p (l n) -> p l n", l=DEPTH)[:, layer]
                lg, l8, m8, i8, f8, oh, ml = (mo[n] for n in ("lg", "l8", "m8", "i8", "f8", "oh", "ml"))
                w, e4, g1, eq0, eq1, A, B = (mo[n] for n in ("w", "e4", "g1", "eq0", "eq1", "A", "B"))
                rank, floor, pos = mo["rank"], mo["floor"], mo["pos"]
                iota = c("iota16")
                dve.wait_ge(cleared, layer + 1)
                full(dve, "rt", layer)
                V.tensor_tensor(lg, bank("rt", layer)[:, 0 : NT * FOLD].rearrange("p (i n) -> p i n", i=NT)[:, :, 0:20],
                                b_rt.unsqueeze(1).to_broadcast([P, NT, 20]), ALU.add).then_inc(free_of("rt", layer), 1)
                freed(dve, "rt", layer)
                link(V.tensor_copy(l8[:, :, 0:NG], lg[:, :, 0:NG]))
                for i in range(NT):
                    link(V.max(m8[:, i, :], l8[:, i, :]))
                    link(V.max_index(i8[:, i, :].bitcast(U32), m8[:, i, :], l8[:, i, :]))
                link(V.tensor_copy(f8, i8.bitcast(U32)))
                V.tensor_tensor(e4, lg[:, :, 0:NG], m8[:, :, 0:1].to_broadcast([P, NT, NG]), ALU.subtract).then_inc(route_max, 1)
                link(V.tensor_tensor(oh, iota[:, 0:NG].unsqueeze(1).to_broadcast([P, NT, NG]), f8[:, :, 0:1].to_broadcast([P, NT, NG]), ALU.is_equal))
                g14 = g1.rearrange("p i (g e) -> p (i g) e", g=NG)
                oh4 = oh.rearrange("p i g -> p (i g)").unsqueeze(2).to_broadcast([P, NT * NG, EPG])
                link(V.tensor_scalar(g14, oh4, 1.0e30, 1.0e30, ALU.mult, ALU.subtract))
                link(V.tensor_tensor(ml, lg[:, :, NG:20], g1, ALU.add))
                for i in range(NT):
                    link(V.max(m8[:, i, :], ml[:, i, :]))
                    link(V.max_index(i8[:, i, :].bitcast(U32), m8[:, i, :], ml[:, i, :]))
                link(V.tensor_copy(f8, i8.bitcast(U32)))
                V.tensor_tensor(w[:, :, 0:1], m8[:, :, 1:2], m8[:, :, 0:1], ALU.subtract).then_inc(route_max, 1)
                it = iota.unsqueeze(1).to_broadcast([P, NT, NE])
                link(V.tensor_tensor(eq0, it, f8[:, :, 0:1].to_broadcast([P, NT, NE]), ALU.is_equal))
                link(V.tensor_tensor(eq1, it, f8[:, :, 1:2].to_broadcast([P, NT, NE]), ALU.is_equal))
                link(V.tensor_tensor(A, eq0, eq1, ALU.add))
                for i in range(NT - 1):
                    link(V.tensor_tensor(B[:, i + 1, :], B[:, i, :], A[:, i, :], ALU.add))
                V.tensor_tensor(B[:, NT, :], B[:, NT - 1, :], A[:, NT - 1, :], ALU.add).then_inc(assigned, 1)
                if layer == 0:
                    for step in LATE_MODS:
                        modulation(*step[1:])
                full(dve, "cum", layer)
                cum = bank("cum", layer)[:, 0 : (NT + 1) * NE]
                above = mo["sel"].rearrange("p i n -> p (i n)")[:, 0 : (NT + 1) * NE * OVER].rearrange("p (n j) -> p n j", j=OVER)
                link(V.tensor_tensor(above, cum.unsqueeze(2).to_broadcast([P, (NT + 1) * NE, OVER]),
                                     c("over").unsqueeze(1).to_broadcast([P, (NT + 1) * NE, OVER]), ALU.is_gt))
                link(V.tensor_reduce(floor.rearrange("p i e -> p (i e)"), above, AX_X, ALU.add))
                V.scalar_tensor_tensor(rank, floor[:, 0:NT, :], float(P - CAP), cum[:, 0 : NT * NE].rearrange("p (i e) -> p i e", i=NT),
                                       ALU.mult, ALU.add).then_inc(free_of("cum", layer), 1)
                freed(dve, "cum", layer)
                two = floor[:, NT, :].rearrange("p (a b) -> p a b", b=2)
                link(V.tensor_tensor(mo["pairs"].unsqueeze(2), two[:, :, 0:1], two[:, :, 1:2], ALU.max))
                link(V.scalar_tensor_tensor(mo["pp"], mo["pairs"].unsqueeze(1).to_broadcast([P, NPAIR + 1, NPAIR]), 1.0,
                                            c("before").rearrange("p (a b) -> p a b", b=NPAIR), ALU.add, ALU.mult))
                link(V.tensor_reduce(mo["first"], mo["pp"], AX_X, ALU.add))
                V.tensor_copy(mo["firsti"].bitcast(mybir.dt.int32), mo["first"]).then_inc(table_ready, 1)
                dve.wait_ge(table_ready, layer + 1)
                link(V.scalar_tensor_tensor(mo["base"].rearrange("p (a b) -> p a b", b=2), mo["first"][:, 0:NPAIR].unsqueeze(2).to_broadcast([P, NPAIR, 2]),
                                            float(P), c("side").rearrange("p (a b) -> p a b", b=2), ALU.mult, ALU.add))
                link(V.tensor_tensor(rank, rank, mo["base"].unsqueeze(1).to_broadcast([P, NT, NE]), ALU.add))
                for n, eq in enumerate((eq0, eq1)):
                    link(V.tensor_tensor(eq, eq, rank, ALU.mult))
                    link(V.tensor_reduce(pos[:, n, :], eq, AX_X, ALU.add))

            def weigh(layer):
                w, e4, pos = mo["w"], mo["e4"], mo["pos"]
                dve.wait_ge(route_exp, 2 * layer + 1)
                link(V.tensor_reduce(w[:, :, 1:2], e4, AX_X, ALU.add))
                dve.wait_ge(route_exp, 2 * layer + 2)
                link(V.tensor_scalar(w[:, :, 2:3], w[:, :, 0:1], 1.0, None, ALU.add))
                link(V.tensor_tensor(w[:, :, 3:4], w[:, :, 1:2], w[:, :, 2:3], ALU.mult))
                link(V.reciprocal(w[:, :, 4:5], w[:, :, 3:4]))
                link(V.tensor_tensor(w[:, :, 5:6], w[:, :, 4:5], w[:, :, 0:1], ALU.mult))
                link(V.tensor_copy(pos[:, 2, :].unsqueeze(2), w[:, :, 4:5]))
                link(V.tensor_copy(pos[:, 3, :].unsqueeze(2), w[:, :, 5:6]))
                for n in range(4):
                    V.tensor_tensor(mo["diag"][:, n, :].rearrange("p (i t) -> p i t", i=NT), ident.unsqueeze(1).to_broadcast([P, NT, P]),
                                    pos[:, n, :].unsqueeze(2).to_broadcast([P, NT, P]), ALU.mult).then_inc(diag_ready, 1)

            def experts(layer):
                y = cT[:, :, :].rearrange("p k t -> p (k t)").rearrange("p (i n) -> p i n", i=NT)
                sems = loops[layer]
                if layer == 0:
                    dve.wait_ge(state_out, 32)
                else:
                    dve.wait_ge(cache_out, 64)
                route(layer)
                dve.wait_ge(sems["primed"], 1)
                sel, sel1, iota = mo["sel"], mo["sel1"], mo["iota"]
                loop_links = sems["primed"]

                def select(tile):
                    it = iota.unsqueeze(1).to_broadcast([P, NT, P])
                    n = tile * 6
                    V.tensor_tensor(sel1, it, mo["pos"][:, 0, :].unsqueeze(2).to_broadcast([P, NT, P]), ALU.is_equal).then_inc(loop_links, 1)
                    V.tensor_tensor(sel, it, mo["pos"][:, 1, :].unsqueeze(2).to_broadcast([P, NT, P]), ALU.is_equal).then_inc(loop_links, 1)
                    dve.wait_ge(loop_links, n - 6 + 1 + 2)
                    V.tensor_scalar(iota, iota, float(P), None, ALU.add).then_inc(loop_links, 1)
                    V.tensor_tensor(sel, sel, sel1, ALU.add).then_inc(sems["selected"], 1)
                    dve.wait_ge(sems["selected"], tile)
                    dve.wait_ge(loop_links, n - 6 + 1 + 3)

                select(1)
                weigh(layer)
                for n in range(4):
                    freed(dve, "pb", layer, n)
                with dve.Fori(0, NPAIR) as i:
                    with dve.Fori(first_tile(dve, i), first_tile(dve, i + 1)) as tile:
                        g = tile + 1
                        n = g * 6
                        dve.wait_ge(sems["gathered"], g * 2)
                        bc, GT, GT1, slot = mo["bc"], mo["GT"], mo["GT1"], mo["slot"]
                        V.scalar_tensor_tensor(GT1, bc[:, 0, :], slot, bc[:, 2, :], ALU.is_equal, ALU.mult).then_inc(loop_links, 1)
                        dve.wait_ge(loop_links, n - 6 + 1 + 4)
                        dve.wait_ge(sems["hidT_full"], g)
                        dve.wait_ge(sems["up_full"], g)
                        dve.wait_ge(sems["sg_ready"], g)
                        V.tensor_tensor(mo["hid"], psum[UP_BANK][:, :], mo["sg"], ALU.mult).then_inc(sems["hid_ready"], 1)
                        for m in range(6):
                            t, half = m // 2, slice(HALF * (m % 2), HALF * (m % 2) + HALF)
                            dve.wait_ge(sems["scattered"], n - 6 + m + 1)
                            dve.wait_ge(sems["summed"], n - 6 + m + 3)
                            V.tensor_tensor(y[:, t, half], psum[SCATTER_BANK + m % 3][:, :], y[:, t, half], ALU.add).then_inc(sems["summed"], 1)
                        V.scalar_tensor_tensor(GT, bc[:, 1, :], slot, bc[:, 3, :], ALU.is_equal, ALU.mult).then_inc(loop_links, 1)
                        dve.wait_ge(loop_links, n - 6 + 1 + 5)
                        V.tensor_scalar(slot, slot, float(P), None, ALU.add).then_inc(loop_links, 1)
                        V.tensor_tensor_reduce(out=GT, in0=GT, in1=GT1, scale=1.0, scalar=0.0, op0=ALU.add, op1=ALU.add,
                                               accum_out=weight).then_inc(sems["weighed"], 1)
                        dve.wait_ge(sems["weighed"], g)
                        V.tensor_scalar(owner[:, :], GT, 0.0, None, ALU.is_gt).then_inc(sems["owner_ready"], 1)
                        dve.wait_ge(sems["owner_ready"], g + 1)
                        dve.wait_ge(loop_links, n + 1)
                        select(g + 1)
                        for half in range(2):
                            cols = slice(HALF * half, HALF * half + HALF)
                            dve.wait_ge(sems["high_ready"], g * 2 + (half - 1))
                            V.scalar_tensor_tensor(low[:, cols], psum[half][:, :], weight, high[:, cols].bitcast(F32), ALU.mult,
                                                   ALU.subtract).then_inc(sems["split"], 1)
                end = first_tile(dve, NPAIR) + 1
                n = end * 6
                for m in range(6):
                    t, half = m // 2, slice(HALF * (m % 2), HALF * (m % 2) + HALF)
                    dve.wait_ge(sems["scattered"], n - 6 + m + 1)
                    dve.wait_ge(sems["summed"], n - 6 + m + 3)
                    V.tensor_tensor(y[:, t, half], psum[SCATTER_BANK + m % 3][:, :], y[:, t, half], ALU.add).then_inc(sems["summed"], 1)
                gate = mod[:, layer, 5 * KD : 6 * KD]
                for k in range(KD):
                    full(dve, "yt", layer, k)
                    for s, seg in enumerate(SEGS):
                        ins = V.scalar_tensor_tensor(xT[:, k, seg], bank("yt", layer, k)[:, seg], gate[:, k, s : s + 1], xT[:, k, seg],
                                                     ALU.mult, ALU.add)
                    ins.then_inc(free_of("yt", layer, k), 1)

            dve.wait_ge(params_in, 16)
            V.tensor_tensor(omlb, omlb, lb, ALU.subtract).then_inc(lb_diff, 1)
            dve.wait_ge(lb_exp, 1)
            link(V.tensor_scalar(omlb, omlb, 1.0, None, ALU.add))
            link(V.reciprocal(lb, omlb))
            link(V.tensor_scalar(omlb, lb, -1.0, 1.0, ALU.mult, ALU.add))
            scaled_tiles = 0
            for step in STEPS0:
                kind, u = step[0], step[-1]
                if kind in ("hf1", "hf2"):
                    sine_argument(kind)
                elif kind == "mod":
                    modulation(*step[1:])
                elif kind == "apply1":
                    norm(0, 0)
                elif kind == "hf3":
                    dve.wait_ge(hyconst_in, 16)
                    filters()
                elif kind == "even" and step[1].startswith("hy"):
                    short_conv(*step[1:])
                    if step[1] == "hy2":
                        freed(dve, *step)
                        V.tensor_tensor(hy["u"][:, 4 + u, :], hy["u"][:, 4 + u, :], hy["u"][:, 8 + u, :], ALU.mult).then_inc(z_ready, 1)
                elif kind == "even" and step[1] in ("ff", "fb"):
                    forget(("ff", "fb").index(step[1]), u)
                elif kind == "dft":
                    spectra()
                elif kind == "inv":
                    for j in range(4):
                        full(dve, "inv", j)
                        V.scalar_tensor_tensor(hy["u"][:, 8 + j, :], hy["u"][:, 4 + j, :], pr("hy_bias")[:, j : j + 1], bank("inv", j)[:, 0:T],
                                               ALU.mult, ALU.add).then_inc(free_of("inv", j), 1)
                        freed(dve, "inv", j)
                        V.tensor_tensor(cT[:, 4 + j, :], hy["u"][:, 8 + j, :], hy["u"][:, j, :], ALU.mult).then_inc(hyena_done, 1)
                    dve.wait_ge(hyena_done, 4)
                elif kind == "decays":
                    if u == 0:
                        for j in range(H):
                            freed(dve, "even", "q", j)
                    scan_scale(u)
                elif kind == "products":
                    scan_states(u)
                elif kind == "outputs":
                    scan_output(u)
                elif kind == "out":
                    add_out(*step[1:])
                elif kind == "scale_heads":
                    for h in range(H):
                        freed(dve, "even", "g", h)
                    full(dve, "ot", u)
                    V.scalar_tensor_tensor(cT[:, 0:H, P * u : P * u + P], bank("ot", u)[:, :].rearrange("p (h n) -> p h n", h=H), pr("hgrn_g"),
                                           sc["g"][:, :, P * u : P * u + P], ALU.mult, ALU.mult).then_inc(free_of("ot", u), 1)
                elif kind == "square_heads":
                    scaled_tiles += 1
                    dve.wait_ge(head_rs, scaled_tiles)
                    o = cT[:, 0:H, P * u : P * u + P]
                    V.tensor_tensor(o, o, sc["mean"][:, u, 0:H].unsqueeze(2).to_broadcast([P, H, P]), ALU.mult).then_inc(head_squares, 1)
            norm(0, 1)
            experts(0)
            norm(1, 0)
            link(V.tensor_tensor_reduce(out=at["t"][:, 0, 0:64], in0=pr("lam")[:, 0:64], in1=pr("lam")[:, 64:128], scale=1.0, scalar=0.0,
                                        op0=ALU.mult, op1=ALU.add, accum_out=at["lam"][:, 0:1]))
            V.tensor_tensor_reduce(out=at["t"][:, 0, 0:64], in0=pr("lam")[:, 128:192], in1=pr("lam")[:, 192:256], scale=1.0, scalar=0.0,
                                   op0=ALU.mult, op1=ALU.add, accum_out=at["lam"][:, 1:2]).then_inc(lam_dots, 1)
            dve.wait_ge(lam_dots, 1)
            norms = {"qc": (4, P, "cq", "cosc", "sinc"), "kv": (2, P, "ck", "cosc", "sinc"),
                     "qd": (8, 64, "dq", "cosd", "sind"), "kd": (8, 64, "dk", "cosd", "sind")}

            def head_squares_of(name, i):
                n, d = norms[name][:2]
                b = NORMED.index(name)
                freed(dve, "odd", name, i)
                x, t = at[f"raw{b}"][:, i, 0 : n * d], at["t"][:, 0, 0 : n * d]
                link(V.tensor_tensor(t, x, x, ALU.mult))
                V.tensor_reduce(at["ss"][:, b, n * i : n * i + n], t.rearrange("p (h d) -> p h d", h=n), AX_X, ALU.add).then_inc(ss_ready, 1)
                dve.wait_ge(ss_ready, NT * b + i + 1)

            def norm_and_rope(name, i):
                n, d, gain, cos, sin = norms[name]
                b = NORMED.index(name)
                dve.wait_ge(qk_rs, NT * b + i + 1)
                raw = at[f"raw{b}"][:, i, 0 : n * d]
                x = raw.rearrange("p (h d) -> p h d", h=n)
                link(V.tensor_tensor(x, x, at["ss"][:, b, n * i : n * i + n].unsqueeze(2).to_broadcast([P, n, d]), ALU.mult))
                ins = V.tensor_tensor(x, x, pr(gain).unsqueeze(1).to_broadcast([P, n, d]), ALU.mult)
                if i == 0:
                    ins.then_inc(normed, 1)
                    dve.wait_ge(normed, b + 1)
                    return
                link(ins)
                x = raw.rearrange("p (h r two) -> p h r two", h=n, two=2)
                x1, x2 = x[:, :, :, 0], x[:, :, :, 1]
                cs = c(cos).rearrange("p (i r) -> p i r", i=2)[:, i - 1].unsqueeze(1).to_broadcast([P, n, d // 2])
                sn = c(sin).rearrange("p (i r) -> p i r", i=2)[:, i - 1].unsqueeze(1).to_broadcast([P, n, d // 2])
                t = [at["t"][:, m, 0 : n * d // 2].rearrange("p (h r) -> p h r", h=n) for m in range(4)]
                V.tensor_tensor(t[0], x1, cs, ALU.mult)
                V.tensor_tensor(t[1], x2, sn, ALU.mult)
                V.tensor_tensor(t[2], x1, sn, ALU.mult)
                link(V.tensor_tensor(t[3], x2, cs, ALU.mult))
                V.tensor_tensor(x1, t[0], t[1], ALU.subtract)
                V.tensor_tensor(x2, t[2], t[3], ALU.add).then_inc(roped, 1)
                dve.wait_ge(roped, (NT - 1) * b + i)

            lam = at["lam"][:, 4:5]

            def row_max(u):
                kind, h, i = ATTN[u]
                nk = P if i == 0 else 3 * P
                for m in maps(u):
                    full(dve, "S", u, m)
                    if u >= 3:
                        dve.wait_ge(probs_ready, u - 2)
                    mx = at["mx"][:, u % 3, 4 * m : 4 * m + 4]
                    link(V.tensor_reduce(mx[:, 0:1], bank("S", u, m)[:, 0:nk], AX_X, ALU.max))
                    V.tensor_scalar(mx[:, 1:2], mx[:, 0:1], -((P if kind == "c" else 64) ** -0.5), None, ALU.mult).then_inc(neg_max, 1)

            def normalise(u):
                kind, h, i = ATTN[u]
                nk = P if i == 0 else 3 * P
                mx, Pb = at["mx"][:, u % 3, :], at["Pb"]
                for m in maps(u):
                    freed(dve, "S", u, m)
                link(V.reciprocal(mx[:, 3:4], mx[:, 2:3]))
                p0 = Pb[:, 2 * (u % 3), 0:nk]
                if kind == "c":
                    V.tensor_scalar(p0, p0, mx[:, 3:4], None, ALU.mult).then_inc(probs_ready, 1)
                else:
                    p1 = Pb[:, 2 * (u % 3) + 1, 0:nk]
                    link(V.reciprocal(mx[:, 7:8], mx[:, 6:7]))
                    link(V.tensor_scalar(p1, p1, mx[:, 7:8], lam, ALU.mult, ALU.mult))
                    V.scalar_tensor_tensor(p0, p0, mx[:, 3:4], p1, ALU.mult, ALU.subtract).then_inc(probs_ready, 1)

            for step in STEPS1:
                kind, u = step[0], step[-1]
                if kind == "sums":
                    head_squares_of(*step[1:])
                elif kind == "rope":
                    norm_and_rope(*step[1:])
                elif kind == "lambda":
                    dve.wait_ge(lam_exps, 1)
                    link(V.tensor_tensor(lam, at["lam"][:, 2:3], at["lam"][:, 3:4], ALU.subtract))
                    link(V.tensor_scalar(lam, lam, LAM_INIT, None, ALU.add))
                    link(V.tensor_scalar(at["lam"][:, 5:6], pr("subln_g"), 1.0 - LAM_INIT, None, ALU.mult))
                elif kind == "attend":
                    if u < len(ATTN):
                        row_max(u)
                    if 1 <= u <= len(ATTN):
                        normalise(u - 1)
                elif kind == "scale_heads":
                    dve.wait_ge(head_rs, NT + u + 1)
                    V.scalar_tensor_tensor(cT[:, 4 + u, :], cT[:, 4 + u, :], at["lam"][:, 5:6], rs[:, :], ALU.mult, ALU.mult).then_inc(mixed, 1)
                elif kind == "out":
                    add_out(*step[1:])
            norm(1, 1)
            experts(1)

        @block.tensor
        def _(pe):
            mm = nc.tensor.matmul

            def open_bank(*name):
                b, n = banks.at[name]
                if n > 1:
                    pe.wait_ge(bank_free[b], n - 1)
                return psum[b]

            def loaded(n):
                s, load = slot_of(n)
                pe.wait_ge(slot_loaded[s], 16 * load)
                return ring[:, s, :].rearrange("p (k n) -> p k n", k=KD)

            def modulation(layer, b):
                w = loaded(index[("mod", layer, b)])
                ps = open_bank("ada", layer, b)
                for k in range(KD):
                    rows = slice(BLK * (k % 4), BLK * (k % 4) + BLK)
                    ins = mm(ps[rows, :], condT[:, k, :], w[:, k, :], start=k < 4, stop=k >= 4)
                ins.then_inc(full_of("ada", layer, b), 1)
                n = MOD_ALL.index((layer, b))
                freed(pe, "ada", layer, b)
                ps = open_bank("adt", layer, b)
                for m in range(4):
                    ins = nc.tensor.transpose(ps[:, P * m : P * m + P], ada[:, n % 2, P * m : P * m + P], ident)
                ins.then_inc(full_of("adt", layer, b), 1)

            def norm(layer, which):
                name = (f"norm{which + 1}", layer)
                ps = open_bank(*name)
                for k in range(KD):
                    pe.wait_ge(squares_ready, KD * (2 * layer + which) + k + 1)
                    ins = mm(ps[:, 0:T], ones, hT[:, k, :], start=k == 0, stop=k == KD - 1)
                ins.then_inc(full_of(*name), 1)

            def h_ready(count, k):
                if k < ACT_CHUNKS:
                    pe.wait_ge(h_by_act, 2 * (ACT_CHUNKS * count + k + 1))
                else:
                    pe.wait_ge(h_by_dve, 2 * ((KD - ACT_CHUNKS) * count + k - ACT_CHUNKS + 1))

            def features_out(ps, w, m, src, count=None):
                for k in range(KD):
                    if count is not None:
                        h_ready(count, k)
                    ins = mm(ps[:, 0:T], w[:, k, P * m : P * m + P], src[:, k, :], start=k == 0, stop=k == KD - 1)
                return ins

            def tokens_out(ps, w, i, src, count=None):
                for k in range(KD):
                    if count is not None:
                        h_ready(count, k)
                    ins = mm(ps[:, :], src[:, k, P * i : P * i + P], w[:, k, :], start=k == 0, stop=k == KD - 1)
                return ins

            def experts(layer):
                sems = loops[layer]
                w_rt = pr("w_rt").rearrange("p (l k n) -> p l k n", l=DEPTH, k=KD)[:, layer]
                ps = open_bank("rk", layer)
                for k in range(KD):
                    rows = slice(BLK * (k % 4), BLK * (k % 4) + BLK)
                    h_ready(2 * layer + 1, k)
                    ins = mm(ps[rows, 0:T], w_rt[:, k, :], hT[:, k, :], start=k < 4, stop=k >= 4)
                ins.then_inc(full_of("rk", layer), 1)
                freed(pe, "rk", layer)
                ps = open_bank("rt", layer)
                for i in range(NT):
                    ins = mm(ps[:, FOLD * i : FOLD * i + FOLD], mo["rk"][:, P * i : P * i + P], c("fold"), start=True, stop=True)
                ins.then_inc(full_of("rt", layer), 1)
                for i in range(NT):
                    for half in range(2):
                        ps = open_bank("ht", layer, i, half)
                        for k in range(4):
                            ins = nc.tensor.transpose(ps[:, P * k : P * k + P], hT[:, 4 * half + k, P * i : P * i + P], ident)
                        ins.then_inc(full_of("ht", layer, i, half), 1)
                if layer == 0:
                    for step in LATE_MODS:
                        modulation(*step[1:])
                pe.wait_ge(assigned, layer + 1)
                ps = open_bank("cum", layer)
                flat = lambda t: t.rearrange("p i e -> p (i e)")
                mm(ps[:, 0 : NT * NE], c("upto"), flat(mo["A"]), start=True, stop=False)
                mm(ps[:, 0 : NT * NE], ones, flat(mo["B"])[:, 0 : NT * NE], start=False, stop=True)
                mm(ps[:, NT * NE : (NT + 1) * NE], ones, mo["B"][:, NT, :], start=True, stop=True).then_inc(full_of("cum", layer), 1)
                freed(pe, "rt", layer)
                freed(pe, "cum", layer)
                if layer == 0:
                    for step in LATE_MODS:
                        freed(pe, "adt", *step[1:])
                for i in range(NT):
                    for half in range(2):
                        freed(pe, "ht", layer, i, half)
                pe.wait_ge(table_ready, layer + 1)
                pe.wait_ge(sems["primed"], 1)

                def gather(tile):
                    pe.wait_ge(sems["selected"], tile)
                    for k in range(KD):
                        for i in range(NT):
                            ins = mm(psum[GATHER_BANK + k // 4][:, P * (k % 4) : P * (k % 4) + P], h_rows[:, i, P * k : P * k + P],
                                     mo["sel"][:, i, :], start=i == 0, stop=i == NT - 1)
                        if k % 4 == 3:
                            ins.then_inc(sems["gathered"], 1)

                def scatter(g, parts):
                    for m in parts:
                        pe.wait_ge(sems["summed"], g * 6 + (m - 5))
                        tokens, cols = slice(P * (m // 2), P * (m // 2) + P), slice(HALF * (m % 2), HALF * (m % 2) + HALF)
                        mm(psum[SCATTER_BANK + m % 3][:, :], owner[:, tokens], high[:, cols], start=True, stop=False)
                        mm(psum[SCATTER_BANK + m % 3][:, :], owner[:, tokens], low[:, cols],
                           start=False, stop=True).then_inc(sems["scattered"], 1)

                def weights_loaded(pair, kind):
                    for side in range(2):
                        pe.wait_ge(moe_loaded(side, kind), pair * 16 + 16 * (moe_loads(layer, side, kind) + 1))

                gather(1)
                for n in range(4):
                    pe.wait_ge(diag_ready, 4 * layer + n + 1)
                    ps = open_bank("pb", layer, n)
                    mm(ps[:, 0:T], ones, mo["diag"][:, n, :], start=True, stop=True).then_inc(full_of("pb", layer, n), 1)
                for n in range(4):
                    freed(pe, "pb", layer, n)
                with pe.Fori(0, NPAIR) as i:
                    with pe.Fori(first_tile(pe, i), first_tile(pe, i + 1)) as tile:
                        g = tile + 1
                        w = [[moe_block(side, kind) for side in range(2)] for kind in range(3)]
                        for kind, done in ((0, "gate_full"), (1, "up_full")):
                            pe.wait_ge(sems["split"], g * 2 + (kind - 1))
                            weights_loaded(i, kind)
                            for k in range(KD):
                                if kind == 0 and k % 4 == 0:
                                    pe.wait_ge(sems["hS_ready"], g * 2 + (k // 4 - 1))
                                for side in range(2):
                                    rows = slice(CAP * side, CAP * side + CAP)
                                    ins = mm(psum[kind][rows, :], mo["hS"][:, k, rows],
                                             w[kind][side].rearrange("p (k n) -> p k n", k=KD)[:, k, :], start=k == 0, stop=k == KD - 1)
                            ins.then_inc(sems[done], 1)
                        pe.wait_ge(sems["owner_ready"], g)
                        pe.wait_ge(sems["split"], g * 2)
                        scatter(g, (0, 1, 2))
                        pe.wait_ge(sems["hid_ready"], g + 1)
                        pe.wait_ge(sems["hidT_ready"], g)
                        for f in range(NF):
                            ins = nc.tensor.transpose(psum[HIDT_BANK][:, P * f : P * f + P], mo["hid"][:, P * f : P * f + P], ident)
                        ins.then_inc(sems["hidT_full"], 1)
                        scatter(g, (3, 4, 5))
                        pe.wait_ge(sems["hidT_ready"], g + 1)
                        weights_loaded(i, 2)
                        for half in range(2):
                            for f in range(NF):
                                for side in range(2):
                                    rows = slice(CAP * side, CAP * side + CAP)
                                    wd = w[2][side].rearrange("p (f n) -> p f n", f=NF)
                                    ins = mm(psum[half][rows, :], mo["hidT"][:, f, rows], wd[:, f, HALF * half : HALF * half + HALF],
                                             start=f == 0, stop=f == NF - 1)
                            ins.then_inc(sems["down_full"], 1)
                        gather(g + 1)
                end = first_tile(pe, NPAIR) + 1
                pe.wait_ge(sems["owner_ready"], end)
                pe.wait_ge(sems["split"], end * 2)
                pe.wait_ge(sems["hS_ready"], end * 2)
                scatter(end, range(6))
                pe.wait_ge(sems["summed"], end * 6 + 3)
                y = cT[:, :, :].rearrange("p k t -> p (k t)").rearrange("p (i n) -> p i n", i=NT)
                for k in range(KD):
                    ps = open_bank("yt", layer, k)
                    for i in range(NT):
                        ins = nc.tensor.transpose(ps[:, P * i : P * i + P], y[:, i, P * k : P * k + P], ident)
                    ins.then_inc(full_of("yt", layer, k), 1)

            def hyena(kind):
                if kind == "hf1":
                    pe.wait_ge(filter_in, 32)
                    ps = open_bank("hf1")
                    mm(ps[0:NHID, 0:T], hyp("w1", NFEAT), hyc("pos")[0:NFEAT], start=True, stop=True).then_inc(full_of("hf1"), 1)
                elif kind == "hf2":
                    pe.wait_ge(sin_done, 1)
                    ps = open_bank("hf2")
                    mm(ps[0:NHID, 0:T], hyp("w2", NHID), hy["s"][0:NHID, :], start=True, stop=True).then_inc(full_of("hf2"), 1)
                elif kind == "hf3":
                    pe.wait_ge(sin_done, 2)
                    for i in range(NT):
                        for half in range(2):
                            ps = open_bank("hf3", i, half)
                            mm(ps[:, :], hy["s"][0:NHID, P * i : P * i + P], hyp("w3", NHID)[:, HALF * half : HALF * half + HALF],
                               start=True, stop=True).then_inc(full_of("hf3", i, half), 1)
                elif kind == "G":
                    pe.wait_ge(hyconst_in, 16)
                    pe.wait_ge(filter_ready, 2 * NT)
                    for g, (seq, part, m) in enumerate(FILTER_DFT):
                        ps = open_bank("G", g)
                        tiles = seq_tiles[seq]
                        src = hy["hm"] if part == "im" else hy["hp"]
                        for n, i in enumerate(tiles):
                            ins = mm(ps[:, :], dft[seq][:, n, dft_columns(seq, part, m)], src[:, i, :], start=n == 0, stop=n == len(tiles) - 1)
                        ins.then_inc(full_of("G", g), 1)
                elif kind == "zt":
                    pe.wait_ge(z_ready, 4)
                    for i in range(NT):
                        ps = open_bank("zt", i)
                        for j in range(4):
                            ins = nc.tensor.transpose(ps[:, P * j : P * j + P], hy["u"][:, 4 + j, P * i : P * i + P], ident)
                        ins.then_inc(full_of("zt", i), 1)
                elif kind == "dft":
                    for i in range(NT):
                        freed(pe, "zt", i)
                    for s, (seq, m) in enumerate(SIGNAL_DFT):
                        tiles = seq_tiles[seq]
                        for grp, part in (("Ur", "re"), ("Ui", "imp")):
                            ps = open_bank(grp, s)
                            for n, i in enumerate(tiles):
                                ins = mm(ps[:, :], dft[seq][:, n, dft_columns(seq, part, m)], z_tm[:, i, :], start=n == 0, stop=n == len(tiles) - 1)
                            ins.then_inc(full_of(grp, s), 1)
                else:
                    pe.wait_ge(spec_ready, 3)
                    for ch in range(4):
                        ps = open_bank("inv", ch)
                        cc = slice(P * ch, P * ch + P)
                        for n, (z, f) in enumerate(((0, 0), (2, 1), (1, 2), (3, 3))):
                            mm(ps[:, LAT], Z[:, z, cc], inv_lat[:, f, :], start=n == 0, stop=n == 3)
                        for f in range(2):
                            ins = mm(ps[:, CTX], Z[:, 4 + f, cc], inv_ctx[:, f, :], start=f == 0, stop=f == 1)
                        ins.then_inc(full_of("inv", ch), 1)

            def heads_of(h):
                return slice(P * h, P * h + P)

            def scan_decays(u):
                d, i = UNITS[u]
                pe.wait_ge(lf_ready, NT * d + i + 1)
                lf, kk = sc[f"lf{d}"][:, i, :], sc[f"k{d}"][:, i, :]
                tri = con[:, CONSTS.at[f"mid{d}"][0] : CONSTS.at[f"mid{d}"][0] + 2 * P]
                for pair, g in enumerate(("b01", "b23")):
                    ps = open_bank("scan", u, g)
                    for x in range(2):
                        ins = mm(ps[:, 2 * P * x : 2 * P * x + 2 * P], lf[:, heads_of(2 * pair + x)], tri, start=True, stop=True)
                    ins.then_inc(full_of("scan", u, g), 1)
                ps = open_bank("scan", u, "kT")
                for h in range(H):
                    ins = nc.tensor.transpose(ps[:, heads_of(h)], kk[:, heads_of(h)], ident)
                ins.then_inc(full_of("scan", u, "kT"), 1)
                ps = open_bank("scan", u, "rl")
                mm(ps[:, :], c(f"last{d}"), lf, start=True, stop=True).then_inc(full_of("scan", u, "rl"), 1)

            def scan_products(u):
                b = u % 2
                pe.wait_ge(qk_scaled, 3 * u + 1)
                freed(pe, "scan", u, "kT")
                ps = open_bank("scan", u, "sc")
                for h in range(H):
                    ins = mm(ps[:, heads_of(h)], sc["en"][:, b, h, :], sc["ep"][:, b, h, :], start=True, stop=True)
                ins.then_inc(full_of("scan", u, "sc"), 1)
                pe.wait_ge(qk_scaled, 3 * u + 2)
                pe.wait_ge(vx_ready, NBLK * (u + 1))
                for h in range(H):
                    ps = open_bank("scan", u, f"U{h}")
                    mm(ps[:, :], sc["el"][:, b, h, :], sc["vx"][:, h].rearrange("p j n -> p (j n)"),
                       start=True, stop=True).then_inc(full_of("scan", u, f"U{h}"), 1)

            def scan_outputs(u):
                d, i = UNITS[u]
                b = u % 2
                pe.wait_ge(qk_scaled, 3 * u + 3)
                freed(pe, "scan", u, "sc")
                if keeps(u):
                    pe.wait_ge(states_ready, carry_of(u) + 1)
                else:
                    for w in (u - 1, u):
                        for h in range(H):
                            freed(pe, "scan", w, f"U{h}")
                ps = open_bank("scan", u, "o")
                order = list(range(NBLK - 1, -1, -1) if d else range(NBLK))
                for h in range(H):
                    blocks = [(slice(BLK * j, BLK * j + BLK), state_before(u, n, h)) for n, j in enumerate(order)]
                    for t, S in blocks:
                        ins = mm(ps[t, heads_of(h)], sc[f"P{d}"][:, h, t], sc["v"][:, i, heads_of(h)], start=True, stop=S is None)
                    for t, S in blocks:
                        if S is not None:
                            ins = mm(ps[t, heads_of(h)], sc["ei"][:, b, h, t], S, start=False, stop=True)
                ins.then_inc(full_of("scan", u, "o"), 1)

            def attend(u):
                if u < len(ATTN):
                    kind, h, i = ATTN[u]
                    if u in (0, len(ATTN) // 2):
                        pe.wait_ge(caches_in, 64)
                        for name in ("qc", "kv") if kind == "c" else ("qd", "kd"):
                            for x in range(NT):
                                freed(pe, "tr", name, x)
                        for x in range(NT):
                            freed(pe, "odd", "kv" if kind == "c" else "vd", x)
                    cols, keys = slice(P * i, P * i + P), slice(0, P) if i == 0 else slice(P, 4 * P)
                    nk = keys.stop - keys.start
                    for m in maps(u):
                        q = at["qcT"] if kind == "c" else at[f"qd{m}"]
                        k_all = at["kcT"][:, h // 2, keys] if kind == "c" else at["kdT"][:, h, keys]
                        ps = open_bank("S", u, m)
                        mm(ps[:, 0:nk], q[:, h, cols], k_all, start=True, stop=True).then_inc(full_of("S", u, m), 1)
                if 2 <= u < len(ATTN) + 2:
                    w = u - 2
                    nt = 1 if ATTN[w][2] == 0 else 3
                    pe.wait_ge(probs_ready, w + 1)
                    ps = open_bank("PT", w)
                    for n in range(nt):
                        ins = nc.tensor.transpose(ps[:, P * n : P * n + P], at["Pb"][:, 2 * (w % 3), P * n : P * n + P], ident)
                    ins.then_inc(full_of("PT", w), 1)
                if u >= 3:
                    w = u - 3
                    kind, h, i = ATTN[w]
                    slots = (0,) if i == 0 else (1, 2, 3)
                    freed(pe, "PT", w)
                    ps = open_bank("O", w)
                    for n, s in enumerate(slots):
                        v = at["vc"][:, s, P * (h // 2) : P * (h // 2) + P] if kind == "c" else at["vd"][:, s, P * h : P * h + P]
                        ins = mm(ps[:, 0:P], v, at["PT"][:, w % 2, P * n : P * n + P], start=n == 0, stop=n == len(slots) - 1)
                    ins.then_inc(full_of("O", w), 1)

            def out_part(layer, half, j):
                w = ring[:, slot_of(index[("out", layer, half)])[0], :].rearrange("p (k n) -> p k n", k=4)
                if j == 0:
                    loaded(index[("out", layer, half)])
                    if layer == 0 and half == 1:
                        pe.wait_ge(hyena_done, 4)
                    elif layer == 1 and half == 0:
                        freed(pe, "O", len(ATTN) // 2 - 1)
                    else:
                        features_mixed(pe, layer)
                ps = open_bank("out", layer, half, j)
                for k in range(4):
                    ins = mm(ps[:, 0:T], w[:, k, P * j : P * j + P], cT[:, 4 * half + k, :], start=k == 0, stop=k == 3)
                ins.then_inc(full_of("out", layer, half, j), 1)

            pe.wait_ge(params_in, 16)
            pe.wait_ge(cond_ready, 1)
            pe.wait_ge(consts_in, 16)
            squared = 0
            for step in STEPS0:
                kind, u = step[0], step[-1]
                if kind == "sum1":
                    norm(0, 0)
                elif kind == "mod":
                    modulation(*step[1:])
                elif kind == "even":
                    _, name, j = step
                    w = loaded(index[("even", name)])
                    ps = open_bank("even", name, j)
                    projection = tokens_out if even_groups(name) == NT else features_out
                    projection(ps, w, j, hT, 0 if (name, j) == ("hy0", 0) else None).then_inc(full_of("even", name, j), 1)
                elif kind == "out":
                    out_part(*step[1:])
                elif kind == "decays":
                    scan_decays(u)
                elif kind == "products":
                    scan_products(u)
                elif kind == "outputs":
                    scan_outputs(u)
                elif kind == "scale_heads":
                    squared += 1
                    pe.wait_ge(head_squares, squared)
                    ps = open_bank("ot", u)
                    for h in range(H):
                        ins = nc.tensor.transpose(ps[:, heads_of(h)], cT[:, h, P * u : P * u + P], ident)
                    ins.then_inc(full_of("ot", u), 1)
                elif kind not in ("apply1", "square_heads"):
                    hyena(kind)
            norm(0, 1)
            experts(0)
            norm(1, 0)
            for step in STEPS1:
                kind, u = step[0], step[-1]
                if kind == "odd":
                    _, name, i = step
                    w = loaded(index[("odd", name)])
                    tokens_out(open_bank(*step), w, i, hT, 2 if (name, i) == ("qc", 0) else None).then_inc(full_of(*step), 1)
                elif kind == "tr":
                    _, name, i = step
                    b = NORMED.index(name)
                    if i == 0:
                        pe.wait_ge(normed, b + 1)
                    else:
                        pe.wait_ge(roped, (NT - 1) * b + i)
                    ps = open_bank(*step)
                    for h in range(2 if name == "kv" else 4):
                        ins = nc.tensor.transpose(ps[:, P * h : P * h + P], at[f"raw{b}"][:, i, P * h : P * h + P], ident)
                    ins.then_inc(full_of(*step), 1)
                elif kind == "attend":
                    attend(u)
                elif kind == "square_heads":
                    squared += 1
                    pe.wait_ge(head_squares, squared)
                    ps = open_bank("heads", u)
                    sq = at["raw0"].rearrange("p i n -> p (i n)")[:, T * u : T * u + T]
                    mm(ps[:, 0:T], ones, sq, start=True, stop=True).then_inc(full_of("heads", u), 1)
                elif kind == "out":
                    out_part(*step[1:])
            norm(1, 1)
            experts(1)


def _constants():
    con = np.zeros((P, CONSTS.total), np.float32)

    def put(name, a):
        start, width = CONSTS.at[name]
        con[: a.shape[0], start : start + width] = a.reshape(a.shape[0], width)

    put("ident", np.eye(P))
    put("ones", np.ones((P, P)))
    put("eps", np.full((P, 1), EPS))
    put("iota16", np.broadcast_to(np.arange(NE), (P, NE)))
    put("fold", np.arange(P)[:, None] % BLK == np.arange(FOLD)[None, :])
    put("upto", np.arange(P)[:, None] <= np.arange(P)[None, :])
    put("iota128", np.broadcast_to(P + np.arange(P), (P, P)))
    put("over", np.broadcast_to(CAP * np.arange(1, OVER + 1), (P, OVER)))
    put("side", np.broadcast_to(P - 1 + CAP * (np.arange(NE) % 2), (P, NE)))
    put("slot_id", P + np.arange(P).reshape(P, 1))
    put("before", np.broadcast_to(np.arange(NPAIR)[None, :] < np.arange(NPAIR + 1)[:, None], (P, NPAIR + 1, NPAIR)))
    s, t = np.arange(P)[:, None], np.arange(P)[None, :]
    same = s // BLK == t // BLK
    middle = t // BLK * BLK + BLK // 2
    put("inc0", same & (s <= t))
    put("mid0", (same & (s <= t)) * 1.0 - (same & (s <= middle - 1)) * 1.0)
    put("last0", same & (s > t))
    put("inc1", same & (s >= t))
    put("mid1", (same & (s >= t)) * 1.0 - (same & (s >= middle)) * 1.0)
    put("last1", same & (s < t))
    row, col = np.arange(DEC) // 64, np.arange(DEC) % 64
    for name, dim in (("c", P), ("d", 64)):
        half = dim // 2
        inv = np.float32(10000.0) ** (-np.arange(0, half, 2, dtype=np.float32) / np.float32(half))
        ang = np.concatenate([row[:, None].astype(np.float32) * inv, col[:, None].astype(np.float32) * inv], -1)
        for fn, f in (("cos", np.cos), ("sin", np.sin)):
            put(fn + name, f(ang).reshape(2, P, half).transpose(1, 0, 2))
    hyc = np.zeros((P, HYCONST.total), np.float32)

    def puth(name, a):
        start, width = HYCONST.at[name]
        hyc[: a.shape[0], start : start + width] = a.reshape(a.shape[0], width)

    pos, win = [], []
    deltas = np.abs(np.linspace(math.log(1e-2) / 1.5, math.log(1e-2) / 0.3, HALF, dtype=np.float32))
    for n in (SEQ, DEC):
        tt = np.linspace(0.0, 1.0, n, dtype=np.float32)[:, None]
        w = (np.float32(2.0 * math.pi) * np.arange(n, dtype=np.float32) / np.float32(n)).astype(np.float32)
        f = np.linspace(1e-4, 15, 16, dtype=np.float32)
        ang = (w[:, None] * f[None, :]).astype(np.float32)
        pos.append(np.concatenate([tt, np.cos(ang), -np.sin(ang)], -1).T)
        win.append(np.exp(-tt * deltas[None, :]))
    puth("pos", np.concatenate(pos, 1))
    puth("window", np.concatenate(win, 0).reshape(NT, P, HALF).transpose(1, 0, 2))
    for name, n in (("lat", DEC), ("ctx", SEQ)):
        t, f = np.arange(n)[:, None], np.arange(n)[None, :]
        re, im = np.cos(np.pi * t * f / n), -np.sin(np.pi * t * f / n)
        nyquist = (-1.0) ** np.arange(n)
        imp, re2 = im[:, :P].copy(), re[:, :P].copy()
        imp[:, 0], re2[:, 0] = nyquist, nyquist
        m = np.concatenate([re, im, imp, re2], 1)
        puth("dft_" + name, m.reshape(n // P, P, -1).transpose(1, 0, 2))
        f, t = np.arange(n)[:, None], np.arange(n)[None, :]
        ire, iim = np.cos(np.pi * t * f / n) / n, -np.sin(np.pi * t * f / n) / n
        ire[0] = 0.5 / n
        iim[0] = 0.5 * (-1.0) ** np.arange(n) / n
        puth("inv_" + name, np.concatenate([ire, iim], 0).reshape(2 * n // P, P, n).transpose(1, 0, 2))
    return con, hyc


def _blocks(w):
    n = w.shape[1] // HALF
    return w.reshape(KD, P, n, HALF).transpose(2, 1, 0, 3).reshape(n, P, KD * HALF)


def _columns(v):
    return np.ascontiguousarray(v.reshape(-1, P).T)


def kernel(**a):
    import concourse.bacc as bacc
    from concourse.bass_utils import run_bass_kernel_spmd

    a = {k: np.asarray(v) for k, v in a.items()}
    par = np.zeros((P, PARAMS.total), np.float32)

    def put(name, v):
        start, width = PARAMS.at[name]
        par[: v.shape[0], start : start + width] = v.reshape(v.shape[0], width)

    rows = lambda v: np.broadcast_to(v.reshape(1, -1), (P, v.size))
    put("cond", np.stack([_columns(a["c_ctx"]), _columns(a["c"][0])], -1))
    put("b_mod", _columns(a["b_mod"]))
    put("n1", _columns(a["norm1_g"]))
    put("n2", _columns(a["norm2_g"]))
    put("conv_w", _columns(a["hy_conv_w"][0]))
    put("conv_b", _columns(a["hy_conv_b"][0]))
    put("hgrn_g", _columns(a["hgrn_norm_g"][0]))
    put("subln_g", _columns(a["d_subln_g"][0]))
    for to, of in (("hb1", "hy_b1"), ("hf1", "hy_freq1"), ("hb2", "hy_b2"), ("hf2", "hy_freq2")):
        put(to, a[of][0].reshape(-1, 1))
    put("hy_bias", _columns(a["hy_bias"][0]))
    put("lower", rows(a["hgrn_lower"]))
    for to, of in (("cq", "c_qnorm_g"), ("ck", "c_knorm_g"), ("dq", "d_qnorm_g"), ("dk", "d_knorm_g")):
        put(to, rows(a[of][0]))
    put("lam", rows(np.concatenate([a["d_lambda_q1"][0], a["d_lambda_k1"][0], a["d_lambda_q2"][0], a["d_lambda_k2"][0]])))
    put("b_rt", rows(np.concatenate([a["moe_b_grp"], a["moe_b_rt"]], -1)))
    w_rt = np.concatenate([a["moe_w_grp"], a["moe_w_rt"]], -1)
    w_rt = np.pad(w_rt, ((0, 0), (0, 0), (0, BLK - 20)))
    put("w_rt", w_rt.reshape(DEPTH, KD, P, BLK).transpose(2, 0, 1, 3).reshape(P, -1))
    hypar = np.zeros((P, HYPAR.total), np.float32)
    for name, v in (("w1", a["hy_w1"][0]), ("w2", a["hy_w2"][0]), ("w3", a["hy_w3"][0])):
        start, width = HYPAR.at[name]
        hypar[: v.shape[0], start : start + width] = v
    con, hyc = _constants()
    x = np.concatenate([a["x_prompt"][0], a["x_sample"][0]], 0)
    mods = [_blocks(w) for w in a["w_mod"]]
    even, odd = _blocks(a["even_w_in"][0]), _blocks(a["odd_w_in"][0])
    w_outs = [a[n][0].reshape(2, KD // 2, P, D).transpose(0, 2, 1, 3).reshape(2, P, -1) for n in ("even_w_out", "odd_w_out")]
    proj = np.stack([mods[n[1]][n[2]] if n[0] == "mod" else even[EVEN_COLUMN[n[1]]] if n[0] == "even"
                     else odd[ODD_COLUMN[n[1]]] if n[0] == "odd" else w_outs[n[1]][n[2]] for n in STREAM])
    moe = np.empty((DEPTH, NE, 3, P, KD * HALF), np.float32)
    for kind, name in enumerate(("moe_w_gate", "moe_w_up")):
        moe[:, :, kind] = a[name].reshape(DEPTH, NE, KD, P, FE).transpose(0, 1, 3, 2, 4).reshape(DEPTH, NE, P, -1)
    moe[:, :, 2] = a["moe_w_down"].reshape(DEPTH, NE, NF, P, D).transpose(0, 1, 3, 2, 4).reshape(DEPTH, NE, P, -1)
    arrays = {
        "params": par, "hypar": hypar, "consts": con, "hyconst": hyc,
        "x": np.ascontiguousarray(x.T.reshape(KD, P, T).transpose(1, 0, 2)),
        "s0": np.ascontiguousarray(a["state_hgrn"][0, 0].transpose(2, 0, 1, 3)),
        "ck": np.ascontiguousarray(a["cache_c_k"][0, 0].transpose(2, 0, 1)),
        "cv": np.ascontiguousarray(a["cache_c_v"][0, 0].transpose(1, 0, 2)).reshape(P, -1),
        "dk": np.ascontiguousarray(a["cache_d_k"][0, 0].transpose(2, 0, 1)),
        "dv": np.ascontiguousarray(a["cache_d_v"][0, 0].transpose(1, 0, 2)).reshape(P, -1),
        "proj": proj, "moe": moe.reshape(DEPTH * NE * 3, P, KD * HALF),
    }
    outs = {"y": (P, KD, T), "state": (2, P, H, P), "ock": (P, 2 * P), "ocv": (P, 2 * P), "odk": (P, HALF), "odv": (P, HALF)}
    nc = bacc.Bacc("TRN2", target_bir_lowering=False, num_devices=1)
    args = [nc.dram_tensor("in_" + n, v.shape, F32, kind="ExternalInput").ap() for n, v in arrays.items()]
    args += [nc.dram_tensor("out_" + n, s, F32, kind="ExternalOutput").ap() for n, s in outs.items()]
    trunk_kernel(nc, *args)
    r = run_bass_kernel_spmd(nc, [{"in_" + n: v for n, v in arrays.items()}], core_ids=[0]).results[0]
    y = np.asarray(r["out_y"]).transpose(2, 1, 0).reshape(T, D)
    heads = lambda n, k: np.asarray(r["out_" + n]).reshape(SEQ, k, P).transpose(1, 0, 2)[None, None]
    return (y[None, :SEQ], y[None, SEQ:], np.asarray(r["out_state"]).transpose(0, 2, 1, 3)[None, None],
            heads("ock", 2), heads("ocv", 2), heads("odk", H), heads("odv", H))
```
